# Optimizing a Trainium2 kernel written in Bass

```python
import math
import jax, jax.numpy as jnp
from jax import lax
import numpy as np

D_MODEL = 1024
BATCH = 1
SEQ = 256
DEPTH = 2

CHUNK = 64
N_META = 16
Q_BLOCK = 128
N_A = DEPTH // 2
N_B = DEPTH - N_A
ALPHA = (2.0 * DEPTH) ** 0.25
BETA = (8.0 * DEPTH) ** -0.25
CONV_W = 31
N_HEADS = 8
HEAD_DIM = D_MODEL // N_HEADS // 2
V_DIM = 2 * HEAD_DIM
ROT_DIM = HEAD_DIM // 4
ROPE_THETA = 500000.0
N_GROUPS = 4
EXPERTS_PER_GROUP = 4
N_EXPERTS = N_GROUPS * EXPERTS_PER_GROUP
TOP_K = 2
D_EXPERT = D_MODEL // 2
EPS = 1e-5

kernel_name = "yoco_conformer_diffattn_hmoe_trunk"

def layernorm(x, g, b):
    xf = x.astype(jnp.float32)
    mu = jnp.mean(xf, axis=-1, keepdims=True)
    var = jnp.mean(jnp.square(xf - mu), axis=-1, keepdims=True)
    y = (xf - mu) * lax.rsqrt(var + EPS)
    return (y * g.astype(jnp.float32) + b.astype(jnp.float32)).astype(x.dtype)

def rmsnorm(x, g):
    xf = x.astype(jnp.float32)
    y = xf * lax.rsqrt(jnp.mean(jnp.square(xf), axis=-1, keepdims=True) + EPS)
    return (y * g.astype(jnp.float32)).astype(x.dtype)

def chunk_ids(n):
    p = jnp.arange(n, dtype=jnp.int32)
    return jnp.where(p < N_META, 0, 1 + (p - N_META) // CHUNK)

def rotary_tables(n):
    pos = jnp.arange(n, dtype=jnp.float32)
    inv = ROPE_THETA ** (-jnp.arange(0, ROT_DIM, 2, dtype=jnp.float32) / ROT_DIM)
    ang = pos[:, None] * inv[None, :]
    return jnp.cos(ang), jnp.sin(ang)

def apply_partial_rope(t, cos, sin):
    half = ROT_DIM // 2
    c = cos[:, None, None, :]
    s = sin[:, None, None, :]
    tf = t[..., :ROT_DIM].astype(jnp.float32)
    t1, t2 = tf[..., :half], tf[..., half:]
    rot = jnp.concatenate([t1 * c - t2 * s, t1 * s + t2 * c], axis=-1).astype(t.dtype)
    return jnp.concatenate([rot, t[..., ROT_DIM:]], axis=-1)

def conformer_conv(x, w_pw1, b_pw1, w_dw, b_dw, ln_g, ln_b, w_pw2, b_pw2):
    h = x @ w_pw1 + b_pw1
    a, g = jnp.split(h, 2, axis=-1)
    h = a * jax.nn.sigmoid(g)
    hp = jnp.pad(h, ((0, 0), (CONV_W - 1, 0), (0, 0)))
    h = lax.conv_general_dilated(hp, w_dw[:, None, :], window_strides=(1,), padding='VALID',
                                 dimension_numbers=('NWC', 'WIO', 'NWC'),
                                 feature_group_count=D_MODEL) + b_dw
    h = jax.nn.silu(layernorm(h, ln_g, ln_b))
    return h @ w_pw2 + b_pw2

def hier_moe(x2d, w_group, b_group, w_expert, b_expert, w1, w3, w2):
    T = x2d.shape[0]
    g_prob = jax.nn.softmax((x2d @ w_group + b_group).astype(jnp.float32), axis=-1)
    g_w, g_idx = lax.top_k(g_prob, 1)
    e_logits = (x2d @ w_expert + b_expert).astype(jnp.float32).reshape(T, N_GROUPS, EXPERTS_PER_GROUP)
    e_logits = jnp.take_along_axis(e_logits, g_idx[:, :, None], axis=1)[:, 0]
    e_prob = jax.nn.softmax(e_logits, axis=-1)
    e_w, e_idx = lax.top_k(e_prob, TOP_K)
    e_w = e_w / jnp.sum(e_w, axis=-1, keepdims=True)
    w = (g_w * e_w).astype(x2d.dtype)
    flat_idx = g_idx * EXPERTS_PER_GROUP + e_idx
    combine = jnp.sum(jax.nn.one_hot(flat_idx, N_EXPERTS, dtype=x2d.dtype) * w[..., None], axis=1)

    def expert_step(acc, p):
        w1e, w3e, w2e, c = p
        h = jax.nn.silu(x2d @ w1e) * (x2d @ w3e)
        return acc + c[:, None] * (h @ w2e), None

    out, _ = lax.scan(expert_step, jnp.zeros_like(x2d), (w1, w3, w2, combine.T))
    return out

def diff_attention(x, k, v, w_q, lam_q1, lam_k1, lam_q2, lam_k2, subln_g, w_o, lam_init, cos, sin):
    B, L, _ = x.shape
    q = apply_partial_rope((x @ w_q).reshape(B, L, N_HEADS, 2, HEAD_DIM), cos, sin)
    lam = (jnp.exp(jnp.sum((lam_q1 * lam_k1).astype(jnp.float32)))
           - jnp.exp(jnp.sum((lam_q2 * lam_k2).astype(jnp.float32))) + lam_init)
    n_blocks = -(-L // Q_BLOCK)
    l_pad = n_blocks * Q_BLOCK
    q = jnp.pad(q, ((0, 0), (0, l_pad - L), (0, 0), (0, 0), (0, 0)))
    qb = q.reshape(B, n_blocks, Q_BLOCK, N_HEADS, 2, HEAD_DIM).transpose(1, 0, 2, 3, 4, 5)
    cid_q = chunk_ids(l_pad).reshape(n_blocks, Q_BLOCK)
    cid_k = chunk_ids(L)
    scale = HEAD_DIM ** -0.5

    def block(args):
        qi, ci = args
        s = jnp.einsum('bqhcd,bkhcd->bhcqk', qi, k).astype(jnp.float32) * scale
        mask = cid_k[None, :] <= ci[:, None]
        s = jnp.where(mask[None, None, None], s, jnp.finfo(jnp.float32).min)
        p = jax.nn.softmax(s, axis=-1)
        pd = (p[:, :, 0] - lam * p[:, :, 1]).astype(v.dtype)
        return jnp.einsum('bhqk,bkhe->bqhe', pd, v)

    o = lax.map(block, (qb, cid_q))
    o = o.transpose(1, 0, 2, 3, 4).reshape(B, l_pad, N_HEADS, V_DIM)[:, :L]
    o = rmsnorm(o, subln_g) * (1.0 - lam_init)
    return o.reshape(B, L, N_HEADS * V_DIM) @ w_o

def setup_inputs(seed: int = 0) -> dict:
    key = jax.random.key(seed)
    ks = jax.random.split(key, 32)
    f32 = jnp.float32

    def nrm(k, shape, scale):
        return jax.random.normal(k, shape, f32) * scale

    d = D_MODEL
    qkw = N_HEADS * 2 * HEAD_DIM
    vw = N_HEADS * V_DIM
    return {
        "x": nrm(ks[0], (BATCH, SEQ, d), 1.0),
        "meta_tokens": nrm(ks[1], (N_META, d), 1.0),
        "conv_w_pw1": nrm(ks[2], (N_A, d, 2 * d), d ** -0.5),
        "conv_b_pw1": nrm(ks[3], (N_A, 2 * d), 0.01),
        "conv_w_dw": nrm(ks[4], (N_A, CONV_W, d), CONV_W ** -0.5),
        "conv_b_dw": nrm(ks[5], (N_A, d), 0.01),
        "conv_ln_g": 1.0 + nrm(ks[6], (N_A, d), 0.02),
        "conv_ln_b": nrm(ks[7], (N_A, d), 0.01),
        "conv_w_pw2": nrm(ks[8], (N_A, d, d), BETA * d ** -0.5),
        "conv_b_pw2": nrm(ks[9], (N_A, d), 0.01),
        "kv_w_k": nrm(ks[10], (d, qkw), d ** -0.5),
        "kv_w_v": nrm(ks[11], (d, vw), BETA * d ** -0.5),
        "attn_w_q": nrm(ks[12], (N_B, d, qkw), d ** -0.5),
        "attn_lam_q1": nrm(ks[13], (N_B, HEAD_DIM), 0.1),
        "attn_lam_k1": nrm(ks[14], (N_B, HEAD_DIM), 0.1),
        "attn_lam_q2": nrm(ks[15], (N_B, HEAD_DIM), 0.1),
        "attn_lam_k2": nrm(ks[16], (N_B, HEAD_DIM), 0.1),
        "attn_subln_g": 1.0 + nrm(ks[17], (N_B, V_DIM), 0.02),
        "attn_w_o": nrm(ks[18], (N_B, vw, d), BETA * vw ** -0.5),
        "post_ln_g": 1.0 + nrm(ks[19], (DEPTH, 2, d), 0.02),
        "post_ln_b": nrm(ks[20], (DEPTH, 2, d), 0.01),
        "moe_w_group": nrm(ks[21], (DEPTH, d, N_GROUPS), d ** -0.5),
        "moe_b_group": nrm(ks[22], (DEPTH, N_GROUPS), 0.01),
        "moe_w_expert": nrm(ks[23], (DEPTH, d, N_EXPERTS), d ** -0.5),
        "moe_b_expert": nrm(ks[24], (DEPTH, N_EXPERTS), 0.01),
        "moe_w1": nrm(ks[25], (DEPTH, N_EXPERTS, d, D_EXPERT), d ** -0.5),
        "moe_w3": nrm(ks[26], (DEPTH, N_EXPERTS, d, D_EXPERT), d ** -0.5),
        "moe_w2": nrm(ks[27], (DEPTH, N_EXPERTS, D_EXPERT, d), BETA * D_EXPERT ** -0.5),
    }

def reference(x, meta_tokens, conv_w_pw1, conv_b_pw1, conv_w_dw, conv_b_dw, conv_ln_g, conv_ln_b,
              conv_w_pw2, conv_b_pw2, kv_w_k, kv_w_v, attn_w_q, attn_lam_q1, attn_lam_k1,
              attn_lam_q2, attn_lam_k2, attn_subln_g, attn_w_o, post_ln_g, post_ln_b,
              moe_w_group, moe_b_group, moe_w_expert, moe_b_expert, moe_w1, moe_w3, moe_w2):
    B, S, D = x.shape
    meta = jnp.broadcast_to(meta_tokens.astype(x.dtype)[None], (B, N_META, D))
    h = jnp.concatenate([meta, x], axis=1)
    L = h.shape[1]
    cos, sin = rotary_tables(L)
    k_shared = None
    v_shared = None
    for l in range(DEPTH):
        if l < N_A:
            a = l
            m = conformer_conv(h, conv_w_pw1[a], conv_b_pw1[a], conv_w_dw[a], conv_b_dw[a],
                               conv_ln_g[a], conv_ln_b[a], conv_w_pw2[a], conv_b_pw2[a])
        else:
            bi = l - N_A
            lam_init = 0.8 - 0.6 * math.exp(-0.3 * l)
            m = diff_attention(h, k_shared, v_shared, attn_w_q[bi], attn_lam_q1[bi], attn_lam_k1[bi],
                               attn_lam_q2[bi], attn_lam_k2[bi], attn_subln_g[bi], attn_w_o[bi],
                               lam_init, cos, sin)
        h = layernorm(ALPHA * h + m, post_ln_g[l, 0], post_ln_b[l, 0])
        f = hier_moe(h.reshape(B * L, D), moe_w_group[l], moe_b_group[l], moe_w_expert[l],
                     moe_b_expert[l], moe_w1[l], moe_w3[l], moe_w2[l]).reshape(B, L, D)
        h = layernorm(ALPHA * h + f, post_ln_g[l, 1], post_ln_b[l, 1])
        if l == N_A - 1:
            k_shared = apply_partial_rope((h @ kv_w_k).reshape(B, L, N_HEADS, 2, HEAD_DIM), cos, sin)
            v_shared = (h @ kv_w_v).reshape(B, L, N_HEADS, V_DIM)
    return h[:, N_META:]


_drawn_inputs = setup_inputs


def setup_inputs(seed=0):
    import zlib

    import numpy as np

    out = dict(_drawn_inputs(seed))
    spreads = {}
    factors = {'conv_b_pw1': 7.674,
     'conv_b_dw': 6.997,
     'conv_ln_g': 4.821,
     'conv_ln_b': 8.0,
     'conv_b_pw2': 4.125,
     'attn_lam_q1': 3.794,
     'attn_lam_k1': 5.185,
     'attn_lam_q2': 3.748,
     'attn_lam_k2': 4.821,
     'attn_subln_g': 64.912,
     'moe_b_group': 6.059,
     'moe_b_expert': 107.837}
    for name, (base, spread) in spreads.items():
        noise = np.random.default_rng([zlib.crc32(name.encode()), seed]).standard_normal(out[name].shape)
        drawn = base * np.exp(spread * noise) if base else spread * noise
        out[name] = __import__('jax').numpy.asarray(drawn.astype(out[name].dtype))
    for name, factor in factors.items():
        out[name] = (out[name] * factor).astype(out[name].dtype)
    return out
```

```python
import math
from contextlib import ExitStack

import numpy as np

import concourse.bass as bass
from concourse import mybir

F32 = mybir.dt.float32
I32 = mybir.dt.int32
U32 = mybir.dt.uint32
ALU = mybir.AluOpType
ACT = mybir.ActivationFunctionType
AX = mybir.AxisListType.X

P = 128
D = 1024
NC_ = D // P
SEQ = 256
META = 16
T0 = SEQ + META
CHUNK = 64
TAPS = 31
PAD = TAPS - 1
HEADS = 8
HEAD_DIM = 64
ROT = HEAD_DIM // 4
GROUPS = 4
PER_GROUP = 4
EXPERTS = GROUPS * PER_GROUP
DE = 512
DEPTH = 2
ALPHA = (2.0 * DEPTH) ** 0.25
EPS = 1e-5
LAM_INIT = 0.8 - 0.6 * math.exp(-0.3 * 1)
THETA = 500000.0

SLOTS = 64
MAX_ITEMS = (2 * T0 + EXPERTS * SLOTS) // SLOTS
TILES = [(T0 + P - 1) // P, SEQ // P]
TOKENS = [T0, SEQ]
BRICK = 4096
RING = 9
BIG = 3.0e38

CONST_AT = {}


def make_constants():
    parts, at = [], 0

    def put(name, a):
        nonlocal at
        a = np.broadcast_to(np.asarray(a, np.float32), (P, np.asarray(a).shape[-1]))
        CONST_AT[name] = (at, at + a.shape[1])
        parts.append(a)
        at += a.shape[1]

    put("ident", np.eye(P))
    put("before", np.triu(np.ones((P, P)), 1))
    put("ones", np.ones((1, P)))
    put("mean_d", np.full((1, P), 1.0 / D))
    put("mean_v", np.full((1, P), 1.0 / P))
    put("slot", np.arange(SLOTS)[None])
    put("neg4", np.arange(4)[None] - 16.0)
    put("full", [[-1.0, 64.0, 128.0, 192.0, 256.0]])
    put("quarter", [[64.0, 128.0, 192.0, 256.0]])
    put("prefix", np.array([[float(e < k) for k in range(EXPERTS + 1) for e in range(EXPERTS)]]))
    t = np.arange(3)[None] * P + np.arange(P)[:, None]
    put("valid", (t < T0).astype(np.float32))
    put("far", np.tile((t >= T0) * 1.0e6, (1, 2)))
    put("eps", [[EPS]])
    half = ROT // 2
    inv = np.float32(THETA) ** (-np.arange(0, ROT, 2, dtype=np.float32) / np.float32(ROT))
    ang = np.arange(T0, dtype=np.float32)[None] * inv.astype(np.float32)[:, None]
    cos, sin = np.ones((P, T0), np.float32), np.zeros((P, T0), np.float32)
    for base in (0, HEAD_DIM):
        for k in range(half):
            cos[base + k] = cos[base + half + k] = np.cos(ang[k])
            sin[base + k] = -np.sin(ang[k])
            sin[base + half + k] = np.sin(ang[k])
    put("cos", cos)
    put("sin", sin)
    for i in range(2):
        q = META + i * P + np.arange(P)
        keys = np.arange(KEYS[i])
        cid = lambda p: np.where(p < META, 0, 1 + (p - META) // CHUNK)
        put(f"mask{i}", np.where(cid(keys)[None] <= cid(q)[:, None], 0.0, -BIG))
    return np.ascontiguousarray(np.concatenate(parts, axis=1), dtype=np.float32)


KEYS = [META + P, T0]
CONSTS = make_constants()

VEC_AT = {"b_pw1": 0, "b_dw": 16, "ln_g": 24, "ln_b": 32, "b_pw2": 40, "post_g": 48, "post_b": 80, "subln": 112}
VEC_ROWS = 113

SWAP = [k + 8 if k < 8 else k - 8 if k < 16 else k for k in range(32)]


def trunk(nc, a, out):
    with ExitStack() as ctx:
        def sb(name, shape, dt=F32):
            return ctx.enter_context(nc.sbuf_tensor(name, shape, dt))

        sems = {}

        def sem(name):
            if name not in sems:
                sems[name] = ctx.enter_context(nc.semaphore(name))
            return sems[name]

        ring = sb("ring", [P, RING, BRICK])
        const = sb("const", [P, CONSTS.shape[1]])
        vec = sb("vec", [P, VEC_ROWS])
        wdw = sb("wdw", [P, TAPS * NC_])
        wr = sb("wr", [P, 2, NC_, 20])
        br = sb("br", [20, 2])
        lamv = sb("lamv", [P, 4, HEAD_DIM])
        tok = sb("tok", [P, 3, D])
        xT = sb("xT", [P, NC_, T0])
        work = sb("work", [P, 6976])
        small = sb("small", [P, 640])
        tab = sb("tab", [1, 2, EXPERTS + 2], I32)
        pos_i = sb("pos_i", [P, 2, 6], I32)
        ps = ctx.enter_context(nc.psum_tensor("ps", [P, 8, 512], F32))
        ybuf = [nc.dram_tensor(f"ybuf{l}", ((MAX_ITEMS + 1) * SLOTS, D), F32, kind="Internal").ap() for l in range(2)]

        def cst(name):
            lo, hi = CONST_AT[name]
            return const[:, lo:hi]

        ident = cst("ident")

        def view(lo, *dims, rows=P):
            n = int(np.prod(dims))
            v = work[0:rows, lo:lo + n]
            if len(dims) == 2:
                v = v.rearrange("p (a b) -> p a b", b=dims[1])
            return v

        glu = view(0, NC_, PAD + T0)
        cv = view(2416, NC_, T0)
        sq = view(4592, NC_, T0)
        sig = view(4592, 2, T0)
        xg, hs, ysb = view(0, 512), view(512, 512), view(1024, 512)
        xTg = view(1536, NC_, SLOTS)
        hT = view(2048, 4, SLOTS)
        pick = view(2304, 3, SLOTS)
        peq = view(2496, 6, SLOTS)
        rows_of = [[view(2880, 2, D), view(4928, 2, D), view(0, 2, D)],
                   [view(2880, 2, D), xT[:, :, :].rearrange("p c t -> p (c t)")[:, 0:2 * D].rearrange("p (a b) -> p a b", b=D)]]
        lnrow = view(4928, 2, D)
        kT = view(0, HEADS, T0)
        qT = view(2176, HEADS, SEQ)
        oT = qT
        raw = view(4224, 2, T0)
        swp = view(4768, T0)
        prob = view(5040, 2, 2 * T0)
        pdT = view(6128, 2, 3 * P)
        vtok = tok
        rawsq = kT
        rstd = view(0, T0)
        std = view(T0, T0)
        o_ = 0

        def sm(n, *dims):
            nonlocal o_
            v = small[:, o_:o_ + n]
            o_ += n
            if len(dims) == 2:
                v = v.rearrange("p (a b) -> p a b", b=dims[1])
            if len(dims) == 3:
                v = v.rearrange("p (a b c) -> p a b c", b=dims[1], c=dims[2])
            return v

        lg = sm(60, 3, 20)
        gmax, gsum, gw, sel = sm(3), sm(3), sm(3), sm(3)
        geq, gex, cand, gone = sm(12, 3, 4), sm(12, 3, 4), sm(12, 3, 4), sm(12, 3, 4)
        el, oh1, oh2, el2 = sm(12, 3, 4), sm(12, 3, 4), sm(12, 3, 4), sm(12, 3, 4)
        m1, m2, e2, wsum = sm(3), sm(3), sm(3), sm(3)
        wts = sm(6, 2, 3)
        AA = sm(96, 2, 3, 16)
        Asum = sm(48, 3, 16)
        rk, bs, qn, pos = sm(6), sm(6), sm(6), sm(6)
        nit, base = sm(16), sm(18)
        bn, mv, tstd, trs = sm(12), sm(6, 3, 2), sm(3), sm(3)
        lam2, lame, nlam, subg = sm(2), sm(2), sm(1), sm(1)
        mx, den, rden, r2 = sm(4, 2, 2), sm(4, 2, 2), sm(4, 2, 2), sm(2)
        alpha_b = sm(8)
        assert o_ <= 640
        lgT = view(544, 3 * P)
        PROD, PROD2 = 1000, 1300

        def prod4(lo, dims):
            v = work[:, lo:lo + int(np.prod(dims))]
            return v.rearrange("p (a b c) -> p a b c", b=dims[1], c=dims[2])

        def V(name, k):
            return vec[:, VEC_AT[name] + k:VEC_AT[name] + k + 1]

        def sq_of(l):
            return sq if l == 0 else view(2176, NC_, SEQ)

        stream = [xT, xT[:, :, META:T0]]

        def brick(b):
            return ring[:, b % RING, :]

        PW1, PW2, E0 = 0, 4, 6
        KB = E0 + 3 * EXPERTS
        VB, QB, OB, E1 = KB + 2, KB + 4, KB + 6, KB + 8
        START = [E0, E1]

        def arrived(b, it=0):
            return sem(f"brick{b % RING}"), (b // RING + (b % RING >= PW2) + it) * 16

        block = ctx.enter_context(nc.Block())

        @block.sync
        def _(sp):
            def load(b, dst, src):
                sp.dma_start(dst, src).then_inc(sem(f"brick{b % RING}"), 16)

            sp.dma_start(tok[0:META, 0, :], a["meta_tokens"]).then_inc(sem("in_x"), 16)
            sp.dma_start(tok[META:P, 0, :], a["x"][0, 0:P - META, :]).then_inc(sem("in_x"), 16)
            sp.dma_start(tok[:, 1, :], a["x"][0, P - META:2 * P - META, :]).then_inc(sem("in_x"), 16)
            sp.dma_start(tok[0:META, 2, :], a["x"][0, 2 * P - META:SEQ, :]).then_inc(sem("in_x"), 16)

            pw1 = a["conv_w_pw1"][0].rearrange("(k p) (s n) -> p k s n", p=P, s=2)
            for b in range(4):
                for s in range(2):
                    sp.dma_start(brick(b).rearrange("p (k s n) -> p k s n", k=NC_, s=2)[:, :, s, :],
                                 pw1[:, :, s, b * 256:(b + 1) * 256]).then_inc(sem(f"pw1_half{b}{s}"), 16)

            def dense(b, w, half):
                load(b, brick(b).rearrange("p (k n) -> p k n", k=NC_),
                     w.rearrange("(k p) n -> p k n", p=P)[:, :, half * 512:(half + 1) * 512])

            for half in range(2):
                dense(PW2 + half, a["conv_w_pw2"][0], half)

            def expert(l, b, e, waits):
                for m, name in enumerate(("moe_w1", "moe_w3", "moe_w2")):
                    waits[m]()
                    k = NC_ if m < 2 else 4
                    if isinstance(e, int):
                        src = a[name][l, e]
                    else:
                        src = a[name][l, bass.ds(e, 1)].rearrange("o r n -> (o r) n")
                    load(b + m, brick(b + m).rearrange("p (k n) -> p k n", k=k),
                         src.rearrange("(k p) n -> p k n", p=P))

            def hold(name, n):
                return lambda: sp.wait_ge(sem(name), n)

            nothing = lambda: None

            def experts(l, first_waits):
                b = START[l]
                for e in range(3):
                    expert(l, b + 3 * e, e, first_waits[3 * e:3 * e + 3])
                sp.wait_ge(sem("tab_ready"), l + 1)

                def later(bb, e, gone_expert):
                    n = sp.value_load(tab[0:1, l, bass.ds(gone_expert + 1, 1)], min_val=1, max_val=MAX_ITEMS)
                    w13 = lambda: sp.wait_ge(sem(f"h_ready{l}"), n)
                    w2 = lambda: sp.wait_ge(sem(f"y_ready{l}"), n)
                    expert(l, bb, e, [w13, nothing, w2])

                with sp.Fori(0, 4) as it:
                    for k in range(3):
                        later(b + 3 * k, it * 3 + (k + 3), it * 3 + k)
                later(b + 9 * 5, EXPERTS - 1, EXPERTS - 4)

            experts(0, [nothing] * 3 + [hold("pw1_ready", 2 * k + 2) for k in range(4)]
                    + [hold("m_ready0", 4), hold("m_ready0", 8)])

            for n, (b, w) in enumerate(((KB, a["kv_w_k"]), (VB, a["kv_w_v"]), (QB, a["attn_w_q"][0]), (OB, a["attn_w_o"][0]))):
                for half in range(2):
                    old = (b + half - RING - E0)
                    items = sp.value_load(tab[0:1, 0, old // 3 + 1:old // 3 + 2], min_val=1, max_val=MAX_ITEMS)
                    sp.wait_ge(sem("y_ready0" if old % 3 == 2 else "h_ready0"), items)
                    dense(b + half, w, half)
            last = sp.value_load(tab[0:1, 0, EXPERTS:EXPERTS + 1], min_val=1, max_val=MAX_ITEMS)
            experts(1, [lambda: sp.wait_ge(sem("y_ready0"), last), hold("kq_ready", 4), hold("kq_ready", 8),
                        hold("v_ready", 5), nothing, hold("kq_ready", 12),
                        hold("kq_ready", 16), hold("m_ready1", 4), hold("m_ready1", 8)])

            for j in range(2):
                sp.wait_ge(sem("out_tile"), j + 1)
                sp.dma_start(out[0, j * P:(j + 1) * P, :], rows_of[1][j][:, 0, :]).then_inc(sem("stored"), 16)
            sp.wait_ge(sem("stored"), 32)

        @block.gpsimd
        def _(pool):
            pool.memset(glu[:, :, 0:PAD], 0.0).then_inc(sem("pad_zero"), 1)
            for l in range(2):
                pool.wait_ge(sem("tab_ready"), l + 1)
                n = pool.value_load(tab[0:1, l, EXPERTS:EXPERTS + 1], min_val=1, max_val=MAX_ITEMS)
                pool.wait_ge(sem(f"tok_ready{l}"), 2 * TILES[l])
                with pool.Fori(n, MAX_ITEMS + 1) as g:
                    pool.dma_start(ybuf[l][bass.ds(g * SLOTS, SLOTS), :], tok[0:SLOTS, 0, :]).then_inc(sem(f"y_filled{l}"), 16)
                left = pool.value_load(tab[0:1, l, EXPERTS + 1:EXPERTS + 2], min_val=1, max_val=MAX_ITEMS)
                pool.wait_ge(sem(f"y_filled{l}"), left * 16)
                for half in range(2):
                    pool.wait_ge(sem(f"y_stored{l}{half}"), n * 16 + 16)
                pool.wait_ge(sem(f"xT_ready{l}"), n + 1)
                pool.sem_inc(sem("items_over"), 1)
                pool.wait_ge(sem("pos_ready"), l + 1)
                for j in range(TILES[l]):
                    rows = min(P, TOKENS[l] - j * P)
                    for c in range(2):
                        pool.indirect_dma_start(
                            out=rows_of[l][j][0:rows, c, :], out_offset=None, in_=ybuf[l],
                            in_offset=bass.IndirectOffsetOnAxis(ap=pos_i[0:rows, l, c * 3 + j:c * 3 + j + 1], axis=0),
                        ).then_inc(sem(f"rows{l}{j}{c}"), 16)

        @block.tensor
        def _(pe):
            pe.wait_ge(sem("in_const"), 16)
            pe.wait_ge(sem("in_x"), 64)
            for j in range(3):
                rows = min(P, T0 - j * P)
                for q in range(2):
                    for c in range(4):
                        last = pe.transpose(ps[:, 2 * j + q, c * rows:(c + 1) * rows],
                                            tok[0:rows, j, (4 * q + c) * P:(4 * q + c + 1) * P], ident[0:rows, 0:rows])
                    last.then_inc(sem("x_turned"), 1)
            pe.wait_ge(sem("in_vec"), 16 * 8)
            pe.wait_ge(sem("in_taps"), 32)
            pe.transpose(ps[:, 6, 0:VEC_ROWS], sq[0:VEC_ROWS, 0, 0:P], ident[0:VEC_ROWS, 0:VEC_ROWS])
            pe.transpose(ps[:, 7, 0:P], sq[:, 1, 0:P], ident)
            pe.transpose(ps[:, 7, P:P + 120], sq[0:120, 2, 0:P], ident[0:120, 0:120]).then_inc(sem("vec_turned"), 1)

            pe.wait_ge(sem("x_moved"), 6)
            for c in range(NC_):
                if c % 2 == 0:
                    pe.wait_ge(sem(f"pw1_half{c // 2}0"), 16)
                    pe.wait_ge(sem(f"pw1_half{c // 2}1"), 16)
                if c >= 2:
                    pe.wait_ge(sem("glu_ready"), c - 1)
                w = brick(c // 2).rearrange("p (k s n) -> p k s n", k=NC_, s=2)
                for s in range(2):
                    for k in range(NC_):
                        last = pe.matmul(ps[:, 2 * (c % 2) + s, 0:T0], w[:, k, s, (c % 2) * P:(c % 2 + 1) * P],
                                         xT[:, k, :], start=(k == 0), stop=(k == NC_ - 1))
                last.then_inc(sem("pw1_ready"), 1)

            def norm_sums(turn, src, squares, T, weight, src_sem, src_n):
                for k in range(NC_):
                    pe.wait_ge(sem(src_sem), src_n + k + 1)
                    last = pe.matmul(ps[:, 4, 0:T], cst(weight), src[:, k, 0:T], start=(k == 0), stop=(k == NC_ - 1))
                last.then_inc(sem("mean_ready"), 1)
                pe.wait_ge(sem("sq_ready"), turn + 1)
                for k in range(NC_):
                    last = pe.matmul(ps[:, 5, 0:T], cst(weight), squares[:, k, 0:T], start=(k == 0), stop=(k == NC_ - 1))
                last.then_inc(sem("var_ready"), 1)

            def project(b0, src, lo, T, ready, free, n0=0, banks=4):
                for c in range(NC_):
                    if c % 4 == 0:
                        pe.wait_ge(*arrived(b0 + c // 4))
                    w = brick(b0 + c // 4).rearrange("p (k n) -> p k n", k=NC_)
                    n = n0 + c
                    if n >= banks:
                        pe.wait_ge(sem(free), n - banks + 1)
                    for k in range(NC_):
                        last = pe.matmul(ps[:, n % banks, 0:T], w[:, k, (c % 4) * P:(c % 4 + 1) * P],
                                         src[:, k, lo:lo + T], start=(k == 0), stop=(k == NC_ - 1))
                    last.then_inc(sem(ready), 1)

            def post_norm_and_route(l):
                T, n = TOKENS[l], TILES[l]
                norm_sums(1 + l, stream[l], sq_of(l), T, "mean_d", f"r_ready{l}", 0)
                for k in range(NC_):
                    pe.wait_ge(sem("normed"), (1 + l) * NC_ + k + 1)
                    last = pe.matmul(ps[0:20, 6, 0:T], wr[:, l, k, :], stream[l][:, k, 0:T], start=(k == 0), stop=(k == NC_ - 1))
                last.then_inc(sem("logits_ready"), 1)
                for j in range(n):
                    rows = min(P, T - j * P)
                    for q in range(2):
                        for c in range(4):
                            last = pe.transpose(ps[0:rows, 2 * j + q, c * P:(c + 1) * P],
                                                stream[l][:, 4 * q + c, j * P:j * P + rows], ident)
                        last.then_inc(sem(f"tok_turned{l}"), 1)
                    if j == 0:
                        pe.wait_ge(sem("logits_moved"), l + 1)
                        for i in range(n):
                            last = pe.transpose(ps[:, 7, 64 + 20 * i:84 + 20 * i], lgT[0:20, i * P:(i + 1) * P], ident[0:20, 0:20])
                        last.then_inc(sem("logits_turned"), 1)
                pe.wait_ge(sem("picks_ready"), l + 1)
                for j in range(n):
                    for i in range(j + 1):
                        pe.matmul(ps[:, 7, 16 * j:16 * j + 16], cst("before" if i == j else "ones"),
                                  Asum[:, i, :], start=(i == 0), stop=(i == j))
                for i in range(n):
                    last = pe.matmul(ps[:, 7, 48:64], cst("ones"), Asum[:, i, :], start=(i == 0), stop=(i == n - 1))
                last.then_inc(sem("ranks_ready"), 1)

            def gather(l, g, first):
                pe.wait_ge(sem(f"pick_ready{l}"), g + 1)
                if not first:
                    pe.wait_ge(sem(f"xg_moved{l}"), g)
                for j in range(TILES[l]):
                    rows = min(P, TOKENS[l] - j * P)
                    for h in range(2):
                        last = pe.matmul(ps[64 * h:64 * h + 64, 2, :], pick[0:rows, j, :],
                                         tok[0:rows, j, h * 512:(h + 1) * 512], start=(j == 0), stop=(j == TILES[l] - 1),
                                         skip_group_check=True)
                last.then_inc(sem(f"xg_ready{l}"), 1)

            def turn_gathered(l, g, first):
                pe.wait_ge(sem(f"xg_moved{l}"), g + 1)
                if not first:
                    pe.wait_ge(sem(f"xT_ready{l}"), g)
                for c in range(4):
                    last = pe.transpose(ps[:, 3, c * P:(c + 1) * P], xg[:, c * P:(c + 1) * P], ident)
                last.then_inc(sem(f"xg_turned{l}"), 1)

            def item(l, g, b, it):
                w1 = brick(b).rearrange("p (k n) -> p k n", k=NC_)
                w3 = brick(b + 1).rearrange("p (k n) -> p k n", k=NC_)
                w2 = brick(b + 2).rearrange("p (k n) -> p k n", k=4)
                pe.wait_ge(sem(f"xT_ready{l}"), g + 1)
                for m in range(2):
                    pe.wait_ge(*arrived(b + m, it))
                for k in range(NC_):
                    pe.matmul(ps[0:64, 0, :], xTg[:, k, :], w1[:, k, :], start=(k == 0), stop=(k == NC_ - 1),
                              skip_group_check=True)
                    last = pe.matmul(ps[64:128, 0, :], xTg[:, k, :], w3[:, k, :], start=(k == 0), stop=(k == NC_ - 1),
                                     skip_group_check=True)
                last.then_inc(sem(f"h_ready{l}"), 1)
                gather(l, g + 1, False)
                pe.wait_ge(sem(f"hs_ready{l}"), g + 1)
                pe.sem_inc(sem("turn_begun"), 1)
                for c in range(4):
                    last = pe.transpose(ps[:, 4, c * 64:(c + 1) * 64], hs[64:128, c * P:(c + 1) * P], ident[64:128, 64:128])
                last.then_inc(sem(f"h_turned{l}"), 1)
                turn_gathered(l, g + 1, False)
                pe.wait_ge(sem(f"hT_ready{l}"), g + 1)
                pe.wait_ge(*arrived(b + 2, it))
                for k in range(4):
                    for h in range(2):
                        last = pe.matmul(ps[64 * h:64 * h + 64, 1, :], hT[:, k, :], w2[:, k, h * 512:(h + 1) * 512],
                                         start=(k == 0), stop=(k == 3), skip_group_check=True)
                last.then_inc(sem(f"y_ready{l}"), 1)

            def mixture(l):
                pe.wait_ge(sem(f"tok_ready{l}"), 2 * TILES[l])
                pe.wait_ge(sem("tab_ready"), l + 1)
                gather(l, 0, True)
                turn_gathered(l, 0, True)

                def expert(b, e, it):
                    lo = pe.value_load(tab[0:1, l, bass.ds(e, 1)], min_val=0, max_val=MAX_ITEMS - 1)
                    hi = pe.value_load(tab[0:1, l, bass.ds(e + 1, 1)], min_val=1, max_val=MAX_ITEMS)
                    with pe.Fori(lo, hi) as g:
                        item(l, g, b, it)

                with pe.Fori(0, 5) as it:
                    for k in range(3):
                        expert(START[l] + 3 * k, it * 3 + k, it)
                expert(START[l] + 45, EXPERTS - 1, 0)

            norm_sums(0, cv, sq, T0, "mean_d", "conv_ready", 0)
            pe.wait_ge(sem("normed"), NC_)
            pe.wait_ge(sem("x_scaled0"), 1)
            project(PW2, cv, 0, T0, "m_ready0", "r_ready0")
            post_norm_and_route(0)
            mixture(0)

            for j in range(3):
                rows = min(P, T0 - j * P)
                pe.wait_ge(sem("z_ready0"), j + 1)
                for q in range(2):
                    for c in range(4):
                        last = pe.transpose(ps[:, 2 * j + q, c * rows:(c + 1) * rows],
                                            rows_of[0][j][0:rows, 0, (4 * q + c) * P:(4 * q + c + 1) * P], ident[0:rows, 0:rows])
                    last.then_inc(sem("z_turned"), 1)

            pe.wait_ge(sem("xT_back"), 24)
            project(KB, xT, 0, T0, "kq_ready", "kq_moved", 0)
            for i, (j, half) in enumerate(((0, 0), (1, 0), (0, 1), (1, 1))):
                w = brick(VB + half).rearrange("p (k n) -> p k n", k=NC_)
                pe.wait_ge(*arrived(VB + half))
                for k in range(NC_):
                    last = pe.matmul(ps[:, 4 + i, :], xT[:, k, j * P:(j + 1) * P], w[:, k, :], start=(k == 0), stop=(k == NC_ - 1))
                last.then_inc(sem("v_ready"), 1)
            pe.wait_ge(sem("v_moved"), 1)
            for k in range(NC_):
                for half in range(2):
                    w = brick(VB + half).rearrange("p (k n) -> p k n", k=NC_)
                    last = pe.matmul(ps[32 * half:32 * half + META, 4, :], xT[:, k, 2 * P:T0], w[:, k, :],
                                     start=(k == 0), stop=(k == NC_ - 1), skip_group_check=True)
            last.then_inc(sem("v_ready"), 1)
            project(QB, xT, META, SEQ, "kq_ready", "kq_moved", NC_)

            pe.wait_ge(sem("kq_moved"), 2 * NC_)
            UNITS = 2 * HEADS

            def scores(u):
                h, i = u // 2, u % 2
                pe.wait_ge(sem("rope_ready"), NC_ + h + 1)
                if u >= 2:
                    pe.wait_ge(sem("scores_moved"), u - 1)
                for c in range(2):
                    r = slice(64 * c, 64 * c + 64)
                    last = pe.matmul(ps[:, 2 * (u % 2) + c, 0:KEYS[i]], qT[r, h, i * P:(i + 1) * P], kT[r, h, 0:KEYS[i]],
                                     start=True, stop=True)
                last.then_inc(sem("scores_ready"), 1)

            def turn_probs(u):
                i = u % 2
                pe.wait_ge(sem("pd_ready"), u + 1)
                if u == 0:
                    pe.wait_ge(sem("v_moved"), 6)
                if u >= 2:
                    pe.wait_ge(sem("pdT_ready"), u - 1)
                for j in range((KEYS[i] + P - 1) // P):
                    w = min(P, KEYS[i] - j * P)
                    last = pe.transpose(ps[0:w, 4 + u % 2, j * P:(j + 1) * P], prob[:, u % 2, j * P:j * P + w], ident)
                last.then_inc(sem("pd_turned"), 1)

            def values(u):
                h, i = u // 2, u % 2
                pe.wait_ge(sem("pdT_ready"), u + 1)
                if i == 0 and h >= 2:
                    pe.wait_ge(sem("o_moved"), h - 1)
                n = (KEYS[i] + P - 1) // P
                for j in range(n):
                    w = min(P, KEYS[i] - j * P)
                    last = pe.matmul(ps[:, 6 + h % 2, i * P:(i + 1) * P], vtok[0:w, j, h * P:(h + 1) * P],
                                     pdT[0:w, u % 2, j * P:(j + 1) * P], start=(j == 0), stop=(j == n - 1))
                last.then_inc(sem("pv_ready"), 1)

            for u in range(UNITS + 2):
                if u < UNITS:
                    scores(u)
                if 1 <= u <= UNITS:
                    turn_probs(u - 1)
                if u >= 2:
                    values(u - 2)
            pe.wait_ge(sem("osq_ready"), 1)
            for h in range(HEADS):
                last = pe.matmul(ps[:, h // 2, (h % 2) * SEQ:(h % 2 + 1) * SEQ], cst("mean_v"), rawsq[:, h, 0:SEQ],
                                 start=True, stop=True)
            last.then_inc(sem("oms_ready"), 1)
            pe.wait_ge(sem("o_normed"), 1)
            pe.wait_ge(sem("x_scaled1"), 1)
            project(OB, oT, 0, SEQ, "m_ready1", "r_ready1")
            post_norm_and_route(1)
            mixture(1)

        @block.scalar
        def _(act):
            act.dma_start(const[:, :], a["consts"]).then_inc(sem("in_const"), 16)
            rows = sq[:, 0, 0:P]
            for name, src in (("b_pw1", a["conv_b_pw1"]), ("b_dw", a["conv_b_dw"]), ("ln_g", a["conv_ln_g"]),
                              ("ln_b", a["conv_ln_b"]), ("b_pw2", a["conv_b_pw2"]), ("subln", a["attn_subln_g"])):
                n = src.shape[0] * src.shape[1] // P
                act.dma_start(rows[VEC_AT[name]:VEC_AT[name] + n, :],
                              src.rearrange("l (c p) -> (l c) p", p=P)).then_inc(sem("in_vec"), 16)
            for name, src in (("post_g", a["post_ln_g"]), ("post_b", a["post_ln_b"])):
                act.dma_start(rows[VEC_AT[name]:VEC_AT[name] + 32, :],
                              src.rearrange("l s (c p) -> (l s c) p", p=P)).then_inc(sem("in_vec"), 16)
            taps = a["conv_w_dw"][0].rearrange("k (c p) -> (k c) p", p=P)
            act.dma_start(sq[:, 1, 0:P], taps[0:P, :]).then_inc(sem("in_taps"), 16)
            act.dma_start(sq[0:120, 2, 0:P], taps[P:P + 120, :]).then_inc(sem("in_taps"), 16)

            def move(dst, src):
                return act.activation(dst, src, ACT.Copy)

            for j in range(3):
                rows_ = min(P, T0 - j * P)
                act.wait_ge(sem("x_turned"), 2 * j + 1)
                move(xT[:, 0:4, j * P:j * P + rows_],
                     ps[:, 2 * j, 0:4 * rows_].rearrange("p (c t) -> p c t", c=4)).then_inc(sem("x_moved"), 1)
            act.wait_ge(sem("vec_ready"), 2)
            for c in range(NC_):
                act.wait_ge(sem("pw1_ready"), c + 1)
                if c >= 2:
                    act.wait_ge(sem("glu_ready"), c - 1)
                act.activation(sig[:, c % 2, :], ps[:, 2 * (c % 2) + 1, 0:T0], ACT.Sigmoid,
                               bias=V("b_pw1", 8 + c)).then_inc(sem("sig_ready"), 1)
            for c in range(NC_):
                last = act.activation(xT[:, c, :], xT[:, c, :], ACT.Identity, scale=ALPHA, bias=alpha_b[:, c:c + 1])
            last.then_inc(sem("x_scaled0"), 1)
            for l in range(2):
                act.dma_start(wr[:, l, :, 0:GROUPS], a["moe_w_group"][l].rearrange("(k p) n -> p k n", p=P)).then_inc(sem("in_router"), 16)
                act.dma_start(wr[:, l, :, GROUPS:20], a["moe_w_expert"][l].rearrange("(k p) n -> p k n", p=P)).then_inc(sem("in_router"), 16)
                act.dma_start(br[0:GROUPS, l:l + 1], a["moe_b_group"][l:l + 1, :].rearrange("o n -> n o")).then_inc(sem("in_router"), 16)
                act.dma_start(br[GROUPS:20, l:l + 1], a["moe_b_expert"][l:l + 1, :].rearrange("o n -> n o")).then_inc(sem("in_router"), 16)
            for k, name in enumerate(("attn_lam_q1", "attn_lam_k1", "attn_lam_q2", "attn_lam_k2")):
                act.dma_start(lamv[:, k, :], a[name].broadcast_to([P, HEAD_DIM])).then_inc(sem("in_lam"), 16)

            def norm(turn, src, squares, dst, T, func, gain, bias):
                act.wait_ge(sem("centred"), turn + 1)
                act.activation(squares[:, :, 0:T], src[:, :, 0:T], ACT.Square).then_inc(sem("sq_ready"), 1)
                act.wait_ge(sem("var_ready"), turn + 1)
                act.activation(std[:, 0:T], ps[:, 5, 0:T], ACT.Sqrt, bias=cst("eps")).then_inc(sem("std_ready"), 1)
                act.wait_ge(sem("scaled"), turn + 1)
                for c in range(NC_):
                    act.activation(dst[:, c, 0:T], src[:, c, 0:T], func, scale=gain(c),
                                   bias=bias(c)).then_inc(sem("normed"), 1)

            def post(l):
                T, n = TOKENS[l], TILES[l]
                norm(1 + l, stream[l], sq_of(l), stream[l], T, ACT.Identity,
                     lambda c: V("post_g", 16 * l + c), lambda c: V("post_b", 16 * l + c))
                act.wait_ge(sem("logits_ready"), l + 1)
                act.wait_ge(sem("pad_ready"), l + 1)
                act.activation(lgT[0:20, 0:T], ps[0:20, 6, 0:T], ACT.Identity, bias=br[0:20, l:l + 1]).then_inc(sem("logits_moved"), 1)
                for j in range(n):
                    rows_ = min(P, T - j * P)
                    act.wait_ge(sem(f"tok_turned{l}"), 2 * j + 1)
                    if j == 0:
                        move(tok[0:rows_, j, 0:512], ps[0:rows_, 0, :]).then_inc(sem(f"tok_ready{l}"), 1)
                        act.wait_ge(sem("gsub_ready"), l + 1)
                        act.activation(gex[:, 0:n, :], gex[:, 0:n, :], ACT.Exp).then_inc(sem("gex_ready"), 1)
                    else:
                        move(tok[0:rows_, j, 0:512], ps[0:rows_, 2 * j, :]).then_inc(sem(f"tok_ready{l}"), 1)
                act.wait_ge(sem("e2_sub"), l + 1)
                act.activation(e2[:, 0:n], e2[:, 0:n], ACT.Exp).then_inc(sem("e2_ready"), 1)

            def mixture(l):
                act.wait_ge(sem("tab_ready"), l + 1)
                n = act.value_load(tab[0:1, l, EXPERTS:EXPERTS + 1], min_val=1, max_val=MAX_ITEMS)
                act.wait_ge(sem(f"xg_ready{l}"), 1)
                move(xg, ps[:, 2, :]).then_inc(sem(f"xg_moved{l}"), 1)
                for half in range(2):
                    act.sem_inc(sem(f"y_stored{l}{half}"), 16)
                with act.Fori(0, n) as g:
                    act.wait_ge(sem(f"h_ready{l}"), g + 1)
                    act.activation(hs[64:128, :], ps[0:64, 0, :], ACT.Silu).then_inc(sem(f"silu_ready{l}"), 1)
                    act.wait_ge(sem(f"xg_ready{l}"), g + 2)
                    act.wait_ge(sem(f"xg_turned{l}"), g + 1)
                    move(xg, ps[:, 2, :]).then_inc(sem(f"xg_moved{l}"), 1)
                    act.wait_ge(sem(f"y_ready{l}"), g + 1)
                    for half in range(2):
                        act.wait_ge(sem(f"y_stored{l}{half}"), g * 16 + 16)
                    move(ysb, ps[:, 1, :]).then_inc(sem(f"y_moved{l}"), 1)
                    act.wait_ge(sem(f"y_moved{l}"), g + 1)
                    for h in range(2):
                        act.dma_start(ybuf[l][bass.ds(g * SLOTS, SLOTS), h * 512:(h + 1) * 512],
                                      ysb[64 * h:64 * h + 64, :]).then_inc(sem(f"y_stored{l}{h}"), 16)

            def combine(l):
                if l == 1:
                    act.wait_ge(sem("attn_over"), 1)
                for j in range(TILES[l]):
                    rows_ = min(P, TOKENS[l] - j * P)
                    act.wait_ge(sem(f"rows{l}{j}0"), 16)
                    r = rows_of[l][j]
                    act.activation(r[0:rows_, 0, :], r[0:rows_, 0, :], ACT.Copy, scale=wts[0:rows_, 0, j:j + 1]).then_inc(sem(f"first_scaled{l}"), 1)
                for j in range(TILES[l]):
                    rows_ = min(P, TOKENS[l] - j * P)
                    act.wait_ge(sem(f"stats_ready{l}"), j + 1)
                    act.activation(tstd[0:rows_, j:j + 1], mv[0:rows_, j, 1:2], ACT.Sqrt, bias=cst("eps")[0:rows_, :]).then_inc(sem(f"tstd_ready{l}"), 1)

            norm(0, cv, sq, cv, T0, ACT.Silu, lambda c: V("ln_g", c), lambda c: V("ln_b", c))
            act.wait_ge(sem("in_router"), 128)
            post(0)
            mixture(0)
            combine(0)
            for j in range(3):
                rows_ = min(P, T0 - j * P)
                act.wait_ge(sem("z_turned"), 2 * j + 1)
                for c in range(4):
                    act.activation(xT[:, c, j * P:j * P + rows_], ps[:, 2 * j, c * rows_:(c + 1) * rows_], ACT.Identity,
                                   scale=V("post_g", 8 + c), bias=V("post_b", 8 + c)).then_inc(sem("xT_back"), 1)
            for c in range(NC_):
                act.wait_ge(sem("kq_ready"), c + 1)
                if c >= 2:
                    act.wait_ge(sem("rope_ready"), c - 1)
                move(raw[:, c % 2, :], ps[:, c % 4, 0:T0]).then_inc(sem("kq_moved"), 1)
            for i, (j, half) in enumerate(((0, 0), (1, 0), (0, 1), (1, 1))):
                act.wait_ge(sem("v_ready"), i + 1)
                move(vtok[:, j, half * 512:(half + 1) * 512], ps[:, 4 + i, :]).then_inc(sem("v_moved"), 1)
            act.wait_ge(sem("v_ready"), 5)
            for half in range(2):
                move(vtok[0:META, 2, half * 512:(half + 1) * 512], ps[32 * half:32 * half + META, 4, :]).then_inc(sem("v_moved"), 1)
            for c in range(NC_):
                n = NC_ + c
                act.wait_ge(sem("kq_ready"), n + 1)
                act.wait_ge(sem("rope_ready"), n - 1)
                move(raw[:, n % 2, 0:SEQ], ps[:, n % 4, 0:SEQ]).then_inc(sem("kq_moved"), 1)
            for c in range(NC_):
                last = act.activation(stream[1][:, c, :], stream[1][:, c, :], ACT.Copy, scale=ALPHA)
            last.then_inc(sem("x_scaled1"), 1)
            act.wait_ge(sem("lam_sums"), 2)
            act.activation(lame, lam2, ACT.Exp).then_inc(sem("lam_exp"), 1)
            for u in range(2 * HEADS):
                h, i = u // 2, u % 2
                act.wait_ge(sem("max_ready"), u + 1)
                for c in range(2):
                    p_ = prob[:, u % 2, c * T0:c * T0 + KEYS[i]]
                    act.activation(p_, p_, ACT.Exp, bias=mx[:, u % 2, c:c + 1],
                                   accum_out=den[:, u % 2, c:c + 1]).then_inc(sem("exp_ready"), 1)
                if u >= 4 and i == 1:
                    hh = h - 2
                    act.wait_ge(sem("pv_ready"), 2 * hh + 2)
                    act.wait_ge(sem("scores_ready"), 2 * hh + 2)
                    move(oT[:, hh, :], ps[:, 6 + hh % 2, 0:SEQ]).then_inc(sem("o_moved"), 1)
            for hh in (HEADS - 2, HEADS - 1):
                act.wait_ge(sem("pv_ready"), 2 * hh + 2)
                move(oT[:, hh, :], ps[:, 6 + hh % 2, 0:SEQ]).then_inc(sem("o_moved"), 1)
            act.wait_ge(sem("o_moved"), HEADS)
            act.activation(rawsq[:, :, 0:SEQ], oT[:, :, :], ACT.Square).then_inc(sem("osq_ready"), 1)
            act.wait_ge(sem("oms_ready"), 1)
            act.wait_ge(sem("oms_free"), 1)
            act.activation(view(0, 4, 512), ps[:, 0:4, :], ACT.Sqrt, bias=cst("eps")).then_inc(sem("ostd_ready"), 1)
            post(1)
            act.wait_ge(sem("tok_ready1"), 4)
            for k, name in enumerate(("post_ln_g", "post_ln_b")):
                act.dma_start(lnrow[:, k, :], a[name][1, 1:2, :].broadcast_to([P, D])).then_inc(sem("in_lnrow"), 16)
            mixture(1)
            combine(1)

        @block.vector
        def _(dve):
            steps = [0]

            def step(ins):
                steps[0] += 1
                ins.then_inc(sem("dve_step"), 1)
                dve.wait_ge(sem("dve_step"), steps[0])

            for j in range(3):
                rows_ = min(P, T0 - j * P)
                dve.wait_ge(sem("x_turned"), 2 * j + 2)
                dve.tensor_copy(xT[:, 4:8, j * P:j * P + rows_],
                                ps[:, 2 * j + 1, 0:4 * rows_].rearrange("p (c t) -> p c t", c=4)).then_inc(sem("x_moved"), 1)
            dve.wait_ge(sem("vec_turned"), 1)
            dve.tensor_copy(vec[:, :], ps[:, 6, 0:VEC_ROWS]).then_inc(sem("vec_ready"), 1)
            dve.tensor_copy(wdw[:, :], ps[:, 7, 0:TAPS * NC_]).then_inc(sem("vec_ready"), 1)
            dve.wait_ge(sem("vec_ready"), 2)
            dve.wait_ge(sem("pad_zero"), 1)
            step(dve.tensor_copy(alpha_b, vec[:, VEC_AT["b_pw2"]:VEC_AT["b_pw2"] + 8]))

            def tap(k, c):
                return wdw[:, k * NC_ + c:k * NC_ + c + 1]

            for c in range(NC_):
                dve.wait_ge(sem("sig_ready"), c + 1)
                dve.scalar_tensor_tensor(glu[:, c, PAD:], ps[:, 2 * (c % 2), 0:T0], V("b_pw1", c), sig[:, c % 2, :],
                                         ALU.add, ALU.mult).then_inc(sem("glu_ready"), 1)
                dve.wait_ge(sem("glu_ready"), c + 1)
                step(dve.tensor_scalar(cv[:, c, :], glu[:, c, 0:T0], tap(0, c), V("b_dw", c), ALU.mult, ALU.add))
                for k in range(1, TAPS):
                    ins = dve.scalar_tensor_tensor(cv[:, c, :], glu[:, c, k:k + T0], tap(k, c), cv[:, c, :], ALU.mult, ALU.add)
                    if k < TAPS - 1:
                        step(ins)
                ins.then_inc(sem("conv_ready"), 1)

            def over_chunks(t, T):
                return t.unsqueeze(1).broadcast_to([P, NC_, T])

            def norm(turn, src, T, src_sem):
                dve.wait_ge(sem(src_sem), NC_)
                dve.wait_ge(sem("mean_ready"), turn + 1)
                dve.tensor_tensor(src[:, :, 0:T], src[:, :, 0:T], over_chunks(ps[:, 4, 0:T], T),
                                  ALU.subtract).then_inc(sem("centred"), 1)
                dve.wait_ge(sem("std_ready"), turn + 1)
                dve.wait_ge(sem("sq_ready"), turn + 1)
                step(dve.reciprocal(rstd[:, 0:T], std[:, 0:T]))
                dve.tensor_tensor(src[:, :, 0:T], src[:, :, 0:T], over_chunks(rstd[:, 0:T], T),
                                  ALU.mult).then_inc(sem("scaled"), 1)

            def residual(l):
                T = TOKENS[l]
                dve.wait_ge(sem(f"x_scaled{l}"), 1)
                for c in range(NC_):
                    dve.wait_ge(sem(f"m_ready{l}"), c + 1)
                    dve.tensor_tensor(stream[l][:, c, 0:T], stream[l][:, c, 0:T], ps[:, c % 4, 0:T], ALU.add).then_inc(sem(f"r_ready{l}"), 1)

            def last_dim(t, n, m):
                return t.unsqueeze(2).broadcast_to([P, n, m])

            def post_and_route(l):
                T, n = TOKENS[l], TILES[l]
                step(dve.memset(lgT[0:20, :], 0.0)) if l == 0 else step(dve.memset(lgT[0:20, 0:SEQ], 0.0))
                dve.engine_nop().then_inc(sem("pad_ready"), 1)
                norm(1 + l, stream[l], T, f"r_ready{l}")
                neg4 = cst("neg4").unsqueeze(1).broadcast_to([P, n, 4])
                dve.wait_ge(sem(f"tok_turned{l}"), 2)
                dve.tensor_copy(tok[:, 0, 512:], ps[:, 1, :]).then_inc(sem(f"tok_ready{l}"), 1)
                dve.wait_ge(sem("logits_turned"), l + 1)
                step(dve.tensor_copy(lg[:, 0:n, :], ps[:, 7, 64:64 + 20 * n].rearrange("p (n e) -> p n e", e=20)))
                G = lg[:, 0:n, 0:4]

                def first_max(values, maxv, onehot):
                    step(dve.tensor_reduce(maxv[:, 0:n], values, AX, ALU.max))
                    step(dve.tensor_tensor(geq[:, 0:n, :], values, last_dim(maxv[:, 0:n], n, 4), ALU.is_equal))
                    step(dve.tensor_tensor(cand[:, 0:n, :], geq[:, 0:n, :], neg4, ALU.mult))
                    step(dve.tensor_reduce(sel[:, 0:n], cand[:, 0:n, :], AX, ALU.min))
                    step(dve.tensor_tensor(onehot[:, 0:n, :], neg4, last_dim(sel[:, 0:n], n, 4), ALU.is_equal))

                first_max(G, gmax, gone)
                dve.tensor_tensor(gex[:, 0:n, :], G, last_dim(gmax[:, 0:n], n, 4), ALU.subtract).then_inc(sem("gsub_ready"), 1)
                chosen = prod4(PROD, (n, 4, 4))
                step(dve.tensor_tensor(chosen, lg[:, 0:n, 4:20].rearrange("p n (g e) -> p n g e", g=4),
                                       gone[:, 0:n, :].unsqueeze(3).broadcast_to([P, n, 4, 4]), ALU.mult))
                step(dve.tensor_reduce(el[:, 0:n, :], chosen.rearrange("p n g e -> p n e g"), AX, ALU.add))
                first_max(el[:, 0:n, :], m1, oh1)
                step(dve.scalar_tensor_tensor(el2[:, 0:n, :], oh1[:, 0:n, :], -BIG, el[:, 0:n, :], ALU.mult, ALU.add))
                first_max(el2[:, 0:n, :], m2, oh2)
                dve.tensor_tensor(e2[:, 0:n], m2[:, 0:n], m1[:, 0:n], ALU.subtract).then_inc(sem("e2_sub"), 1)
                step(dve.tensor_tensor(gone[:, 0:n, :], gone[:, 0:n, :], last_dim(cst("valid")[:, 0:n] if l == 0 else cst("ones")[:, 0:n], n, 4), ALU.mult))
                for c, oh in enumerate((oh1, oh2)):
                    step(dve.tensor_tensor(AA[:, c, 0:n, :].rearrange("p n (g e) -> p n g e", g=4),
                                           gone[:, 0:n, :].unsqueeze(3).broadcast_to([P, n, 4, 4]),
                                           oh[:, 0:n, :].unsqueeze(2).broadcast_to([P, n, 4, 4]), ALU.mult))
                dve.tensor_tensor(Asum[:, 0:n, :], AA[:, 0, 0:n, :], AA[:, 1, 0:n, :], ALU.add).then_inc(sem("picks_ready"), 1)
                dve.wait_ge(sem("gex_ready"), l + 1)
                step(dve.tensor_reduce(gsum[:, 0:n], gex[:, 0:n, :], AX, ALU.add))
                step(dve.reciprocal(gw[:, 0:n], gsum[:, 0:n]))
                dve.wait_ge(sem("e2_ready"), l + 1)
                step(dve.tensor_scalar(wsum[:, 0:n], e2[:, 0:n], 1.0, None, ALU.add))
                step(dve.reciprocal(wsum[:, 0:n], wsum[:, 0:n]))
                step(dve.tensor_tensor(wts[:, 0, 0:n], wsum[:, 0:n], gw[:, 0:n], ALU.mult))
                step(dve.tensor_tensor(wts[:, 1, 0:n], wts[:, 0, 0:n], e2[:, 0:n], ALU.mult))
                dve.wait_ge(sem("ranks_ready"), l + 1)
                step(dve.tensor_copy(nit, ps[:, 7, 48:64]))
                over = prod4(PROD, (1, 16, 5))[:, 0]
                step(dve.tensor_tensor(over, nit.unsqueeze(2).broadcast_to([P, 16, 5]),
                                       cst("full").unsqueeze(1).broadcast_to([P, 16, 5]), ALU.is_gt))
                step(dve.tensor_reduce(nit, over, AX, ALU.add))
                pre = prod4(PROD, (1, 17, 16))[:, 0]
                step(dve.tensor_tensor(pre, nit.unsqueeze(1).broadcast_to([P, 17, 16]),
                                       cst("prefix").rearrange("p (k e) -> p k e", e=16), ALU.mult))
                step(dve.tensor_reduce(base[:, 0:17], pre, AX, ALU.add))
                step(dve.tensor_scalar(base[:, 17:18], base[:, 16:17], -1.0, MAX_ITEMS + 1.0, ALU.mult, ALU.add))
                dve.tensor_copy(tab[0:1, l, :], base[0:1, :]).then_inc(sem("tab_ready"), 1)
                pr = prod4(PROD2, (2, n, 16))
                for c in range(2):
                    step(dve.tensor_tensor(pr[:, c], AA[:, c, 0:n, :], ps[:, 7, 0:16 * n].rearrange("p (n e) -> p n e", e=16), ALU.mult))
                rk2, bs2, qn2, pos2 = (t.rearrange("p (c n) -> p c n", c=2)[:, :, 0:n] for t in (rk, bs, qn, pos))
                step(dve.tensor_reduce(rk2, pr, AX, ALU.add))
                for c in range(2):
                    step(dve.tensor_tensor(pr[:, c], AA[:, c, 0:n, :], base[:, 0:16].unsqueeze(1).broadcast_to([P, n, 16]), ALU.mult))
                step(dve.tensor_reduce(bs2, pr, AX, ALU.add))
                step(dve.scalar_tensor_tensor(pos2, bs2, float(SLOTS), rk2, ALU.mult, ALU.add))
                step(dve.tensor_copy(pos_i[:, l, :].rearrange("p (c n) -> p c n", c=2)[:, :, 0:n], pos2))
                dve.engine_nop().then_inc(sem("pos_ready"), 1)
                if l == 0:
                    step(dve.tensor_tensor(pos2, pos2, cst("far").rearrange("p (c n) -> p c n", c=2), ALU.add))
                pick_item(l, 0, True)
                for j in range(1, n):
                    rows_ = min(P, T - j * P)
                    dve.wait_ge(sem(f"tok_turned{l}"), 2 * j + 2)
                    dve.tensor_copy(tok[0:rows_, j, 512:], ps[0:rows_, 2 * j + 1, :]).then_inc(sem(f"tok_ready{l}"), 1)

            def pick_item(l, g, first):
                n = TILES[l]
                if not first:
                    dve.wait_ge(sem(f"xg_ready{l}"), g)
                    dve.wait_ge(sem(f"pos_next{l}"), g)
                eq = peq[:, 0:2 * n, :].rearrange("p (c n) s -> p c n s", c=2)
                pos2 = pos.rearrange("p (c n) -> p c n", c=2)
                for c in range(2):
                    ins = dve.tensor_tensor(eq[:, c], cst("slot").unsqueeze(1).broadcast_to([P, n, SLOTS]),
                                            pos2[:, c, 0:n].unsqueeze(2).broadcast_to([P, n, SLOTS]), ALU.is_equal)
                ins.then_inc(sem(f"peq_ready{l}"), 1)
                dve.wait_ge(sem(f"peq_ready{l}"), g + 1)
                dve.tensor_tensor(pick[:, 0:n, :], eq[:, 0], eq[:, 1], ALU.add).then_inc(sem(f"pick_ready{l}"), 1)
                dve.tensor_scalar(pos2[:, :, 0:n], pos2[:, :, 0:n], -float(SLOTS), None, ALU.add).then_inc(sem(f"pos_next{l}"), 1)

            def move_gathered(l, g, first):
                dve.wait_ge(sem(f"xg_turned{l}"), g + 1)
                if not first:
                    dve.wait_ge(sem(f"h_ready{l}"), g)
                dve.tensor_copy(xTg.rearrange("p (h c) s -> p c h s", h=2),
                                ps[:, 3, :].rearrange("p (c h s) -> p c h s", c=4, h=2)).then_inc(sem(f"xT_ready{l}"), 1)

            def mixture(l):
                dve.wait_ge(sem("tab_ready"), l + 1)
                n = dve.value_load(tab[0:1, l, EXPERTS:EXPERTS + 1], min_val=1, max_val=MAX_ITEMS)
                move_gathered(l, 0, True)
                with dve.Fori(0, n) as g:
                    pick_item(l, g + 1, False)
                    dve.wait_ge(sem(f"silu_ready{l}"), g + 1)
                    dve.tensor_tensor(hs[64:128, :], hs[64:128, :], ps[64:128, 0, :], ALU.mult).then_inc(sem(f"hs_ready{l}"), 1)
                    dve.wait_ge(sem(f"h_turned{l}"), g + 1)
                    dve.tensor_copy(hT.rearrange("p c s -> p (c s)"), ps[:, 4, 0:256]).then_inc(sem(f"hT_ready{l}"), 1)
                    move_gathered(l, g + 1, False)

            def combine(l):
                for j in range(TILES[l]):
                    rows_ = min(P, TOKENS[l] - j * P)
                    r = rows_of[l][j]
                    dve.wait_ge(sem(f"rows{l}{j}1"), 16)
                    dve.wait_ge(sem(f"first_scaled{l}"), j + 1)
                    first, second = r[0:rows_, 0, :], r[0:rows_, 1, :]
                    step(dve.scalar_tensor_tensor(first, second, wts[0:rows_, 1, j:j + 1], first, ALU.mult, ALU.add))
                    step(dve.scalar_tensor_tensor(first, tok[0:rows_, j, :], ALPHA, first, ALU.mult, ALU.add))
                    for h in range(2):
                        step(dve.bn_stats(bn[0:rows_, 6 * h:6 * h + 6], r[0:rows_, 0, h * 512:(h + 1) * 512]))
                    dve.bn_aggr(mv[0:rows_, j, :], bn[0:rows_, :]).then_inc(sem(f"stats_ready{l}"), 1)
                    dve.wait_ge(sem(f"tstd_ready{l}"), j + 1)
                    step(dve.reciprocal(trs[0:rows_, j:j + 1], tstd[0:rows_, j:j + 1]))
                    ins = dve.tensor_scalar(first, first, mv[0:rows_, j, 0:1], trs[0:rows_, j:j + 1], ALU.subtract, ALU.mult)
                    if l == 0:
                        ins.then_inc(sem("z_ready0"), 1)
                        continue
                    step(ins)
                    if j == 0:
                        dve.wait_ge(sem("in_lnrow"), 32)
                    step(dve.tensor_tensor(first, first, lnrow[:, 0, :], ALU.mult))
                    dve.tensor_tensor(first, first, lnrow[:, 1, :], ALU.add).then_inc(sem("out_tile"), 1)

            norm(0, cv, T0, "conv_ready")
            residual(0)
            post_and_route(0)
            mixture(0)
            combine(0)
            for j in range(3):
                rows_ = min(P, T0 - j * P)
                dve.wait_ge(sem("z_turned"), 2 * j + 2)
                for c in range(4):
                    dve.tensor_scalar(xT[:, 4 + c, j * P:j * P + rows_], ps[:, 2 * j + 1, c * rows_:(c + 1) * rows_],
                                      V("post_g", 12 + c), V("post_b", 12 + c), ALU.mult, ALU.add).then_inc(sem("xT_back"), 1)

            dve.wait_ge(sem("in_lam"), 64)
            for k in range(2):
                dve.tensor_tensor_reduce(lamv[:, 2 * k, :], lamv[:, 2 * k, :], lamv[:, 2 * k + 1, :], 1.0, 0.0,
                                         ALU.mult, ALU.add, lam2[:, k:k + 1]).then_inc(sem("lam_sums"), 1)
            step(dve.tensor_scalar(subg, V("subln", 0), 1.0 - LAM_INIT, None, ALU.mult))

            for n in range(2 * NC_):
                c, T, lo = n % NC_, (T0, SEQ)[n // NC_], (0, META)[n // NC_]
                dst = kT[:, c, :] if n < NC_ else qT[:, c, :]
                if n:
                    dve.wait_ge(sem("rope_ready"), n)
                dve.wait_ge(sem("kq_moved"), n + 1)
                r = raw[:, n % 2, 0:T]
                step(dve.stream_shuffle(swp[:, 0:T], r, SWAP))
                step(dve.tensor_tensor(swp[:, 0:T], swp[:, 0:T], cst("sin")[:, lo:lo + T], ALU.mult))
                step(dve.tensor_tensor(dst, r, cst("cos")[:, lo:lo + T], ALU.mult))
                dve.tensor_tensor(dst, dst, swp[:, 0:T], ALU.add).then_inc(sem("rope_ready"), 1)

            dve.wait_ge(sem("lam_exp"), 1)
            step(dve.tensor_tensor(nlam, lame[:, 1:2], lame[:, 0:1], ALU.subtract))
            step(dve.tensor_scalar(nlam, nlam, -LAM_INIT, None, ALU.add))

            def mask_and_max(u):
                i = u % 2
                b = u % 2
                w = KEYS[i]
                dve.wait_ge(sem("scores_ready"), u + 1)
                if u >= 2:
                    dve.wait_ge(sem("pd_turned"), u - 1)
                s = prob[:, b, :].rearrange("p (c k) -> p c k", c=2)[:, :, 0:w]
                dve.scalar_tensor_tensor(s, ps[:, 2 * b:2 * b + 2, 0:w], HEAD_DIM ** -0.5,
                                         cst(f"mask{i}").unsqueeze(1).broadcast_to([P, 2, w]),
                                         ALU.mult, ALU.add).then_inc(sem("scores_moved"), 1)
                dve.wait_ge(sem("scores_moved"), u + 1)
                dve.tensor_reduce(mx[:, b, :], s, AX, ALU.max, negate=True).then_inc(sem("max_ready"), 1)

            def difference(u):
                i, b = u % 2, u % 2
                w = KEYS[i]
                dve.wait_ge(sem("exp_ready"), 2 * u + 2)
                step(dve.reciprocal(rden[:, b, :], den[:, b, :]))
                step(dve.tensor_tensor(r2[:, b:b + 1], rden[:, b, 1:2], nlam, ALU.mult))
                step(dve.tensor_scalar(prob[:, b, 0:w], prob[:, b, 0:w], rden[:, b, 0:1], None, ALU.mult))
                dve.scalar_tensor_tensor(prob[:, b, 0:w], prob[:, b, T0:T0 + w], r2[:, b:b + 1], prob[:, b, 0:w],
                                         ALU.mult, ALU.add).then_inc(sem("pd_ready"), 1)

            def move_probs(u):
                i, b = u % 2, u % 2
                dve.wait_ge(sem("pd_turned"), u + 1)
                if u >= 2:
                    dve.wait_ge(sem("pv_ready"), u - 1)
                full = KEYS[i] // P
                dve.tensor_copy(pdT[:, b, 0:full * P], ps[:, 4 + b, 0:full * P])
                dve.tensor_copy(pdT[0:META, b, full * P:(full + 1) * P],
                                ps[0:META, 4 + b, full * P:(full + 1) * P]).then_inc(sem("pdT_ready"), 1)

            for u in range(2 * HEADS + 2):
                if u < 2 * HEADS:
                    mask_and_max(u)
                if 1 <= u <= 2 * HEADS:
                    difference(u - 1)
                if u >= 2:
                    move_probs(u - 2)
            dve.engine_nop().then_inc(sem("oms_free"), 1)
            dve.wait_ge(sem("ostd_ready"), 1)
            ostd = view(0, 4, 512)
            orstd = view(4224, 4, 512)
            step(dve.reciprocal(orstd, ostd))
            flat = oT.rearrange("p h t -> p (h t)")
            dve.scalar_tensor_tensor(flat, flat, subg, orstd.rearrange("p a b -> p (a b)"),
                                     ALU.mult, ALU.mult).then_inc(sem("o_normed"), 1)
            residual(1)
            dve.engine_nop().then_inc(sem("attn_over"), 1)
            post_and_route(1)
            mixture(1)
            combine(1)


def kernel(**inputs):
    import concourse.bacc as bacc
    from concourse.bass_utils import run_bass_kernel_spmd

    nc = bacc.Bacc("TRN2", target_bir_lowering=False, num_devices=1)
    arrays, aps = {}, {}
    for name, value in {**inputs, "consts": CONSTS}.items():
        v = np.ascontiguousarray(value)
        arrays[f"in_{name}"] = v
        aps[name] = nc.dram_tensor(f"in_{name}", v.shape, mybir.dt.from_np(v.dtype), kind="ExternalInput").ap()
    out = nc.dram_tensor("out", (1, SEQ, D), F32, kind="ExternalOutput").ap()
    trunk(nc, aps, out)
    return run_bass_kernel_spmd(nc, [arrays], core_ids=[0]).results[0]["out"]
```

```python
import math
from contextlib import ExitStack

import numpy as np

import concourse.bass as bass
from concourse import mybir

F32 = mybir.dt.float32
I32 = mybir.dt.int32
U32 = mybir.dt.uint32
ALU = mybir.AluOpType
ACT = mybir.ActivationFunctionType
AX = mybir.AxisListType.X

P = 128
D = 1024
NC_ = D // P
SEQ = 256
META = 16
T0 = SEQ + META
CHUNK = 64
TAPS = 31
PAD = TAPS - 1
HEADS = 8
HEAD_DIM = 64
ROT = HEAD_DIM // 4
GROUPS = 4
PER_GROUP = 4
EXPERTS = GROUPS * PER_GROUP
DE = 512
DEPTH = 2
ALPHA = (2.0 * DEPTH) ** 0.25
EPS = 1e-5
LAM_INIT = 0.8 - 0.6 * math.exp(-0.3 * 1)
THETA = 500000.0

SLOTS = 32
MAX_ITEMS = (2 * T0 + EXPERTS * (SLOTS - 1)) // SLOTS
MIN_ITEMS = 2 * SEQ // SLOTS
TILES = [(T0 + P - 1) // P, SEQ // P]
TOKENS = [T0, SEQ]
QUARTERS = 4
BRICK = 4096
RING = 9
AHEAD = RING // 3
ORDER = EXPERTS + 2
BIG = 3.0e38
DVE_CHUNKS = 6
DIAGS = (NC_ - DVE_CHUNKS) * TAPS
FULL = len(range(0, T0, SLOTS))

CONST_AT = {}


def make_constants():
    parts, at = [], 0

    def put(name, a):
        nonlocal at
        a = np.broadcast_to(np.asarray(a, np.float32), (P, np.asarray(a).shape[-1]))
        CONST_AT[name] = (at, at + a.shape[1])
        parts.append(a)
        at += a.shape[1]

    put("ident", np.eye(P))
    put("before", np.triu(np.ones((P, P)), 1))
    put("ones", np.ones((1, P)))
    put("mean_d", np.full((1, P), 1.0 / D))
    put("mean_v", np.full((1, P), 1.0 / P))
    put("slot", np.arange(SLOTS)[None])
    put("neg4", np.arange(4)[None] - 16.0)
    put("full", [list(range(0, T0, SLOTS))])
    put("minus_e", -np.arange(EXPERTS)[None])
    put("expert", np.arange(EXPERTS)[None])
    put("turn", np.arange(EXPERTS + 1)[None] - AHEAD)
    t = np.arange(3)[None] * P + np.arange(P)[:, None]
    put("valid", (t < T0).astype(np.float32))
    put("far", np.tile((t >= T0) * 1.0e6, (1, 2)))
    put("eps", [[EPS]])
    half = ROT // 2
    inv = np.float32(THETA) ** (-np.arange(0, ROT, 2, dtype=np.float32) / np.float32(ROT))
    ang = np.arange(T0, dtype=np.float32)[None] * inv.astype(np.float32)[:, None]
    cos, sin = np.ones((P, T0), np.float32), np.zeros((P, T0), np.float32)
    for base in (0, HEAD_DIM):
        for k in range(half):
            cos[base + k] = cos[base + half + k] = np.cos(ang[k])
            sin[base + k] = -np.sin(ang[k])
            sin[base + half + k] = np.sin(ang[k])
    CONST_AT["late"] = (at, None)
    put("cos", cos)
    put("sin", sin)
    for i in range(2):
        q = META + i * P + np.arange(P)
        keys = np.arange(KEYS[i])
        cid = lambda p: np.where(p < META, 0, 1 + (p - META) // CHUNK)
        put(f"mask{i}", np.where(cid(keys)[None] <= cid(q)[:, None], 0.0, -BIG))
    return np.ascontiguousarray(np.concatenate(parts, axis=1), dtype=np.float32)


KEYS = [META + P, T0]
CONSTS = make_constants()

VEC_AT = {"b_pw1": 0, "b_dw": 16, "ln_g": 24, "ln_b": 32, "b_pw2": 40, "post_g": 48, "post_b": 80, "subln": 112}
VEC_ROWS = 113

SWAP = [k + 8 if k < 8 else k - 8 if k < 16 else k for k in range(32)]


def trunk(nc, a, out):
    with ExitStack() as ctx:
        def sb(name, shape, dt=F32):
            return ctx.enter_context(nc.sbuf_tensor(name, shape, dt))

        sems = {}

        def sem(name):
            if name not in sems:
                sems[name] = ctx.enter_context(nc.semaphore(name))
            return sems[name]

        ring = sb("ring", [P, RING, BRICK])
        const = sb("const", [P, CONSTS.shape[1]])
        vec = sb("vec", [P, VEC_ROWS])
        wdw = sb("wdw", [P, TAPS * NC_])
        wr = sb("wr", [P, 2, NC_, 20])
        br = sb("br", [20, 2])
        lamv = sb("lamv", [P, 4, HEAD_DIM])
        tok = sb("tok", [P, 3, D])
        xT = sb("xT", [P, NC_, T0])
        work = sb("work", [P, 7104])
        small = sb("small", [P, 640])
        tab = sb("tab", [1, 2, ORDER + EXPERTS], I32)
        pos_i = sb("pos_i", [P, 2, 6], I32)
        ps = ctx.enter_context(nc.psum_tensor("ps", [P, 8, 512], F32))
        ybuf = [nc.dram_tensor(f"ybuf{l}", ((MAX_ITEMS + 1) * SLOTS, D), F32, kind="Internal").ap() for l in range(2)]

        def cst(name):
            lo, hi = CONST_AT[name]
            return const[:, lo:hi]

        ident = cst("ident")

        def view(lo, *dims, rows=P):
            n = int(np.prod(dims))
            v = work[0:rows, lo:lo + n]
            if len(dims) == 2:
                v = v.rearrange("p (a b) -> p a b", b=dims[1])
            return v

        def diag(i):
            return tok[:, i % 16 // NC_, (i % NC_) * P:(i % NC_ + 1) * P]

        glu = view(0, NC_, PAD + T0)
        cv = view(2416, NC_, T0)
        sq = view(4592, NC_, T0)
        sig = view(4592, 2, T0)
        vrow = view(5200, 3, P)
        xg, hs = view(0, 256), view(256, 256)
        ysb = view(1440, 2, 256)
        xTg = view(768, NC_, SLOTS)
        hT = view(1024, 4, SLOTS)
        pick = view(1152, 3, SLOTS)
        peq = view(1248, 6, SLOTS)
        rows_of = [[view(2560, 2, D), view(4608, 2, D), view(0, 2, D)],
                   [view(2560, 2, D), xT[:, :, :].rearrange("p c t -> p (c t)")[:, 0:2 * D].rearrange("p (a b) -> p a b", b=D)]]
        lnrow = view(4608, 2, D)
        kT = view(0, HEADS, T0)
        qT = view(2176, HEADS, SEQ)
        oT = qT
        raw = view(4224, 2, T0)
        swp = view(4768, T0)
        qz = view(4224, 4, SEQ)
        prob = view(5248, 2, 2 * T0)
        pdT = view(6336, 2, 3 * P)
        vtok = tok
        rawsq = kT
        rstd = view(0, T0)
        std = view(T0, T0)
        o_ = 0

        def sm(n, *dims):
            nonlocal o_
            v = small[:, o_:o_ + n]
            o_ += n
            if len(dims) == 2:
                v = v.rearrange("p (a b) -> p a b", b=dims[1])
            if len(dims) == 3:
                v = v.rearrange("p (a b c) -> p a b c", b=dims[1], c=dims[2])
            return v

        lg = sm(60, 3, 20)
        gmax, gsum, gw, sel = sm(3), sm(3), sm(3), sm(3)
        geq, gex, cand, gone = sm(12, 3, 4), sm(12, 3, 4), sm(12, 3, 4), sm(12, 3, 4)
        el, oh1, oh2, el2 = sm(12, 3, 4), sm(12, 3, 4), sm(12, 3, 4), sm(12, 3, 4)
        m1, m2, e2, wsum = sm(3), sm(3), sm(3), sm(3)
        wts = sm(6, 2, 3)
        AA = sm(96, 2, 3, 16)
        Asum = sm(48, 3, 16)
        rk, bs, qn, pos = sm(6), sm(6), sm(6), sm(6)
        nit, table, ebase = sm(16), sm(ORDER + EXPERTS), sm(16)
        key, srt, srt2, turn_of = sm(16), sm(13), sm(13), sm(16)
        live13, live, live2 = sm(13), sm(1), sm(1)
        bn, mv, tstd, trs = sm(12), sm(6, 3, 2), sm(3), sm(3)
        lam2, lame, nlam, subg = sm(2), sm(2), sm(1), sm(1)
        mx, den, rden, r2 = sm(4, 2, 2), sm(4, 2, 2), sm(4, 2, 2), sm(2)
        alpha_b = sm(8)
        assert o_ <= 640
        lgT = view(544, 3 * P)
        PROD, PROD2 = 1000, 1300

        def prod4(lo, dims):
            v = work[:, lo:lo + int(np.prod(dims))]
            return v.rearrange("p (a b c) -> p a b c", b=dims[1], c=dims[2])

        def V(name, k):
            return vec[:, VEC_AT[name] + k:VEC_AT[name] + k + 1]

        def tap(k, c):
            return wdw[:, k * NC_ + c:k * NC_ + c + 1]

        def sq_of(l):
            return sq if l == 0 else view(2176, NC_, SEQ)

        stream = [xT, xT[:, :, META:T0]]

        def brick(b):
            return ring[:, b % RING, :]

        PW1, PW2, E0 = 0, 4, 6
        KB = E0 + 3 * EXPERTS
        VB, QB, OB, E1 = KB + 2, KB + 4, KB + 6, KB + 8
        START = [E0, E1]

        def arrived(b, half, it=0):
            return sem(f"brick{b % RING}_{half}"), (b // RING + 1 + it) * 16

        block = ctx.enter_context(nc.Block())

        @block.sync
        def _(sp):
            def skip(b, it):
                for half in range(2):
                    sp.wait_ge(*arrived(b - 1, half, it))
                    sp.sem_inc(sem(f"brick{b % RING}_{half}"), 16)

            def load(b, k, src, it=0):
                dst = brick(b).rearrange("p (k n) -> p k n", k=k)
                for half in range(2):
                    if b > PW2:
                        sp.wait_ge(*arrived(b - 1, half, it))
                    r = slice(half * k // 2, (half + 1) * k // 2)
                    sp.dma_start(dst[:, r, :], src[:, r, :]).then_inc(sem(f"brick{b % RING}_{half}"), 16)

            sp.dma_start(tok[0:META, 0, :], a["meta_tokens"]).then_inc(sem("in_x"), 16)
            sp.dma_start(tok[META:P, 0, :], a["x"][0, 0:P - META, :]).then_inc(sem("in_x"), 16)
            sp.dma_start(tok[:, 1, :], a["x"][0, P - META:2 * P - META, :]).then_inc(sem("in_x"), 16)
            sp.wait_ge(sem("tok_zero"), 1)
            sp.dma_start(tok[0:META, 2, :], a["x"][0, 2 * P - META:SEQ, :]).then_inc(sem("in_x"), 16)

            pw1 = a["conv_w_pw1"][0].rearrange("(k p) (s n) -> p k s n", p=P, s=2)
            for b in range(4):
                for s in range(2):
                    sp.dma_start(brick(b).rearrange("p (k s n) -> p k s n", k=NC_, s=2)[:, :, s, :],
                                 pw1[:, :, s, b * 256:(b + 1) * 256]).then_inc(sem(f"brick{b}_{s}"), 16)

            def dense(b, w, half):
                load(b, NC_, w.rearrange("(k p) n -> p k n", p=P)[:, :, half * 512:(half + 1) * 512])

            for half in range(2):
                dense(PW2 + half, a["conv_w_pw2"][0], half)

            def expert(l, b, e, waits, it=0):
                for m, name in enumerate(("moe_w1", "moe_w3", "moe_w2")):
                    waits[m]()
                    k = NC_ if m < 2 else 4
                    if isinstance(e, int):
                        src = a[name][l, e]
                    else:
                        src = a[name][l, bass.ds(e, 1)].rearrange("o r n -> (o r) n")
                    load(b + m, k, src.rearrange("(k p) n -> p k n", p=P), it)

            def hold(name, n):
                return lambda: sp.wait_ge(sem(name), n)

            nothing = lambda: None

            def experts(l, first_waits):
                b = START[l]
                for e in range(3):
                    expert(l, b + 3 * e, e, first_waits[3 * e:3 * e + 3])
                sp.wait_ge(sem("tab_ready"), l + 1)

                def later(bb, turn, it=0):
                    e = sp.value_load(tab[0:1, l, bass.ds(turn + ORDER, 1)], min_val=AHEAD, max_val=EXPERTS - 1)
                    n = sp.value_load(tab[0:1, l, bass.ds(turn - (AHEAD - 1), 1)], min_val=0, max_val=MAX_ITEMS)
                    lo = sp.value_load(tab[0:1, l, bass.ds(turn, 1)], min_val=0, max_val=MAX_ITEMS)
                    hi = sp.value_load(tab[0:1, l, bass.ds(turn + 1, 1)], min_val=0, max_val=MAX_ITEMS)
                    w13 = lambda: sp.wait_ge(sem(f"h_ready{l}"), n + 1)
                    w2 = lambda: sp.wait_ge(sem(f"y_ready{l}"), n + 1)
                    with sp.If(hi - lo):
                        expert(l, bb, e, [w13, nothing, w2], it)
                    with sp.Else():
                        for m in range(3):
                            skip(bb + m, it)

                with sp.Fori(0, 4) as it:
                    for k in range(3):
                        later(b + RING + 3 * k, it * 3 + (k + AHEAD), it)
                later(b + RING * 5, EXPERTS - 1)

            experts(0, [nothing] * 3 + [hold("pw1_ready", 2 * k + 2) for k in range(4)]
                    + [hold("m_ready0", 4), hold("m_ready0", 8)])

            for n, (b, w) in enumerate(((KB, a["kv_w_k"]), (VB, a["kv_w_v"]), (QB, a["attn_w_q"][0]), (OB, a["attn_w_o"][0]))):
                if b == VB:
                    for c in range(2):
                        sp.wait_ge(sem(f"rows{TILES[0] - 1}{c}"), 16)
                for half in range(2):
                    old = (b + half - RING - E0)
                    items = sp.value_load(tab[0:1, 0, old // 3 + 1:old // 3 + 2], min_val=1, max_val=MAX_ITEMS)
                    sp.wait_ge(sem("y_ready0" if old % 3 == 2 else "h_ready0"), items + 1)
                    dense(b + half, w, half)
            last = sp.value_load(tab[0:1, 0, EXPERTS:EXPERTS + 1], min_val=MIN_ITEMS, max_val=MAX_ITEMS)
            experts(1, [lambda: sp.wait_ge(sem("y_ready0"), last + 1), hold("kq_ready", 4), hold("kq_ready", 8),
                        hold("v_ready", 5), nothing, hold("kq_ready", 12),
                        hold("kq_ready", 16), hold("m_ready1", 4), hold("m_ready1", 8)])

            for j in range(2):
                sp.wait_ge(sem("out_tile"), j + 1)
                sp.dma_start(out[0, j * P:(j + 1) * P, :], rows_of[1][j][:, 0, :]).then_inc(sem("stored"), 16)
            sp.wait_ge(sem("stored"), 32)

        def heads(pool):
            pool.wait_ge(sem("rope_ready"), 2 * NC_)
            pool.memset(qz[64:128, 0:4:2, :], 0.0).then_inc(sem("qz_ready"), 1)
            pool.memset(qz[0:64, 1:4:2, :], 0.0).then_inc(sem("qz_ready"), 1)
            pool.wait_ge(sem("qz_ready"), 2)
            pool.memset(pdT[:, 0, P:2 * P], 0.0).then_inc(sem("pdT_zero"), 1)
            pool.memset(pdT[:, 1, 2 * P:3 * P], 0.0).then_inc(sem("pdT_zero"), 1)
            pool.wait_ge(sem("pdT_zero"), 2)
            for h in range(HEADS):
                if h >= 2:
                    pool.wait_ge(sem("scores_ready"), 2 * h - 2)
                for c in range(2):
                    r = slice(64 * c, 64 * c + 64)
                    pool.tensor_copy(qz[r, 2 * (h % 2) + c, :], qT[r, h, :]).then_inc(sem("qz_ready"), 1)
                    pool.wait_ge(sem("qz_ready"), 2 * h + c + 3)

        @block.gpsimd
        def _(pool):
            pool.memset(glu[:, :, 0:PAD], 0.0).then_inc(sem("pad_zero"), 1)
            pool.memset(tok[:, 2, :], 0.0).then_inc(sem("tok_zero"), 1)
            for l in range(2):
                pool.wait_ge(sem("tab_ready"), l + 1)
                n = pool.value_load(tab[0:1, l, EXPERTS:EXPERTS + 1], min_val=MIN_ITEMS, max_val=MAX_ITEMS)
                pool.wait_ge(sem(f"tok_ready{l}"), 2 * TILES[l])
                with pool.Fori(n, MAX_ITEMS + 1) as g:
                    pool.dma_start(ybuf[l][bass.ds(g * SLOTS, SLOTS), :], tok[0:SLOTS, 0, :]).then_inc(sem(f"y_filled{l}"), 16)
                left = pool.value_load(tab[0:1, l, EXPERTS + 1:EXPERTS + 2], min_val=1, max_val=MAX_ITEMS)
                pool.wait_ge(sem(f"y_filled{l}"), left * 16)
                pool.wait_ge(sem(f"y_stored{l}_0"), ((n + 1) >> 1) * 16 + 16)
                pool.wait_ge(sem(f"y_stored{l}_1"), (n >> 1) * 16 + 16)
                pool.wait_ge(sem(f"xT_ready{l}"), n + 1)
                pool.sem_inc(sem("items_over"), 1)
                pool.wait_ge(sem("pos_ready"), l + 1)
                for j in range(TILES[l]):
                    rows = min(P, TOKENS[l] - j * P)
                    for c in range(2):
                        pool.indirect_dma_start(
                            out=rows_of[l][j][0:rows, c, :], out_offset=None, in_=ybuf[l],
                            in_offset=bass.IndirectOffsetOnAxis(ap=pos_i[0:rows, l, c * 3 + j:c * 3 + j + 1], axis=0),
                        ).then_inc(sem(f"rows{j}{c}"), 16)
                if l == 0:
                    heads(pool)

        @block.tensor
        def _(pe):
            pe.wait_ge(sem("in_const"), 16)
            pe.wait_ge(sem("in_x"), 64)
            for j in range(3):
                rows = min(P, T0 - j * P)
                for q in range(2):
                    for c in range(4):
                        last = pe.transpose(ps[:, 2 * j + q, c * rows:(c + 1) * rows],
                                            tok[0:rows, j, (4 * q + c) * P:(4 * q + c + 1) * P], ident[0:rows, 0:rows])
                    last.then_inc(sem("x_turned"), 1)
            pe.wait_ge(sem("x_moved"), 6)
            for c in range(NC_):
                if c % 2 == 0:
                    for s in range(2):
                        pe.wait_ge(*arrived(c // 2, s))
                if c >= 2:
                    pe.wait_ge(sem("glu_ready"), c - 1)
                w = brick(c // 2).rearrange("p (k s n) -> p k s n", k=NC_, s=2)
                for s in range(2):
                    for k in range(NC_):
                        last = pe.matmul(ps[:, 2 * (c % 2) + s, 0:T0], w[:, k, s, (c % 2) * P:(c % 2 + 1) * P],
                                         xT[:, k, :], start=(k == 0), stop=(k == NC_ - 1))
                last.then_inc(sem("pw1_ready"), 1)
                if c == 0:
                    pe.wait_ge(sem("in_vec"), 16 * 8)
                    pe.wait_ge(sem("in_taps"), 32)
                    pe.transpose(ps[:, 6, 0:VEC_ROWS], vrow[0:VEC_ROWS, 0, :], ident[0:VEC_ROWS, 0:VEC_ROWS])
                    pe.transpose(ps[:, 7, 0:P], vrow[:, 1, :], ident)
                    pe.transpose(ps[:, 7, P:P + 120], vrow[0:120, 2, :], ident[0:120, 0:120]).then_inc(sem("vec_turned"), 1)

            def norm_sums(turn, src, squares, T, weight, src_sem, src_n):
                for k in range(NC_):
                    if turn == 0 and k >= DVE_CHUNKS:
                        pe.wait_ge(sem("conv_moved"), k - DVE_CHUNKS + 1)
                    else:
                        pe.wait_ge(sem(src_sem), src_n + k + 1)
                    last = pe.matmul(ps[:, 4, 0:T], cst(weight), src[:, k, 0:T], start=(k == 0), stop=(k == NC_ - 1))
                last.then_inc(sem("mean_ready"), 1)
                pe.wait_ge(sem("sq_ready"), turn + 1)
                for k in range(NC_):
                    last = pe.matmul(ps[:, 5, 0:T], cst(weight), squares[:, k, 0:T], start=(k == 0), stop=(k == NC_ - 1))
                last.then_inc(sem("var_ready"), 1)

            def project(b0, src, lo, T, ready, free, n0=0, banks=4):
                for c in range(NC_):
                    if c % 4 == 0:
                        for half in range(2):
                            pe.wait_ge(*arrived(b0 + c // 4, half))
                    w = brick(b0 + c // 4).rearrange("p (k n) -> p k n", k=NC_)
                    n = n0 + c
                    if n >= banks:
                        pe.wait_ge(sem(free), n - banks + 1)
                    for k in range(NC_):
                        last = pe.matmul(ps[:, n % banks, 0:T], w[:, k, (c % 4) * P:(c % 4 + 1) * P],
                                         src[:, k, lo:lo + T], start=(k == 0), stop=(k == NC_ - 1))
                    last.then_inc(sem(ready), 1)

            def post_norm_and_route(l):
                T, n = TOKENS[l], TILES[l]
                norm_sums(1 + l, stream[l], sq_of(l), T, "mean_d", f"r_ready{l}", 0)
                for k in range(NC_):
                    pe.wait_ge(sem("normed"), (1 + l) * NC_ + k + 1)
                    last = pe.matmul(ps[0:20, 6, 0:T], wr[:, l, k, :], stream[l][:, k, 0:T], start=(k == 0), stop=(k == NC_ - 1))
                last.then_inc(sem("logits_ready"), 1)
                for j in range(n):
                    rows = min(P, T - j * P)
                    for q in range(2):
                        for c in range(4):
                            last = pe.transpose(ps[0:rows, 2 * j + q, c * P:(c + 1) * P],
                                                stream[l][:, 4 * q + c, j * P:j * P + rows], ident)
                        last.then_inc(sem(f"tok_turned{l}"), 1)
                    if j == 0:
                        pe.wait_ge(sem("logits_moved"), l + 1)
                        for i in range(n):
                            last = pe.transpose(ps[:, 7, 64 + 20 * i:84 + 20 * i], lgT[0:20, i * P:(i + 1) * P], ident[0:20, 0:20])
                        last.then_inc(sem("logits_turned"), 1)
                pe.wait_ge(sem("picks_ready"), l + 1)
                for j in range(n):
                    for i in range(j + 1):
                        pe.matmul(ps[:, 7, 16 * j:16 * j + 16], cst("before" if i == j else "ones"),
                                  Asum[:, i, :], start=(i == 0), stop=(i == j))
                for i in range(n):
                    last = pe.matmul(ps[:, 7, 48:64], cst("ones"), Asum[:, i, :], start=(i == 0), stop=(i == n - 1))
                last.then_inc(sem("ranks_ready"), 1)

            def gather(l, g, first):
                pe.wait_ge(sem(f"pick_ready{l}"), g + 1)
                if not first:
                    pe.wait_ge(sem(f"xg_moved{l}"), g)
                for j in range(TILES[l]):
                    for q in range(QUARTERS):
                        last = pe.matmul(ps[SLOTS * q:SLOTS * (q + 1), 2, 0:256], pick[:, j, :],
                                         tok[:, j, q * 256:(q + 1) * 256], start=(j == 0), stop=(j == TILES[l] - 1),
                                         skip_group_check=True)
                last.then_inc(sem(f"xg_ready{l}"), 1)

            def turn_gathered(l, g, first):
                pe.wait_ge(sem(f"xg_moved{l}"), g + 1)
                if not first:
                    pe.wait_ge(sem(f"xT_ready{l}"), g)
                for m in range(2):
                    last = pe.transpose(ps[:, 3, m * P:(m + 1) * P], xg[:, m * P:(m + 1) * P], ident)
                last.then_inc(sem(f"xg_turned{l}"), 1)

            def item(l, g, b, it):
                w1 = brick(b).rearrange("p (k n) -> p k n", k=NC_)
                w3 = brick(b + 1).rearrange("p (k n) -> p k n", k=NC_)
                w2 = brick(b + 2).rearrange("p (k n) -> p k n", k=4)
                pe.wait_ge(sem(f"xT_ready{l}"), g + 1)
                for k in range(NC_):
                    if k % 4 == 0:
                        for m in range(2):
                            pe.wait_ge(*arrived(b + m, k // 4, it))
                    for q in range(QUARTERS):
                        w = (w1, w3)[q // 2]
                        last = pe.matmul(ps[SLOTS * q:SLOTS * (q + 1), 0, 0:256], xTg[:, k, :],
                                         w[:, k, (q % 2) * 256:(q % 2 + 1) * 256], start=(k == 0), stop=(k == NC_ - 1),
                                         skip_group_check=True)
                last.then_inc(sem(f"h_ready{l}"), 1)
                gather(l, g + 1, False)
                pe.wait_ge(sem(f"hs_ready{l}"), g + 1)
                pe.sem_inc(sem("turn_begun"), 1)
                for m in range(2):
                    last = pe.transpose(ps[:, 4, m * 64:(m + 1) * 64], hs[64:128, m * P:(m + 1) * P], ident[64:128, 64:128])
                last.then_inc(sem(f"h_turned{l}"), 1)
                turn_gathered(l, g + 1, False)
                pe.wait_ge(sem(f"hT_ready{l}"), g + 1)
                for k in range(4):
                    if k % 2 == 0:
                        pe.wait_ge(*arrived(b + 2, k // 2, it))
                    for q in range(QUARTERS):
                        last = pe.matmul(ps[SLOTS * q:SLOTS * (q + 1), 1, 0:256], hT[:, k, :], w2[:, k, q * 256:(q + 1) * 256],
                                         start=(k == 0), stop=(k == 3), skip_group_check=True)
                last.then_inc(sem(f"y_ready{l}"), 1)

            def mixture(l):
                pe.sem_inc(sem(f"h_ready{l}"), 1)
                pe.sem_inc(sem(f"y_ready{l}"), 1)
                pe.wait_ge(sem(f"tok_ready{l}"), 2 * TILES[l])
                pe.wait_ge(sem("tab_ready"), l + 1)
                gather(l, 0, True)
                turn_gathered(l, 0, True)

                def expert(b, e, it):
                    lo = pe.value_load(tab[0:1, l, bass.ds(e, 1)], min_val=0, max_val=MAX_ITEMS)
                    hi = pe.value_load(tab[0:1, l, bass.ds(e + 1, 1)], min_val=0, max_val=MAX_ITEMS)
                    with pe.If(hi - lo):
                        with pe.Fori(lo, hi) as g:
                            item(l, g, b, it)

                with pe.Fori(0, 5) as it:
                    for k in range(3):
                        expert(START[l] + 3 * k, it * 3 + k, it)
                expert(START[l] + 45, EXPERTS - 1, 0)

            for i in range(DIAGS):
                k, c = i % TAPS, DVE_CHUNKS + i // TAPS
                if k == 0:
                    pe.wait_ge(sem("glu_ready"), c + 1)
                pe.wait_ge(sem("diag_ready"), i + 1)
                pe.matmul(ps[:, 6 + i // TAPS, 0:T0], diag(i), glu[:, c, k:k + T0],
                          start=(k == 0), stop=(k == TAPS - 1)).then_inc(sem("diag_used"), 1)
            norm_sums(0, cv, sq, T0, "mean_d", "conv_ready", 0)
            pe.wait_ge(sem("normed"), NC_)
            pe.wait_ge(sem("x_scaled0"), 1)
            project(PW2, cv, 0, T0, "m_ready0", "r_ready0")
            post_norm_and_route(0)
            mixture(0)

            for j in range(3):
                rows = min(P, T0 - j * P)
                pe.wait_ge(sem("z_ready0"), j + 1)
                for q in range(2):
                    for c in range(4):
                        last = pe.transpose(ps[:, 2 * j + q, c * rows:(c + 1) * rows],
                                            rows_of[0][j][0:rows, 0, (4 * q + c) * P:(4 * q + c + 1) * P], ident[0:rows, 0:rows])
                    last.then_inc(sem("z_turned"), 1)

            pe.wait_ge(sem("xT_back"), 24)
            project(KB, xT, 0, T0, "kq_ready", "kq_moved", 0)
            for i, (j, half) in enumerate(((0, 0), (1, 0), (0, 1), (1, 1))):
                w = brick(VB + half).rearrange("p (k n) -> p k n", k=NC_)
                for part in range(2):
                    pe.wait_ge(*arrived(VB + half, part))
                for k in range(NC_):
                    last = pe.matmul(ps[:, 4 + i, :], xT[:, k, j * P:(j + 1) * P], w[:, k, :], start=(k == 0), stop=(k == NC_ - 1))
                last.then_inc(sem("v_ready"), 1)
            pe.wait_ge(sem("v_moved"), 1)
            for k in range(NC_):
                for half in range(2):
                    w = brick(VB + half).rearrange("p (k n) -> p k n", k=NC_)
                    last = pe.matmul(ps[32 * half:32 * half + META, 4, :], xT[:, k, 2 * P:T0], w[:, k, :],
                                     start=(k == 0), stop=(k == NC_ - 1), skip_group_check=True)
            last.then_inc(sem("v_ready"), 1)
            project(QB, xT, META, SEQ, "kq_ready", "kq_moved", NC_)

            pe.wait_ge(sem("kq_moved"), 2 * NC_)
            UNITS = 2 * HEADS

            def scores(u):
                h, i = u // 2, u % 2
                pe.wait_ge(sem("rope_ready"), NC_ + h + 1)
                if u >= 2:
                    pe.wait_ge(sem("scores_moved"), u - 1)
                pe.wait_ge(sem("qz_ready"), 2 * h + 4)
                for c in range(2):
                    last = pe.matmul(ps[:, 2 * (u % 2) + c, 0:KEYS[i]], qz[:, 2 * (h % 2) + c, i * P:(i + 1) * P],
                                     kT[:, h, 0:KEYS[i]], start=True, stop=True)
                last.then_inc(sem("scores_ready"), 1)

            def turn_probs(u):
                i = u % 2
                pe.wait_ge(sem("pd_ready"), u + 1)
                if u == 0:
                    pe.wait_ge(sem("v_moved"), 6)
                if u >= 2:
                    pe.wait_ge(sem("pdT_ready"), u - 1)
                for j in range((KEYS[i] + P - 1) // P):
                    w = min(P, KEYS[i] - j * P)
                    last = pe.transpose(ps[0:w, 4 + u % 2, j * P:(j + 1) * P], prob[:, u % 2, j * P:j * P + w], ident)
                last.then_inc(sem("pd_turned"), 1)

            def values(u):
                h, i = u // 2, u % 2
                pe.wait_ge(sem("pdT_ready"), u + 1)
                if i == 0 and h >= 2:
                    pe.wait_ge(sem("o_moved"), h - 1)
                n = (KEYS[i] + P - 1) // P
                for j in range(n):
                    last = pe.matmul(ps[:, 6 + h % 2, i * P:(i + 1) * P], vtok[:, j, h * P:(h + 1) * P],
                                     pdT[:, u % 2, j * P:(j + 1) * P], start=(j == 0), stop=(j == n - 1))
                last.then_inc(sem("pv_ready"), 1)

            for u in range(UNITS + 2):
                if u < UNITS:
                    scores(u)
                if 1 <= u <= UNITS:
                    turn_probs(u - 1)
                if u >= 2:
                    values(u - 2)
            pe.wait_ge(sem("osq_ready"), 1)
            for h in range(HEADS):
                last = pe.matmul(ps[:, h // 2, (h % 2) * SEQ:(h % 2 + 1) * SEQ], cst("mean_v"), rawsq[:, h, 0:SEQ],
                                 start=True, stop=True)
            last.then_inc(sem("oms_ready"), 1)
            pe.wait_ge(sem("o_normed"), 1)
            pe.wait_ge(sem("x_scaled1"), 1)
            project(OB, oT, 0, SEQ, "m_ready1", "r_ready1")
            post_norm_and_route(1)
            mixture(1)

        @block.scalar
        def _(act):
            late = CONST_AT["late"][0]
            act.dma_start(const[:, 0:late], a["consts"][:, 0:late]).then_inc(sem("in_const"), 16)
            rows = vrow[:, 0, :]
            for name, src in (("b_pw1", a["conv_b_pw1"]), ("b_dw", a["conv_b_dw"]), ("ln_g", a["conv_ln_g"]),
                              ("ln_b", a["conv_ln_b"]), ("b_pw2", a["conv_b_pw2"]), ("subln", a["attn_subln_g"])):
                n = src.shape[0] * src.shape[1] // P
                act.dma_start(rows[VEC_AT[name]:VEC_AT[name] + n, :],
                              src.rearrange("l (c p) -> (l c) p", p=P)).then_inc(sem("in_vec"), 16)
            for name, src in (("post_g", a["post_ln_g"]), ("post_b", a["post_ln_b"])):
                act.dma_start(rows[VEC_AT[name]:VEC_AT[name] + 32, :],
                              src.rearrange("l s (c p) -> (l s c) p", p=P)).then_inc(sem("in_vec"), 16)
            taps = a["conv_w_dw"][0].rearrange("k (c p) -> (k c) p", p=P)
            act.dma_start(vrow[:, 1, :], taps[0:P, :]).then_inc(sem("in_taps"), 16)
            act.dma_start(vrow[0:120, 2, :], taps[P:P + 120, :]).then_inc(sem("in_taps"), 16)

            def move(dst, src):
                return act.activation(dst, src, ACT.Copy)

            for j in range(3):
                rows_ = min(P, T0 - j * P)
                act.wait_ge(sem("x_turned"), 2 * j + 1)
                move(xT[:, 0:4, j * P:j * P + rows_],
                     ps[:, 2 * j, 0:4 * rows_].rearrange("p (c t) -> p c t", c=4)).then_inc(sem("x_moved"), 1)
            act.wait_ge(sem("vec_ready"), 2)
            act.wait_ge(sem("x_turned"), 6)

            def build_diags(first, last):
                for i in range(first, last):
                    if i >= 16:
                        act.wait_ge(sem("diag_used"), i - 15)
                    act.activation(diag(i), ident, ACT.Copy, scale=tap(i % TAPS, DVE_CHUNKS + i // TAPS)).then_inc(sem("diag_ready"), 1)

            build_diags(0, 8)
            for c in range(NC_):
                act.wait_ge(sem("pw1_ready"), c + 1)
                if c >= 2:
                    act.wait_ge(sem("glu_ready"), c - 1)
                act.activation(sig[:, c % 2, :], ps[:, 2 * (c % 2) + 1, 0:T0], ACT.Sigmoid,
                               bias=V("b_pw1", 8 + c)).then_inc(sem("sig_ready"), 1)
                if c in (2, 3):
                    build_diags(4 * c, 4 * c + 4)
            build_diags(16, DIAGS)
            for i in range(NC_ - DVE_CHUNKS):
                act.wait_ge(sem("diag_used"), (i + 1) * TAPS)
                act.activation(cv[:, DVE_CHUNKS + i, :], ps[:, 6 + i, 0:T0], ACT.Identity,
                               bias=V("b_dw", DVE_CHUNKS + i)).then_inc(sem("conv_moved"), 1)
            for c in range(NC_):
                last = act.activation(xT[:, c, :], xT[:, c, :], ACT.Identity, scale=ALPHA, bias=alpha_b[:, c:c + 1])
            last.then_inc(sem("x_scaled0"), 1)
            act.dma_start(const[:, late:], a["consts"][:, late:]).then_inc(sem("in_const_late"), 16)
            for l in range(2):
                act.dma_start(wr[:, l, :, 0:GROUPS], a["moe_w_group"][l].rearrange("(k p) n -> p k n", p=P)).then_inc(sem("in_router"), 16)
                act.dma_start(wr[:, l, :, GROUPS:20], a["moe_w_expert"][l].rearrange("(k p) n -> p k n", p=P)).then_inc(sem("in_router"), 16)
                act.dma_start(br[0:GROUPS, l:l + 1], a["moe_b_group"][l:l + 1, :].rearrange("o n -> n o")).then_inc(sem("in_router"), 16)
                act.dma_start(br[GROUPS:20, l:l + 1], a["moe_b_expert"][l:l + 1, :].rearrange("o n -> n o")).then_inc(sem("in_router"), 16)
            for k, name in enumerate(("attn_lam_q1", "attn_lam_k1", "attn_lam_q2", "attn_lam_k2")):
                act.dma_start(lamv[:, k, :], a[name].broadcast_to([P, HEAD_DIM])).then_inc(sem("in_lam"), 16)

            def norm(turn, src, squares, dst, T, func, gain, bias):
                act.wait_ge(sem("centred"), turn + 1)
                act.activation(squares[:, :, 0:T], src[:, :, 0:T], ACT.Square).then_inc(sem("sq_ready"), 1)
                act.wait_ge(sem("var_ready"), turn + 1)
                act.activation(std[:, 0:T], ps[:, 5, 0:T], ACT.Sqrt, bias=cst("eps")).then_inc(sem("std_ready"), 1)
                act.wait_ge(sem("scaled"), turn + 1)
                for c in range(NC_):
                    act.activation(dst[:, c, 0:T], src[:, c, 0:T], func, scale=gain(c),
                                   bias=bias(c)).then_inc(sem("normed"), 1)

            def post(l):
                T, n = TOKENS[l], TILES[l]
                norm(1 + l, stream[l], sq_of(l), stream[l], T, ACT.Identity,
                     lambda c: V("post_g", 16 * l + c), lambda c: V("post_b", 16 * l + c))
                act.wait_ge(sem("logits_ready"), l + 1)
                act.wait_ge(sem("pad_ready"), l + 1)
                act.activation(lgT[0:20, 0:T], ps[0:20, 6, 0:T], ACT.Identity, bias=br[0:20, l:l + 1]).then_inc(sem("logits_moved"), 1)
                for j in range(n):
                    rows_ = min(P, T - j * P)
                    act.wait_ge(sem(f"tok_turned{l}"), 2 * j + 1)
                    if j == 0:
                        move(tok[0:rows_, j, 0:512], ps[0:rows_, 0, :]).then_inc(sem(f"tok_ready{l}"), 1)
                        act.wait_ge(sem("gsub_ready"), l + 1)
                        act.activation(gex[:, 0:n, :], gex[:, 0:n, :], ACT.Exp).then_inc(sem("gex_ready"), 1)
                    else:
                        move(tok[0:rows_, j, 0:512], ps[0:rows_, 2 * j, :]).then_inc(sem(f"tok_ready{l}"), 1)
                act.wait_ge(sem("e2_sub"), l + 1)
                act.activation(e2[:, 0:n], e2[:, 0:n], ACT.Exp).then_inc(sem("e2_ready"), 1)

            def mixture(l):
                act.wait_ge(sem("tab_ready"), l + 1)
                n = act.value_load(tab[0:1, l, EXPERTS:EXPERTS + 1], min_val=MIN_ITEMS, max_val=MAX_ITEMS)
                act.wait_ge(sem(f"xg_ready{l}"), 1)
                move(xg, ps[:, 2, 0:256]).then_inc(sem(f"xg_moved{l}"), 1)
                for buf in range(2):
                    act.sem_inc(sem(f"y_stored{l}_{buf}"), 16)

                def item(g, buf, turn):
                    act.wait_ge(sem(f"h_ready{l}"), g + 2)
                    act.activation(hs[64:128, :], ps[0:64, 0, 0:256], ACT.Silu).then_inc(sem(f"silu_ready{l}"), 1)
                    act.wait_ge(sem(f"xg_ready{l}"), g + 2)
                    act.wait_ge(sem(f"xg_turned{l}"), g + 1)
                    move(xg, ps[:, 2, 0:256]).then_inc(sem(f"xg_moved{l}"), 1)
                    act.wait_ge(sem(f"y_ready{l}"), g + 2)
                    act.wait_ge(sem(f"y_stored{l}_{buf}"), turn * 16 + 16)
                    move(ysb[:, buf, :], ps[:, 1, 0:256]).then_inc(sem(f"y_moved{l}"), 1)
                    act.wait_ge(sem(f"y_moved{l}"), g + 1)
                    act.dma_start(ybuf[l][bass.ds(g * SLOTS, SLOTS), :].rearrange("s (q c) -> q s c", q=QUARTERS),
                                  ysb[:, buf, :]).then_inc(sem(f"y_stored{l}_{buf}"), 16)

                with act.Fori(0, n >> 1) as turn:
                    item(turn * 2, 0, turn)
                    item(turn * 2 + 1, 1, turn)
                with act.If(n & 1):
                    item(n - 1, 0, n >> 1)

            def combine(l):
                if l == 1:
                    act.wait_ge(sem("attn_over"), 1)
                for j in range(TILES[l]):
                    rows_ = min(P, TOKENS[l] - j * P)
                    act.wait_ge(sem(f"rows{j}0"), 16 * l + 16)
                    r = rows_of[l][j]
                    act.activation(r[0:rows_, 0, :], r[0:rows_, 0, :], ACT.Copy, scale=wts[0:rows_, 0, j:j + 1]).then_inc(sem(f"first_scaled{l}"), 1)
                for j in range(TILES[l]):
                    rows_ = min(P, TOKENS[l] - j * P)
                    act.wait_ge(sem(f"stats_ready{l}"), j + 1)
                    act.activation(tstd[0:rows_, j:j + 1], mv[0:rows_, j, 1:2], ACT.Sqrt, bias=cst("eps")[0:rows_, :]).then_inc(sem(f"tstd_ready{l}"), 1)

            norm(0, cv, sq, cv, T0, ACT.Silu, lambda c: V("ln_g", c), lambda c: V("ln_b", c))
            act.wait_ge(sem("in_router"), 128)
            post(0)
            mixture(0)
            combine(0)
            for j in range(3):
                rows_ = min(P, T0 - j * P)
                act.wait_ge(sem("z_turned"), 2 * j + 1)
                for c in range(4):
                    act.activation(xT[:, c, j * P:j * P + rows_], ps[:, 2 * j, c * rows_:(c + 1) * rows_], ACT.Identity,
                                   scale=V("post_g", 8 + c), bias=V("post_b", 8 + c)).then_inc(sem("xT_back"), 1)
            for c in range(NC_):
                act.wait_ge(sem("kq_ready"), c + 1)
                if c >= 2:
                    act.wait_ge(sem("rope_ready"), c - 1)
                move(raw[:, c % 2, :], ps[:, c % 4, 0:T0]).then_inc(sem("kq_moved"), 1)
            for i, (j, half) in enumerate(((0, 0), (1, 0), (0, 1), (1, 1))):
                act.wait_ge(sem("v_ready"), i + 1)
                move(vtok[:, j, half * 512:(half + 1) * 512], ps[:, 4 + i, :]).then_inc(sem("v_moved"), 1)
            act.wait_ge(sem("v_ready"), 5)
            for half in range(2):
                move(vtok[0:META, 2, half * 512:(half + 1) * 512], ps[32 * half:32 * half + META, 4, :]).then_inc(sem("v_moved"), 1)
            for c in range(NC_):
                n = NC_ + c
                act.wait_ge(sem("kq_ready"), n + 1)
                act.wait_ge(sem("rope_ready"), n - 1)
                move(raw[:, n % 2, 0:SEQ], ps[:, n % 4, 0:SEQ]).then_inc(sem("kq_moved"), 1)
            for c in range(NC_):
                last = act.activation(stream[1][:, c, :], stream[1][:, c, :], ACT.Copy, scale=ALPHA)
            last.then_inc(sem("x_scaled1"), 1)
            act.wait_ge(sem("lam_sums"), 2)
            act.activation(lame, lam2, ACT.Exp).then_inc(sem("lam_exp"), 1)
            for u in range(2 * HEADS):
                h, i = u // 2, u % 2
                act.wait_ge(sem("max_ready"), u + 1)
                for c in range(2):
                    p_ = prob[:, u % 2, c * T0:c * T0 + KEYS[i]]
                    act.activation(p_, p_, ACT.Exp, bias=mx[:, u % 2, c:c + 1],
                                   accum_out=den[:, u % 2, c:c + 1]).then_inc(sem("exp_ready"), 1)
                if u >= 4 and i == 1:
                    hh = h - 2
                    act.wait_ge(sem("pv_ready"), 2 * hh + 2)
                    act.wait_ge(sem("scores_ready"), 2 * hh + 2)
                    move(oT[:, hh, :], ps[:, 6 + hh % 2, 0:SEQ]).then_inc(sem("o_moved"), 1)
            for hh in (HEADS - 2, HEADS - 1):
                act.wait_ge(sem("pv_ready"), 2 * hh + 2)
                move(oT[:, hh, :], ps[:, 6 + hh % 2, 0:SEQ]).then_inc(sem("o_moved"), 1)
            act.wait_ge(sem("o_moved"), HEADS)
            act.activation(rawsq[:, :, 0:SEQ], oT[:, :, :], ACT.Square).then_inc(sem("osq_ready"), 1)
            act.wait_ge(sem("oms_ready"), 1)
            act.wait_ge(sem("oms_free"), 1)
            act.activation(view(0, 4, 512), ps[:, 0:4, :], ACT.Sqrt, bias=cst("eps")).then_inc(sem("ostd_ready"), 1)
            post(1)
            act.wait_ge(sem("tok_ready1"), 4)
            for k, name in enumerate(("post_ln_g", "post_ln_b")):
                act.dma_start(lnrow[:, k, :], a[name][1, 1:2, :].broadcast_to([P, D])).then_inc(sem("in_lnrow"), 16)
            mixture(1)
            combine(1)

        @block.vector
        def _(dve):
            steps = [0]

            def step(ins):
                steps[0] += 1
                ins.then_inc(sem("dve_step"), 1)
                dve.wait_ge(sem("dve_step"), steps[0])

            for j in range(3):
                rows_ = min(P, T0 - j * P)
                dve.wait_ge(sem("x_turned"), 2 * j + 2)
                dve.tensor_copy(xT[:, 4:8, j * P:j * P + rows_],
                                ps[:, 2 * j + 1, 0:4 * rows_].rearrange("p (c t) -> p c t", c=4)).then_inc(sem("x_moved"), 1)
            dve.wait_ge(sem("vec_turned"), 1)
            dve.tensor_copy(vec[:, :], ps[:, 6, 0:VEC_ROWS]).then_inc(sem("vec_ready"), 1)
            dve.tensor_copy(wdw[:, :], ps[:, 7, 0:TAPS * NC_]).then_inc(sem("vec_ready"), 1)
            dve.wait_ge(sem("vec_ready"), 2)
            dve.wait_ge(sem("pad_zero"), 1)
            step(dve.tensor_copy(alpha_b, vec[:, VEC_AT["b_pw2"]:VEC_AT["b_pw2"] + 8]))

            def gate(c):
                dve.wait_ge(sem("sig_ready"), c + 1)
                dve.scalar_tensor_tensor(glu[:, c, PAD:], ps[:, 2 * (c % 2), 0:T0], V("b_pw1", c), sig[:, c % 2, :],
                                         ALU.add, ALU.mult).then_inc(sem("glu_ready"), 1)

            def convolve(cs, glus, then=lambda k: None):
                dve.wait_ge(sem("glu_ready"), glus)
                first = steps[0]
                for k in range(TAPS):
                    for i, c in enumerate(cs):
                        if k:
                            dve.wait_ge(sem("dve_step"), first + (k - 1) * len(cs) + i + 1)
                            ins = dve.scalar_tensor_tensor(cv[:, c, :], glu[:, c, k:k + T0], tap(k, c), cv[:, c, :], ALU.mult, ALU.add)
                        else:
                            ins = dve.tensor_scalar(cv[:, c, :], glu[:, c, 0:T0], tap(0, c), V("b_dw", c), ALU.mult, ALU.add)
                        if k < TAPS - 1:
                            ins.then_inc(sem("dve_step"), 1)
                            steps[0] += 1
                        else:
                            ins.then_inc(sem("conv_ready"), 1)
                    then(k)

            gate(0)
            gate(1)
            convolve((0, 1), 2, lambda k: gate({9: 2, 20: 3}[k]) if k in (9, 20) else None)
            convolve((2, 3), 4, lambda k: gate({0: 4, 10: 5, 20: 6, 29: 7}[k]) if k in (0, 10, 20, 29) else None)
            convolve((4, 5), 6)

            def over_chunks(t, T):
                return t.unsqueeze(1).broadcast_to([P, NC_, T])

            def norm(turn, src, T, src_sem, src_n=NC_):
                dve.wait_ge(sem(src_sem), src_n)
                dve.wait_ge(sem("mean_ready"), turn + 1)
                dve.tensor_tensor(src[:, :, 0:T], src[:, :, 0:T], over_chunks(ps[:, 4, 0:T], T),
                                  ALU.subtract).then_inc(sem("centred"), 1)
                dve.wait_ge(sem("std_ready"), turn + 1)
                dve.wait_ge(sem("sq_ready"), turn + 1)
                step(dve.reciprocal(rstd[:, 0:T], std[:, 0:T]))
                dve.tensor_tensor(src[:, :, 0:T], src[:, :, 0:T], over_chunks(rstd[:, 0:T], T),
                                  ALU.mult).then_inc(sem("scaled"), 1)

            def residual(l):
                T = TOKENS[l]
                dve.wait_ge(sem(f"x_scaled{l}"), 1)
                for c in range(NC_):
                    dve.wait_ge(sem(f"m_ready{l}"), c + 1)
                    dve.tensor_tensor(stream[l][:, c, 0:T], stream[l][:, c, 0:T], ps[:, c % 4, 0:T], ALU.add).then_inc(sem(f"r_ready{l}"), 1)

            def last_dim(t, n, m):
                return t.unsqueeze(2).broadcast_to([P, n, m])

            def post_and_route(l):
                T, n = TOKENS[l], TILES[l]
                step(dve.memset(lgT[0:20, :], 0.0)) if l == 0 else step(dve.memset(lgT[0:20, 0:SEQ], 0.0))
                dve.engine_nop().then_inc(sem("pad_ready"), 1)
                norm(1 + l, stream[l], T, f"r_ready{l}")
                neg4 = cst("neg4").unsqueeze(1).broadcast_to([P, n, 4])
                dve.wait_ge(sem(f"tok_turned{l}"), 2)
                dve.tensor_copy(tok[:, 0, 512:], ps[:, 1, :]).then_inc(sem(f"tok_ready{l}"), 1)
                dve.wait_ge(sem("logits_turned"), l + 1)
                step(dve.tensor_copy(lg[:, 0:n, :], ps[:, 7, 64:64 + 20 * n].rearrange("p (n e) -> p n e", e=20)))
                G = lg[:, 0:n, 0:4]

                def first_max(values, maxv, onehot):
                    step(dve.tensor_reduce(maxv[:, 0:n], values, AX, ALU.max))
                    step(dve.tensor_tensor(geq[:, 0:n, :], values, last_dim(maxv[:, 0:n], n, 4), ALU.is_equal))
                    step(dve.tensor_tensor(cand[:, 0:n, :], geq[:, 0:n, :], neg4, ALU.mult))
                    step(dve.tensor_reduce(sel[:, 0:n], cand[:, 0:n, :], AX, ALU.min))
                    step(dve.tensor_tensor(onehot[:, 0:n, :], neg4, last_dim(sel[:, 0:n], n, 4), ALU.is_equal))

                first_max(G, gmax, gone)
                dve.tensor_tensor(gex[:, 0:n, :], G, last_dim(gmax[:, 0:n], n, 4), ALU.subtract).then_inc(sem("gsub_ready"), 1)
                chosen = prod4(PROD, (n, 4, 4))
                step(dve.tensor_tensor(chosen, lg[:, 0:n, 4:20].rearrange("p n (g e) -> p n g e", g=4),
                                       gone[:, 0:n, :].unsqueeze(3).broadcast_to([P, n, 4, 4]), ALU.mult))
                step(dve.tensor_reduce(el[:, 0:n, :], chosen.rearrange("p n g e -> p n e g"), AX, ALU.add))
                first_max(el[:, 0:n, :], m1, oh1)
                step(dve.scalar_tensor_tensor(el2[:, 0:n, :], oh1[:, 0:n, :], -BIG, el[:, 0:n, :], ALU.mult, ALU.add))
                first_max(el2[:, 0:n, :], m2, oh2)
                dve.tensor_tensor(e2[:, 0:n], m2[:, 0:n], m1[:, 0:n], ALU.subtract).then_inc(sem("e2_sub"), 1)
                step(dve.tensor_tensor(gone[:, 0:n, :], gone[:, 0:n, :], last_dim(cst("valid")[:, 0:n] if l == 0 else cst("ones")[:, 0:n], n, 4), ALU.mult))
                for c, oh in enumerate((oh1, oh2)):
                    step(dve.tensor_tensor(AA[:, c, 0:n, :].rearrange("p n (g e) -> p n g e", g=4),
                                           gone[:, 0:n, :].unsqueeze(3).broadcast_to([P, n, 4, 4]),
                                           oh[:, 0:n, :].unsqueeze(2).broadcast_to([P, n, 4, 4]), ALU.mult))
                dve.tensor_tensor(Asum[:, 0:n, :], AA[:, 0, 0:n, :], AA[:, 1, 0:n, :], ALU.add).then_inc(sem("picks_ready"), 1)
                dve.wait_ge(sem("gex_ready"), l + 1)
                step(dve.tensor_reduce(gsum[:, 0:n], gex[:, 0:n, :], AX, ALU.add))
                step(dve.reciprocal(gw[:, 0:n], gsum[:, 0:n]))
                dve.wait_ge(sem("e2_ready"), l + 1)
                step(dve.tensor_scalar(wsum[:, 0:n], e2[:, 0:n], 1.0, None, ALU.add))
                step(dve.reciprocal(wsum[:, 0:n], wsum[:, 0:n]))
                step(dve.tensor_tensor(wts[:, 0, 0:n], wsum[:, 0:n], gw[:, 0:n], ALU.mult))
                step(dve.tensor_tensor(wts[:, 1, 0:n], wts[:, 0, 0:n], e2[:, 0:n], ALU.mult))
                step(dve.tensor_copy(turn_of[:, 0:AHEAD], cst("turn")[:, 0:AHEAD]))
                dve.wait_ge(sem("ranks_ready"), l + 1)
                step(dve.tensor_copy(nit, ps[:, 7, 48:64]))
                over = prod4(PROD, (1, 16, FULL))[:, 0]
                step(dve.tensor_tensor(over, nit.unsqueeze(2).broadcast_to([P, 16, FULL]),
                                       cst("full").unsqueeze(1).broadcast_to([P, 16, FULL]), ALU.is_gt))
                step(dve.tensor_reduce(nit, over, AX, ALU.add))
                rest = EXPERTS - AHEAD
                step(dve.scalar_tensor_tensor(key, nit, float(EXPERTS), cst("minus_e"), ALU.mult, ALU.add))
                later, above = key[:, AHEAD:], prod4(PROD, (1, rest, rest))[:, 0]
                step(dve.tensor_tensor(above, later.unsqueeze(1).broadcast_to([P, rest, rest]),
                                       later.unsqueeze(2).broadcast_to([P, rest, rest]), ALU.is_gt))
                step(dve.tensor_reduce(srt, above, AX, ALU.add))
                step(dve.tensor_scalar(live13, nit[:, AHEAD:], 0.0, None, ALU.is_gt))
                step(dve.tensor_reduce(live, live13, AX, ALU.add))
                step(dve.tensor_scalar(live2, live, 2.0, -1.0, ALU.mult, ALU.add))
                step(dve.tensor_scalar(srt2, srt, -2.0, live2, ALU.mult, ALU.add))
                step(dve.scalar_tensor_tensor(srt2, srt, 2.0, srt2, ALU.mult, ALU.min))
                step(dve.scalar_tensor_tensor(srt, srt, live, srt, ALU.is_ge, ALU.mult))
                step(dve.tensor_tensor(turn_of[:, AHEAD:], srt, srt2, ALU.max))
                n17 = EXPERTS + 1
                pre = prod4(PROD, (1, n17, 16))[:, 0]
                step(dve.tensor_tensor(pre, turn_of.unsqueeze(1).broadcast_to([P, n17, 16]),
                                       cst("turn").unsqueeze(2).broadcast_to([P, n17, 16]), ALU.is_lt))
                step(dve.tensor_tensor(pre, pre, nit.unsqueeze(1).broadcast_to([P, n17, 16]), ALU.mult))
                step(dve.tensor_reduce(table[:, 0:n17], pre, AX, ALU.add))
                step(dve.tensor_scalar(table[:, 17:18], table[:, 16:17], -1.0, MAX_ITEMS + 1.0, ALU.mult, ALU.add))
                own = prod4(PROD, (1, 16, 16))[:, 0]
                step(dve.tensor_tensor(own, turn_of.unsqueeze(1).broadcast_to([P, 16, 16]),
                                       cst("turn")[:, 0:16].unsqueeze(2).broadcast_to([P, 16, 16]), ALU.is_equal))
                step(dve.tensor_tensor(own, own, cst("expert").unsqueeze(1).broadcast_to([P, 16, 16]), ALU.mult))
                step(dve.tensor_reduce(table[:, ORDER:], own, AX, ALU.add))
                dve.tensor_copy(tab[0:1, l, :], table[0:1, :]).then_inc(sem("tab_ready"), 1)
                step(dve.tensor_tensor(own, turn_of.unsqueeze(1).broadcast_to([P, 16, 16]),
                                       turn_of.unsqueeze(2).broadcast_to([P, 16, 16]), ALU.is_lt))
                step(dve.tensor_tensor(own, own, nit.unsqueeze(1).broadcast_to([P, 16, 16]), ALU.mult))
                step(dve.tensor_reduce(ebase, own, AX, ALU.add))
                pr = prod4(PROD2, (2, n, 16))
                for c in range(2):
                    step(dve.tensor_tensor(pr[:, c], AA[:, c, 0:n, :], ps[:, 7, 0:16 * n].rearrange("p (n e) -> p n e", e=16), ALU.mult))
                rk2, bs2, qn2, pos2 = (t.rearrange("p (c n) -> p c n", c=2)[:, :, 0:n] for t in (rk, bs, qn, pos))
                step(dve.tensor_reduce(rk2, pr, AX, ALU.add))
                for c in range(2):
                    step(dve.tensor_tensor(pr[:, c], AA[:, c, 0:n, :], ebase.unsqueeze(1).broadcast_to([P, n, 16]), ALU.mult))
                step(dve.tensor_reduce(bs2, pr, AX, ALU.add))
                step(dve.scalar_tensor_tensor(pos2, bs2, float(SLOTS), rk2, ALU.mult, ALU.add))
                step(dve.tensor_copy(pos_i[:, l, :].rearrange("p (c n) -> p c n", c=2)[:, :, 0:n], pos2))
                dve.engine_nop().then_inc(sem("pos_ready"), 1)
                if l == 0:
                    step(dve.tensor_tensor(pos2, pos2, cst("far").rearrange("p (c n) -> p c n", c=2), ALU.add))
                pick_item(l, 0, True)
                for j in range(1, n):
                    rows_ = min(P, T - j * P)
                    dve.wait_ge(sem(f"tok_turned{l}"), 2 * j + 2)
                    dve.tensor_copy(tok[0:rows_, j, 512:], ps[0:rows_, 2 * j + 1, :]).then_inc(sem(f"tok_ready{l}"), 1)

            def pick_item(l, g, first):
                n = TILES[l]
                if not first:
                    dve.wait_ge(sem(f"xg_ready{l}"), g)
                    dve.wait_ge(sem(f"pos_next{l}"), g)
                eq = peq[:, 0:2 * n, :].rearrange("p (c n) s -> p c n s", c=2)
                pos2 = pos.rearrange("p (c n) -> p c n", c=2)
                for c in range(2):
                    ins = dve.tensor_tensor(eq[:, c], cst("slot").unsqueeze(1).broadcast_to([P, n, SLOTS]),
                                            pos2[:, c, 0:n].unsqueeze(2).broadcast_to([P, n, SLOTS]), ALU.is_equal)
                ins.then_inc(sem(f"peq_ready{l}"), 1)
                dve.wait_ge(sem(f"peq_ready{l}"), g + 1)
                dve.tensor_tensor(pick[:, 0:n, :], eq[:, 0], eq[:, 1], ALU.add).then_inc(sem(f"pick_ready{l}"), 1)
                dve.tensor_scalar(pos2[:, :, 0:n], pos2[:, :, 0:n], -float(SLOTS), None, ALU.add).then_inc(sem(f"pos_next{l}"), 1)

            def move_gathered(l, g, first):
                dve.wait_ge(sem(f"xg_turned{l}"), g + 1)
                if not first:
                    dve.wait_ge(sem(f"h_ready{l}"), g + 1)
                dve.tensor_copy(xTg.rearrange("p (q m) s -> p m q s", m=2),
                                ps[:, 3, 0:256].rearrange("p (m q s) -> p m q s", m=2, q=QUARTERS)).then_inc(sem(f"xT_ready{l}"), 1)

            def mixture(l):
                dve.wait_ge(sem("tab_ready"), l + 1)
                n = dve.value_load(tab[0:1, l, EXPERTS:EXPERTS + 1], min_val=MIN_ITEMS, max_val=MAX_ITEMS)
                move_gathered(l, 0, True)
                with dve.Fori(0, n) as g:
                    pick_item(l, g + 1, False)
                    dve.wait_ge(sem(f"silu_ready{l}"), g + 1)
                    dve.tensor_tensor(hs[64:128, :], hs[64:128, :], ps[64:128, 0, 0:256], ALU.mult).then_inc(sem(f"hs_ready{l}"), 1)
                    dve.wait_ge(sem(f"h_turned{l}"), g + 1)
                    dve.tensor_copy(hT.rearrange("p (a m) s -> p m a s", a=2),
                                    ps[:, 4, 0:128].rearrange("p (m a s) -> p m a s", m=2, a=2)).then_inc(sem(f"hT_ready{l}"), 1)
                    move_gathered(l, g + 1, False)

            def combine(l):
                for j in range(TILES[l]):
                    rows_ = min(P, TOKENS[l] - j * P)
                    r = rows_of[l][j]
                    dve.wait_ge(sem(f"rows{j}1"), 16 * l + 16)
                    dve.wait_ge(sem(f"first_scaled{l}"), j + 1)
                    first, second = r[0:rows_, 0, :], r[0:rows_, 1, :]
                    step(dve.scalar_tensor_tensor(first, second, wts[0:rows_, 1, j:j + 1], first, ALU.mult, ALU.add))
                    step(dve.scalar_tensor_tensor(first, tok[0:rows_, j, :], ALPHA, first, ALU.mult, ALU.add))
                    for h in range(2):
                        step(dve.bn_stats(bn[0:rows_, 6 * h:6 * h + 6], r[0:rows_, 0, h * 512:(h + 1) * 512]))
                    dve.bn_aggr(mv[0:rows_, j, :], bn[0:rows_, :]).then_inc(sem(f"stats_ready{l}"), 1)
                    dve.wait_ge(sem(f"tstd_ready{l}"), j + 1)
                    step(dve.reciprocal(trs[0:rows_, j:j + 1], tstd[0:rows_, j:j + 1]))
                    ins = dve.tensor_scalar(first, first, mv[0:rows_, j, 0:1], trs[0:rows_, j:j + 1], ALU.subtract, ALU.mult)
                    if l == 0:
                        ins.then_inc(sem("z_ready0"), 1)
                        continue
                    step(ins)
                    if j == 0:
                        dve.wait_ge(sem("in_lnrow"), 32)
                    step(dve.tensor_tensor(first, first, lnrow[:, 0, :], ALU.mult))
                    dve.tensor_tensor(first, first, lnrow[:, 1, :], ALU.add).then_inc(sem("out_tile"), 1)

            norm(0, cv, T0, "conv_ready", DVE_CHUNKS)
            residual(0)
            post_and_route(0)
            mixture(0)
            combine(0)
            for j in range(3):
                rows_ = min(P, T0 - j * P)
                dve.wait_ge(sem("z_turned"), 2 * j + 2)
                for c in range(4):
                    dve.tensor_scalar(xT[:, 4 + c, j * P:j * P + rows_], ps[:, 2 * j + 1, c * rows_:(c + 1) * rows_],
                                      V("post_g", 12 + c), V("post_b", 12 + c), ALU.mult, ALU.add).then_inc(sem("xT_back"), 1)

            dve.wait_ge(sem("in_lam"), 64)
            for k in range(2):
                dve.tensor_tensor_reduce(lamv[:, 2 * k, :], lamv[:, 2 * k, :], lamv[:, 2 * k + 1, :], 1.0, 0.0,
                                         ALU.mult, ALU.add, lam2[:, k:k + 1]).then_inc(sem("lam_sums"), 1)
            step(dve.tensor_scalar(subg, V("subln", 0), 1.0 - LAM_INIT, None, ALU.mult))

            dve.wait_ge(sem("in_const_late"), 16)
            for n in range(2 * NC_):
                c, T, lo = n % NC_, (T0, SEQ)[n // NC_], (0, META)[n // NC_]
                dst = kT[:, c, :] if n < NC_ else qT[:, c, :]
                if n:
                    dve.wait_ge(sem("rope_ready"), n)
                dve.wait_ge(sem("kq_moved"), n + 1)
                r = raw[:, n % 2, 0:T]
                step(dve.stream_shuffle(swp[:, 0:T], r, SWAP))
                step(dve.tensor_tensor(swp[:, 0:T], swp[:, 0:T], cst("sin")[:, lo:lo + T], ALU.mult))
                step(dve.tensor_tensor(dst, r, cst("cos")[:, lo:lo + T], ALU.mult))
                dve.tensor_tensor(dst, dst, swp[:, 0:T], ALU.add).then_inc(sem("rope_ready"), 1)

            dve.wait_ge(sem("lam_exp"), 1)
            step(dve.tensor_tensor(nlam, lame[:, 1:2], lame[:, 0:1], ALU.subtract))
            step(dve.tensor_scalar(nlam, nlam, -LAM_INIT, None, ALU.add))

            def mask_and_max(u):
                i = u % 2
                b = u % 2
                w = KEYS[i]
                dve.wait_ge(sem("scores_ready"), u + 1)
                if u >= 2:
                    dve.wait_ge(sem("pd_turned"), u - 1)
                s = prob[:, b, :].rearrange("p (c k) -> p c k", c=2)[:, :, 0:w]
                dve.scalar_tensor_tensor(s, ps[:, 2 * b:2 * b + 2, 0:w], HEAD_DIM ** -0.5,
                                         cst(f"mask{i}").unsqueeze(1).broadcast_to([P, 2, w]),
                                         ALU.mult, ALU.add).then_inc(sem("scores_moved"), 1)
                dve.wait_ge(sem("scores_moved"), u + 1)
                dve.tensor_reduce(mx[:, b, :], s, AX, ALU.max, negate=True).then_inc(sem("max_ready"), 1)

            def difference(u):
                i, b = u % 2, u % 2
                w = KEYS[i]
                dve.wait_ge(sem("exp_ready"), 2 * u + 2)
                step(dve.reciprocal(rden[:, b, :], den[:, b, :]))
                step(dve.tensor_tensor(r2[:, b:b + 1], rden[:, b, 1:2], nlam, ALU.mult))
                step(dve.tensor_scalar(prob[:, b, 0:w], prob[:, b, 0:w], rden[:, b, 0:1], None, ALU.mult))
                dve.scalar_tensor_tensor(prob[:, b, 0:w], prob[:, b, T0:T0 + w], r2[:, b:b + 1], prob[:, b, 0:w],
                                         ALU.mult, ALU.add).then_inc(sem("pd_ready"), 1)

            def move_probs(u):
                i, b = u % 2, u % 2
                dve.wait_ge(sem("pd_turned"), u + 1)
                if u >= 2:
                    dve.wait_ge(sem("pv_ready"), u - 1)
                full = KEYS[i] // P
                if u < 2:
                    dve.wait_ge(sem("pdT_zero"), 2)
                dve.tensor_copy(pdT[:, b, 0:full * P], ps[:, 4 + b, 0:full * P])
                dve.tensor_copy(pdT[0:META, b, full * P:(full + 1) * P],
                                ps[0:META, 4 + b, full * P:(full + 1) * P]).then_inc(sem("pdT_ready"), 1)

            for u in range(2 * HEADS + 2):
                if u < 2 * HEADS:
                    mask_and_max(u)
                if 1 <= u <= 2 * HEADS:
                    difference(u - 1)
                if u >= 2:
                    move_probs(u - 2)
            dve.engine_nop().then_inc(sem("oms_free"), 1)
            dve.wait_ge(sem("ostd_ready"), 1)
            ostd = view(0, 4, 512)
            orstd = view(4224, 4, 512)
            step(dve.reciprocal(orstd, ostd))
            flat = oT.rearrange("p h t -> p (h t)")
            dve.scalar_tensor_tensor(flat, flat, subg, orstd.rearrange("p a b -> p (a b)"),
                                     ALU.mult, ALU.mult).then_inc(sem("o_normed"), 1)
            residual(1)
            dve.engine_nop().then_inc(sem("attn_over"), 1)
            post_and_route(1)
            mixture(1)
            combine(1)


def kernel(**inputs):
    import concourse.bacc as bacc
    from concourse.bass_utils import run_bass_kernel_spmd

    nc = bacc.Bacc("TRN2", target_bir_lowering=False, num_devices=1)
    arrays, aps = {}, {}
    for name, value in {**inputs, "consts": CONSTS}.items():
        v = np.ascontiguousarray(value)
        arrays[f"in_{name}"] = v
        aps[name] = nc.dram_tensor(f"in_{name}", v.shape, mybir.dt.from_np(v.dtype), kind="ExternalInput").ap()
    out = nc.dram_tensor("out", (1, SEQ, D), F32, kind="ExternalOutput").ap()
    trunk(nc, aps, out)
    return run_bass_kernel_spmd(nc, [arrays], core_ids=[0]).results[0]["out"]
```

```python
import math
from contextlib import ExitStack

import numpy as np

import concourse.bass as bass
from concourse import mybir

F32 = mybir.dt.float32
I32 = mybir.dt.int32
ALU = mybir.AluOpType
ACT = mybir.ActivationFunctionType
AX = mybir.AxisListType.X

P = 128
D = 1024
NC_ = D // P
SEQ = 256
META = 16
T0 = SEQ + META
CHUNK = 64
TAPS = 31
PAD = TAPS - 1
HEADS = 8
HEAD_DIM = 64
ROT = HEAD_DIM // 4
GROUPS = 4
PER_GROUP = 4
EXPERTS = GROUPS * PER_GROUP
DEPTH = 2
ALPHA = (2.0 * DEPTH) ** 0.25
EPS = 1e-5
LAM_INIT = 0.8 - 0.6 * math.exp(-0.3 * 1)
THETA = 500000.0

SLOTS = 32
MAX_ITEMS = (2 * T0 + EXPERTS * (SLOTS - 1)) // SLOTS
MIN_ITEMS = 2 * SEQ // SLOTS
TILES = [(T0 + P - 1) // P, SEQ // P]
TOKENS = [T0, SEQ]
QUARTERS = 4
BRICK = 4096
RING = 9
AHEAD = RING // 3
ORDER = EXPERTS + 1
BIG = 3.0e38
DVE_CHUNKS = 6
PIECES = NC_ // 2
DIAGS = (NC_ - DVE_CHUNKS) * TAPS
FULL = len(range(0, T0, SLOTS))

CONST_AT = {}


def make_constants():
    parts, at = [], 0

    def put(name, a):
        nonlocal at
        a = np.broadcast_to(np.asarray(a, np.float32), (P, np.asarray(a).shape[-1]))
        CONST_AT[name] = (at, at + a.shape[1])
        parts.append(a)
        at += a.shape[1]

    put("ident", np.eye(P))
    put("before", np.triu(np.ones((P, P)), 1))
    put("ones", np.ones((1, P)))
    put("mean_d", np.full((1, P), 1.0 / D))
    put("slot", np.arange(SLOTS)[None])
    put("neg4", np.arange(4)[None] - 16.0)
    put("full", [list(range(0, T0, SLOTS))])
    put("minus_e", -np.arange(EXPERTS)[None])
    put("expert", np.arange(EXPERTS)[None])
    put("turn", np.arange(EXPERTS + 1)[None] - AHEAD)
    t = np.arange(3)[None] * P + np.arange(P)[:, None]
    put("valid", (t < T0).astype(np.float32))
    put("far", np.tile((t >= T0) * 1.0e6, (1, 2)))
    put("eps", [[EPS]])
    half = ROT // 2
    inv = np.float32(THETA) ** (-np.arange(0, ROT, 2, dtype=np.float32) / np.float32(ROT))
    ang = np.arange(T0, dtype=np.float32)[None] * inv.astype(np.float32)[:, None]
    cos, sin = np.ones((P, T0), np.float32), np.zeros((P, T0), np.float32)
    for base in (0, HEAD_DIM):
        for k in range(half):
            cos[base + k] = cos[base + half + k] = np.cos(ang[k])
            sin[base + k] = -np.sin(ang[k])
            sin[base + half + k] = np.sin(ang[k])
    CONST_AT["late"] = (at, None)
    put("cos", cos)
    put("sin", sin)
    for i in range(2):
        q = META + i * P + np.arange(P)
        keys = np.arange(KEYS[i])
        cid = lambda p: np.where(p < META, 0, 1 + (p - META) // CHUNK)
        put(f"mask{i}", np.where(cid(keys)[None] <= cid(q)[:, None], 0.0, -BIG))
    return np.ascontiguousarray(np.concatenate(parts, axis=1), dtype=np.float32)


KEYS = [META + P, T0]
CONSTS = make_constants()

VEC_AT = {"b_pw1": 0, "b_dw": 16, "ln_g": 24, "ln_b": 32, "b_pw2": 40, "post_g": 48, "post_b": 80, "subln": 112}
VEC_ROWS = 113

SWAP = [k + 8 if k < 8 else k - 8 if k < 16 else k for k in range(32)]


def trunk(nc, a, out):
    with ExitStack() as ctx:
        def sb(name, shape, dt=F32):
            return ctx.enter_context(nc.sbuf_tensor(name, shape, dt))

        sems = {}

        def sem(name):
            if name not in sems:
                sems[name] = ctx.enter_context(nc.semaphore(name))
            return sems[name]

        ring = sb("ring", [P, RING, BRICK])
        const = sb("const", [P, CONSTS.shape[1]])
        vec = sb("vec", [P, VEC_ROWS])
        wdw = sb("wdw", [P, TAPS * NC_])
        wr = sb("wr", [P, 2, NC_, 20])
        br = sb("br", [20, 2])
        lamv = sb("lamv", [P, 4, HEAD_DIM])
        tok = sb("tok", [P, 3, D])
        xT = sb("xT", [P, NC_, T0])
        work = sb("work", [P, 7104])
        small = sb("small", [P, 660])
        tab = sb("tab", [1, 2, ORDER + EXPERTS], I32)
        qswp = sb("qswp", [P, SEQ])
        pos_i = sb("pos_i", [P, 2, 6], I32)
        ps = ctx.enter_context(nc.psum_tensor("ps", [P, 8, 512], F32))
        ybuf = [nc.dram_tensor(f"ybuf{l}", (MAX_ITEMS * SLOTS, D), F32, kind="Internal").ap() for l in range(2)]

        def cst(name):
            lo, hi = CONST_AT[name]
            return const[:, lo:hi]

        ident = cst("ident")

        def view(lo, *dims, rows=P):
            n = int(np.prod(dims))
            v = work[0:rows, lo:lo + n]
            if len(dims) == 2:
                v = v.rearrange("p (a b) -> p a b", b=dims[1])
            return v

        def scores_of(i):
            if i == 0:
                return ps[:, 0, :].rearrange("p (c k) -> p c k", c=2)[:, :, 0:KEYS[0]]
            return ps[:, 2:4, 0:KEYS[1]]

        def m_bank(c):
            return (0, 1, 2, 3, 6, 7, 0, 1)[c]

        def diag(i):
            return tok[:, i % 16 // NC_, (i % NC_) * P:(i % NC_ + 1) * P]

        glu = view(0, NC_, PAD + T0)
        cv = view(2416, NC_, T0)
        sq = view(4592, NC_, T0)
        sig = view(4592, 2, T0)
        vrow = view(5200, 3, P)
        xg, hs = view(0, 256), view(256, 256)
        ysb = view(1440, 2, 256)
        xTg = view(768, NC_, SLOTS)
        hT = view(1024, 4, SLOTS)
        pick = view(1152, 3, SLOTS)
        peq = view(1248, 6, SLOTS)
        wdiag = view(2048, 4, P)
        rows_of = [[view(2560, 2, D), view(4608, 2, D), view(0, 2, D)],
                   [view(2560, 2, D), xT[:, :, :].rearrange("p c t -> p (c t)")[:, 0:2 * D].rearrange("p (a b) -> p a b", b=D)]]
        lnrow = view(4608, 2, D)
        kT = view(0, HEADS, T0)
        qT = view(2176, HEADS, SEQ)
        otok = qT
        oT = view(0, HEADS, SEQ)
        raw = view(4224, 2, T0)
        swp = view(4768, T0)
        qz = view(4224, 4, SEQ)
        prob = view(5248, 2, 2 * T0)
        pdT = view(6336, 2, 3 * P)
        vtok = tok
        rstd = view(0, T0)
        std = view(T0, T0)
        o_ = 0

        def sm(n, *dims):
            nonlocal o_
            v = small[:, o_:o_ + n]
            o_ += n
            if len(dims) == 2:
                v = v.rearrange("p (a b) -> p a b", b=dims[1])
            if len(dims) == 3:
                v = v.rearrange("p (a b c) -> p a b c", b=dims[1], c=dims[2])
            return v

        lg = sm(60, 3, 20)
        gmax, gsum, gw, sel = sm(3), sm(3), sm(3), sm(3)
        geq, gex, cand, gone = sm(12, 3, 4), sm(12, 3, 4), sm(12, 3, 4), sm(12, 3, 4)
        el, oh1, oh2, el2 = sm(12, 3, 4), sm(12, 3, 4), sm(12, 3, 4), sm(12, 3, 4)
        m1, m2, e2, wsum = sm(3), sm(3), sm(3), sm(3)
        wts = sm(6, 2, 3)
        AA = sm(96, 2, 3, 16)
        Asum = sm(48, 3, 16)
        rk, bs, pos = sm(6), sm(6), sm(6)
        nit, table, ebase = sm(16), sm(ORDER + EXPERTS), sm(16)
        key, srt, srt2, turn_of = sm(16), sm(13), sm(13), sm(16)
        osum, orms = sm(16), sm(16)
        live13, live, live2 = sm(13), sm(1), sm(1)
        bn, mv, tstd, trs, centre = sm(12), sm(6, 3, 2), sm(3), sm(3), sm(3)
        lam2, lame, nlam, subg = sm(2), sm(2), sm(1), sm(1)
        mx, den, rden, r2 = sm(4, 2, 2), sm(4, 2, 2), sm(4, 2, 2), sm(2)
        alpha_b = sm(8)
        assert o_ <= 660
        lgT = view(544, 3 * P)
        PROD, PROD2, PROD3, PROD4 = 1000, 1300, 1600, 1900

        def prod4(lo, dims):
            v = work[:, lo:lo + int(np.prod(dims))]
            return v.rearrange("p (a b c) -> p a b c", b=dims[1], c=dims[2])

        def V(name, k):
            return vec[:, VEC_AT[name] + k:VEC_AT[name] + k + 1]

        def tap(k, c):
            return wdw[:, k * NC_ + c:k * NC_ + c + 1]

        def sq_of(l):
            return sq if l == 0 else view(2176, NC_, SEQ)

        stream = [xT, xT[:, :, META:T0]]

        def brick(b):
            return ring[:, b % RING, :]

        PW1, PW2, E0 = 0, 4, 6
        KB = E0 + 3 * EXPERTS
        VB, QB, OB, E1 = KB + 2, KB + 4, KB + 6, KB + 8
        START = [E0, E1]

        def first_items(engine, l, turn, n, smallest=0):
            _, values = nc.values_load_multi_w_load_instructions(
                tab[0:1, l, bass.ds(turn, n)], engines=[engine.engine], min_val=smallest, max_val=MAX_ITEMS)
            return values

        def arrived(b, half, it=0):
            return sem(f"brick{b % RING}_{half}"), (b // RING + 1 + it) * 16

        block = ctx.enter_context(nc.Block())

        @block.sync
        def _(sp):
            def load_half(b, half, k, src):
                dst = brick(b).rearrange("p (k n) -> p k n", k=k)
                r = slice(half * k // 2, (half + 1) * k // 2)
                sp.dma_start(dst[:, r, :], src[:, r, :]).then_inc(sem(f"brick{b % RING}_{half}"), 16)

            sp.dma_start(tok[0:META, 0, :], a["meta_tokens"]).then_inc(sem("in_x"), 16)
            sp.dma_start(tok[META:P, 0, :], a["x"][0, 0:P - META, :]).then_inc(sem("in_x"), 16)
            sp.dma_start(tok[:, 1, :], a["x"][0, P - META:2 * P - META, :]).then_inc(sem("in_x"), 16)
            sp.wait_ge(sem("tok_zero"), 1)
            sp.dma_start(tok[0:META, 2, :], a["x"][0, 2 * P - META:SEQ, :]).then_inc(sem("in_x"), 16)

            pw1 = a["conv_w_pw1"][0].rearrange("(k p) (s n) -> p k s n", p=P, s=2)
            for b in range(4):
                if b == 1:
                    sp.wait_ge(sem("in_vec"), 16 * 8)
                    sp.wait_ge(sem("in_taps"), 32)
                for s in range(2):
                    sp.dma_start(brick(b).rearrange("p (k s n) -> p k s n", k=NC_, s=2)[:, :, s, :],
                                 pw1[:, :, s, b * 256:(b + 1) * 256]).then_inc(sem(f"brick{b}_{s}"), 16)

            def dense(b, w, half):
                for part in range(2):
                    if b > PW2:
                        sp.wait_ge(*arrived(b - 1, part))
                    load_half(b, part, NC_, w.rearrange("(k p) n -> p k n", p=P)[:, :, half * 512:(half + 1) * 512])

            for half in range(2):
                dense(PW2 + half, a["conv_w_pw2"][0], half)

            ORDER_OF_HALVES = ((-1, 0), (-1, 1), (0, 0), (1, 0), (0, 1), (1, 1), (2, 0), (2, 1))

            def expert(l, b, e, waits, it=0):
                for i, (m, half) in enumerate(ORDER_OF_HALVES[2:]):
                    if half == 0:
                        waits[m]()
                    m_before, half_before = ORDER_OF_HALVES[i]
                    sp.wait_ge(*arrived(b + m_before, half_before, it))
                    w = a[("moe_w1", "moe_w3", "moe_w2")[m]]
                    src = w[l, e] if isinstance(e, int) else w[l, bass.ds(e, 1)].rearrange("o r n -> (o r) n")
                    load_half(b + m, half, NC_ if m < 2 else 4, src.rearrange("(k p) n -> p k n", p=P))

            def skip(b, it):
                for i, (m, half) in enumerate(ORDER_OF_HALVES[2:]):
                    m_before, half_before = ORDER_OF_HALVES[i]
                    sp.wait_ge(*arrived(b + m_before, half_before, it))
                    sp.sem_inc(sem(f"brick{(b + m) % RING}_{half}"), 16)

            def hold(name, n):
                return lambda: sp.wait_ge(sem(name), n)

            nothing = lambda: None

            def experts(l, first_waits):
                b = START[l]
                for e in range(3):
                    expert(l, b + 3 * e, e, first_waits[3 * e:3 * e + 3])
                sp.wait_ge(sem("tab_ready"), l + 1)
                sp.wait_ge(sem("order_ready"), l + 1)

                def later(bb, turn, it=0):
                    n, _, lo, hi = first_items(sp, l, turn - (AHEAD - 1), 4)
                    w13 = lambda: sp.wait_ge(sem(f"h_ready{l}"), n + 1)
                    w2 = lambda: sp.wait_ge(sem(f"y_ready{l}"), n + 1)
                    with sp.If(hi - lo):
                        e = sp.value_load(tab[0:1, l, bass.ds(turn + ORDER, 1)], min_val=AHEAD, max_val=EXPERTS - 1)
                        expert(l, bb, e, [w13, nothing, w2], it)
                    with sp.Else():
                        skip(bb, it)

                with sp.Fori(0, 4) as it:
                    for k in range(3):
                        later(b + RING + 3 * k, it * 3 + (k + AHEAD), it)
                later(b + RING * 5, EXPERTS - 1)

            experts(0, [nothing] * 3 + [hold("pw1_ready", 2 * k + 2) for k in range(4)]
                    + [hold("m_ready0", 4), hold("m_ready0", 8)])

            for c in range(2):
                sp.wait_ge(sem(f"rows{TILES[0] - 1}{c}"), 16)
            for n, (b, w) in enumerate(((KB, a["kv_w_k"]), (VB, a["kv_w_v"]), (QB, a["attn_w_q"][0]), (OB, a["attn_w_o"][0]))):
                for half in range(2):
                    dense(b + half, w, half)
            last = sp.value_load(tab[0:1, 0, EXPERTS:EXPERTS + 1], min_val=MIN_ITEMS, max_val=MAX_ITEMS)
            experts(1, [lambda: sp.wait_ge(sem("y_ready0"), last + 1), hold("kq_ready", 4), hold("kq_ready", 8),
                        hold("v_ready", 5), nothing, hold("kq_ready", 12),
                        hold("kq_ready", 16), hold("m_ready1", 4), hold("m_ready1", 8)])

            for j in range(2):
                for h in range(2):
                    cols = slice(h * 512, (h + 1) * 512)
                    sp.wait_ge(sem("out_half"), 2 * j + h + 1)
                    sp.dma_start(out[0, j * P:(j + 1) * P, cols], rows_of[1][j][:, 0, cols]).then_inc(sem("stored"), 16)
            sp.wait_ge(sem("stored"), 64)

        def heads(pool):
            pool.wait_ge(sem("rope_ready"), NC_)
            pool.memset(qz[64:128, 0:4:2, :], 0.0).then_inc(sem("qz_ready"), 1)
            pool.memset(qz[0:64, 1:4:2, :], 0.0).then_inc(sem("qz_ready"), 1)
            pool.wait_ge(sem("qz_ready"), 2)
            pool.memset(pdT[:, 0, P:2 * P], 0.0).then_inc(sem("pdT_zero"), 1)
            pool.memset(pdT[:, 1, 2 * P:3 * P], 0.0).then_inc(sem("pdT_zero"), 1)
            pool.wait_ge(sem("pdT_zero"), 2)
            for h in range(HEADS):
                pool.wait_ge(sem("rope_ready"), NC_ + h + 1)
                if h >= 2:
                    pool.wait_ge(sem("scores_ready"), 2 * h - 2)
                for c in range(2):
                    r = slice(64 * c, 64 * c + 64)
                    pool.tensor_copy(qz[r, 2 * (h % 2) + c, :], qT[r, h, :]).then_inc(sem("qz_ready"), 1)
                    pool.wait_ge(sem("qz_ready"), 2 * h + c + 3)

        @block.gpsimd
        def _(pool):
            pool.memset(glu[:, :, 0:PAD], 0.0).then_inc(sem("pad_zero"), 1)
            pool.memset(tok[:, 2, :], 0.0).then_inc(sem("tok_zero"), 1)

            def fill(l):
                rest = ybuf[l][MIN_ITEMS * SLOTS:, :].rearrange("(a p) d -> p a d", p=P)
                blocks = (MAX_ITEMS - MIN_ITEMS) * SLOTS // P
                pool.dma_start(rest, const[:, 0:D].unsqueeze(1).broadcast_to([P, blocks, D])).then_inc(sem(f"y_filled{l}"), 16)

            pool.wait_ge(sem("in_const"), 16)
            pool.wait_ge(sem("in_const_late"), 16)
            pool.wait_ge(sem("mean_ready"), 1)
            fill(0)
            for l in range(2):
                pool.wait_ge(sem("tab_ready"), l + 1)
                n = pool.value_load(tab[0:1, l, EXPERTS:EXPERTS + 1], min_val=MIN_ITEMS, max_val=MAX_ITEMS)
                pool.wait_ge(sem(f"y_stored{l}_0"), ((n + 1) >> 1) * 16 + 16)
                pool.wait_ge(sem(f"y_stored{l}_1"), (n >> 1) * 16 + 16)
                pool.wait_ge(sem(f"xT_ready{l}"), n + 1)
                pool.sem_inc(sem("items_over"), 1)
                pool.wait_ge(sem("pos_ready"), l + 1)
                for j in range(TILES[l]):
                    rows = min(P, TOKENS[l] - j * P)
                    for c in range(2):
                        pool.indirect_dma_start(
                            out=rows_of[l][j][0:rows, c, :], out_offset=None, in_=ybuf[l],
                            in_offset=bass.IndirectOffsetOnAxis(ap=pos_i[0:rows, l, c * 3 + j:c * 3 + j + 1], axis=0),
                        ).then_inc(sem(f"rows{j}{c}"), 16)
                if l == 0:
                    heads(pool)
                    fill(1)

        @block.tensor
        def _(pe):
            pe.wait_ge(sem("in_const"), 16)
            pe.wait_ge(sem("in_x"), 64)
            for j in range(3):
                rows = min(P, T0 - j * P)
                for q in range(2):
                    for c in range(4):
                        last = pe.transpose(ps[:, 2 * j + q, c * rows:(c + 1) * rows],
                                            tok[0:rows, j, (4 * q + c) * P:(4 * q + c + 1) * P], ident[0:rows, 0:rows])
                    last.then_inc(sem("x_turned"), 1)
            pe.wait_ge(sem("x_moved"), 6)
            for c in range(NC_):
                if c % 2 == 0:
                    for s in range(2):
                        pe.wait_ge(*arrived(c // 2, s))
                if c >= 2:
                    pe.wait_ge(sem("glu_ready"), c - 1)
                w = brick(c // 2).rearrange("p (k s n) -> p k s n", k=NC_, s=2)
                for s in range(2):
                    for k in range(NC_):
                        last = pe.matmul(ps[:, 2 * (c % 2) + s, 0:T0], w[:, k, s, (c % 2) * P:(c % 2 + 1) * P],
                                         xT[:, k, :], start=(k == 0), stop=(k == NC_ - 1))
                last.then_inc(sem("pw1_ready"), 1)
                if c == 0:
                    pe.wait_ge(sem("in_vec"), 16 * 8)
                    pe.wait_ge(sem("in_taps"), 32)
                    pe.transpose(ps[:, 6, 0:VEC_ROWS], vrow[0:VEC_ROWS, 0, :], ident[0:VEC_ROWS, 0:VEC_ROWS])
                    pe.transpose(ps[:, 7, 0:P], vrow[:, 1, :], ident)
                    pe.transpose(ps[:, 7, P:P + 120], vrow[0:120, 2, :], ident[0:120, 0:120]).then_inc(sem("vec_turned"), 1)

            def add_means(turn, src, T, chunks):
                for k in chunks:
                    first, final = (k == 0), (k == (DVE_CHUNKS - 1 if turn == 0 else NC_ - 1))
                    if turn == 0 and k >= DVE_CHUNKS:
                        pe.wait_ge(sem("conv_moved"), k - DVE_CHUNKS + 1)
                    else:
                        pe.wait_ge(sem("conv_ready" if turn == 0 else f"r_ready{turn - 1}"), k + 1)
                    last = pe.matmul(ps[:, 4, 0:T], cst("mean_d"), src[:, k, 0:T], start=first, stop=final)
                if final:
                    last.then_inc(sem("mean_ready"), 1)

            def keep_warm(bank, n):
                for _ in range(n):
                    pe.matmul(ps[:, bank, :], ident, const[:, 0:512], start=True, stop=True)

            def add_squares(turn, squares, T):
                for k in range(NC_):
                    if k % 2 == 0:
                        pe.wait_ge(sem("sq_ready"), PIECES * turn + k // 2 + 1)
                    last = pe.matmul(ps[:, 5, 0:T], cst("mean_d"), squares[:, k, 0:T], start=(k == 0), stop=(k == NC_ - 1))
                last.then_inc(sem("var_ready"), 1)
                keep_warm(4, 4)

            def combine(l):
                for j in range(2):
                    half = slice(512, D)
                    pe.wait_ge(sem("weights_turned"), 4 * l + 2 * j + 2)
                    pe.wait_ge(sem(f"tok_scaled{l}"), j + 1)
                    pe.matmul(ps[:, 6 + j, :], ident, tok[:, j, half], start=True, stop=False)
                    for c in range(2):
                        pe.wait_ge(sem(f"rows{j}{c}"), 16 * l + 16)
                        last = pe.matmul(ps[:, 6 + j, :], wdiag[:, 2 * j + c, :], rows_of[l][j][:, c, half], start=False, stop=(c == 1))
                    last.then_inc(sem("half_ready"), 1)

            def project_and_norm(l, b0, src, ready):
                T = TOKENS[l]
                w = brick(b0).rearrange("p (k n) -> p k n", k=NC_)
                for k in range(NC_):
                    ready(k)
                    if k % 4 == 0:
                        pe.wait_ge(*arrived(b0, k // 4))
                    for c in range(4):
                        last = pe.matmul(ps[:, c, 0:T], w[:, k, c * P:(c + 1) * P], src[:, k, 0:T],
                                         start=(k == 0), stop=(k == NC_ - 1))
                        if k == NC_ - 1:
                            last.then_inc(sem(f"m_ready{l}"), 1)
                w = brick(b0 + 1).rearrange("p (k n) -> p k n", k=NC_)
                for half in range(2):
                    pe.wait_ge(*arrived(b0 + 1, half))
                for c in range(4, NC_):
                    if m_bank(c) < 4:
                        pe.wait_ge(sem(f"r_ready{l}"), m_bank(c) + 1)
                    for k in range(NC_):
                        last = pe.matmul(ps[:, m_bank(c), 0:T], w[:, k, (c - 4) * P:(c - 3) * P], src[:, k, 0:T],
                                         start=(k == 0), stop=(k == NC_ - 1))
                    last.then_inc(sem(f"m_ready{l}"), 1)
                    if c > 4:
                        add_means(1 + l, stream[l], T, {5: (0, 1, 2, 3), 6: (4,), 7: (5, 6, 7)}[c])

            def project(b0, src, lo, T, ready, free, n0=0, banks=4):
                for c in range(NC_):
                    if c % 4 == 0:
                        for half in range(2):
                            pe.wait_ge(*arrived(b0 + c // 4, half))
                    w = brick(b0 + c // 4).rearrange("p (k n) -> p k n", k=NC_)
                    n = n0 + c
                    if n >= banks:
                        pe.wait_ge(sem(free), n - banks + 1)
                    for k in range(NC_):
                        last = pe.matmul(ps[:, n % banks, 0:T], w[:, k, (c % 4) * P:(c % 4 + 1) * P],
                                         src[:, k, lo:lo + T], start=(k == 0), stop=(k == NC_ - 1))
                    last.then_inc(sem(ready), 1)

            def post_norm_and_route(l):
                T, n = TOKENS[l], TILES[l]
                add_squares(1 + l, sq_of(l), T)
                for k in range(NC_):
                    pe.wait_ge(sem("normed"), (1 + l) * NC_ + k + 1)
                    last = pe.matmul(ps[0:20, 6, 0:T], wr[:, l, k, :], stream[l][:, k, 0:T], start=(k == 0), stop=(k == NC_ - 1))
                last.then_inc(sem("logits_ready"), 1)
                for j in range(n):
                    rows = min(P, T - j * P)
                    for q in range(2):
                        for c in range(4):
                            last = pe.transpose(ps[0:rows, 2 * j + q, c * P:(c + 1) * P],
                                                stream[l][:, 4 * q + c, j * P:j * P + rows], ident)
                        last.then_inc(sem(f"tok_turned{l}"), 1)
                    if j == 0:
                        pe.wait_ge(sem("logits_moved"), l + 1)
                        for i in range(n):
                            last = pe.transpose(ps[:, 7, 64 + 20 * i:84 + 20 * i], lgT[0:20, i * P:(i + 1) * P], ident[0:20, 0:20])
                        last.then_inc(sem("logits_turned"), 1)
                pe.wait_ge(sem("picks_ready"), l + 1)
                pe.matmul(ps[:, 6, 0:16 * n], cst("ones"), Asum[:, 0:n, :], start=True, stop=True).then_inc(sem("totals_ready"), 1)
                pe.matmul(ps[:, 7, 0:16 * n], cst("before"), Asum[:, 0:n, :], start=True, stop=False, skip_group_check=True)
                for i in range(n - 1):
                    last = pe.matmul(ps[:, 7, 16 * (i + 1):16 * n], cst("ones"),
                                     Asum[:, i:i + 1, :].broadcast_to([P, n - 1 - i, 16]), start=False, stop=(i == n - 2),
                                     skip_group_check=True)
                last.then_inc(sem("ranks_ready"), 1)

            def gather(l, g, first, tiles):
                if tiles[0] == 0:
                    pe.wait_ge(sem(f"pick_ready{l}"), g + 1)
                    if not first:
                        pe.wait_ge(sem(f"xg_moved{l}"), g)
                for j in tiles:
                    for q in range(QUARTERS):
                        last = pe.matmul(ps[SLOTS * q:SLOTS * (q + 1), 2, 0:256], pick[:, j, :],
                                         tok[:, j, q * 256:(q + 1) * 256], start=(j == 0), stop=(j == TILES[l] - 1),
                                         skip_group_check=True)
                if j == TILES[l] - 1:
                    last.then_inc(sem(f"xg_ready{l}"), 1)

            def turn_gathered(l, g, first):
                pe.wait_ge(sem(f"xg_moved{l}"), g + 1)
                if not first:
                    pe.wait_ge(sem(f"xT_ready{l}"), g)
                for m in range(2):
                    last = pe.transpose(ps[:, 3, m * P:(m + 1) * P], xg[:, m * P:(m + 1) * P], ident)
                last.then_inc(sem(f"xg_turned{l}"), 1)

            def item(l, g, b, it):
                w1 = brick(b).rearrange("p (k n) -> p k n", k=NC_)
                w3 = brick(b + 1).rearrange("p (k n) -> p k n", k=NC_)
                w2 = brick(b + 2).rearrange("p (k n) -> p k n", k=4)
                pe.wait_ge(sem(f"xT_ready{l}"), g + 1)
                for k in range(NC_):
                    if k % 4 == 0:
                        for m in range(2):
                            pe.wait_ge(*arrived(b + m, k // 4, it))
                    for q in range(QUARTERS):
                        w = (w1, w3)[q // 2]
                        last = pe.matmul(ps[SLOTS * q:SLOTS * (q + 1), 0, 0:256], xTg[:, k, :],
                                         w[:, k, (q % 2) * 256:(q % 2 + 1) * 256], start=(k == 0), stop=(k == NC_ - 1),
                                         skip_group_check=True)
                last.then_inc(sem(f"h_ready{l}"), 1)
                gather(l, g + 1, False, (0, 1))
                pe.wait_ge(sem(f"hs_ready{l}"), g + 1)
                pe.sem_inc(sem("turn_begun"), 1)
                for m in range(2):
                    last = pe.transpose(ps[:, 4, m * 64:(m + 1) * 64], hs[64:128, m * P:(m + 1) * P], ident[64:128, 64:128])
                last.then_inc(sem(f"h_turned{l}"), 1)
                if l == 0:
                    gather(l, g + 1, False, (2,))
                else:
                    turn_gathered(l, g + 1, False)
                pe.wait_ge(sem(f"hT_ready{l}"), g + 1)
                for k in range(4):
                    if k == 2 and l == 0:
                        turn_gathered(l, g + 1, False)
                    if k % 2 == 0:
                        pe.wait_ge(*arrived(b + 2, k // 2, it))
                    for q in range(QUARTERS):
                        last = pe.matmul(ps[SLOTS * q:SLOTS * (q + 1), 1, 0:256], hT[:, k, :], w2[:, k, q * 256:(q + 1) * 256],
                                         start=(k == 0), stop=(k == 3), skip_group_check=True)
                last.then_inc(sem(f"y_ready{l}"), 1)

            def mixture(l):
                pe.sem_inc(sem(f"h_ready{l}"), 1)
                pe.sem_inc(sem(f"y_ready{l}"), 1)
                pe.wait_ge(sem(f"tok_ready{l}"), 2 * TILES[l])
                keep_warm(2, 8)
                pe.wait_ge(sem("tab_ready"), l + 1)
                gather(l, 0, True, range(TILES[l]))
                turn_gathered(l, 0, True)

                def expert(b, lo, hi, it):
                    with pe.If(hi - lo):
                        with pe.Fori(lo, hi) as g:
                            item(l, g, b, it)

                with pe.Fori(0, 5) as it:
                    at = first_items(pe, l, it * 3, 4)
                    for k in range(3):
                        expert(START[l] + 3 * k, at[k], at[k + 1], it)
                expert(START[l] + 45, *first_items(pe, l, EXPERTS - 1, 2), 0)

            for i in range(DIAGS):
                k, c = i % TAPS, DVE_CHUNKS + i // TAPS
                if k == 0:
                    pe.wait_ge(sem("glu_ready"), c + 1)
                pe.wait_ge(sem("diag_ready"), i + 1)
                pe.matmul(ps[:, 6 + i // TAPS, 0:T0], diag(i), glu[:, c, k:k + T0],
                          start=(k == 0), stop=(k == TAPS - 1)).then_inc(sem("diag_used"), 1)
            add_means(0, cv, T0, (0, 1, 2, 3, 6, 7, 4, 5))
            add_squares(0, sq, T0)
            project_and_norm(0, PW2, cv, lambda k: pe.wait_ge(sem("normed"), k + 1))
            post_norm_and_route(0)
            mixture(0)

            combine(0)
            for j in range(3):
                rows = min(P, T0 - j * P)
                pe.wait_ge(sem("z_ready0"), j + 1)
                for q in range(2):
                    for c in range(4):
                        last = pe.transpose(ps[:, 2 * j + q, c * rows:(c + 1) * rows],
                                            rows_of[0][j][0:rows, 0, (4 * q + c) * P:(4 * q + c + 1) * P], ident[0:rows, 0:rows])
                    last.then_inc(sem("z_turned"), 1)

            pe.wait_ge(sem("xT_back"), 24)
            project(KB, xT, 0, T0, "kq_ready", "kq_moved", 0)
            for i, (j, half) in enumerate(((0, 0), (1, 0), (0, 1), (1, 1))):
                w = brick(VB + half).rearrange("p (k n) -> p k n", k=NC_)
                for part in range(2):
                    pe.wait_ge(*arrived(VB + half, part))
                for k in range(NC_):
                    last = pe.matmul(ps[:, 4 + i, :], xT[:, k, j * P:(j + 1) * P], w[:, k, :], start=(k == 0), stop=(k == NC_ - 1))
                last.then_inc(sem("v_ready"), 1)
            pe.wait_ge(sem("v_moved"), 1)
            for k in range(NC_):
                for q in range(QUARTERS):
                    w = brick(VB + q // 2).rearrange("p (k n) -> p k n", k=NC_)
                    last = pe.matmul(ps[32 * q:32 * q + META, 4, 0:256], xT[:, k, 2 * P:T0],
                                     w[:, k, (q % 2) * 256:(q % 2 + 1) * 256], start=(k == 0), stop=(k == NC_ - 1), skip_group_check=True)
            last.then_inc(sem("v_ready"), 1)

            UNITS = 2 * HEADS

            def queries(c, part):
                w = brick(QB + c // 4).rearrange("p (k n) -> p k n", k=NC_)
                pe.wait_ge(*arrived(QB + c // 4, part))
                if part == 0 and c > 0:
                    pe.wait_ge(sem("kq_moved"), NC_ + c)
                for k in range(4 * part, 4 * part + 4):
                    last = pe.matmul(ps[:, 1, 0:SEQ], w[:, k, (c % 4) * P:(c % 4 + 1) * P],
                                     xT[:, k, META:T0], start=(k == 0), stop=(k == NC_ - 1))
                if part == 1:
                    last.then_inc(sem("kq_ready"), 1)

            pe.wait_ge(sem("kq_moved"), NC_)
            for c in range(3):
                for part in range(2):
                    queries(c, part)

            def scores(u):
                h, i = u // 2, u % 2
                pe.wait_ge(sem("rope_ready"), NC_ + h + 1)
                if u >= 2:
                    pe.wait_ge(sem("scores_moved"), u - 1)
                pe.wait_ge(sem("qz_ready"), 2 * h + 4)
                for c in range(2):
                    last = pe.matmul(scores_of(i)[:, c, :], qz[:, 2 * (h % 2) + c, i * P:(i + 1) * P],
                                     kT[:, h, 0:KEYS[i]], start=True, stop=True)
                last.then_inc(sem("scores_ready"), 1)

            def turn_probs(u):
                i = u % 2
                pe.wait_ge(sem("pd_ready"), u + 1)
                if u == 0:
                    pe.wait_ge(sem("v_moved"), 8)
                if u >= 2:
                    pe.wait_ge(sem("pdT_ready"), u - 1)
                for j in range((KEYS[i] + P - 1) // P):
                    w = min(P, KEYS[i] - j * P)
                    last = pe.transpose(ps[0:w, 4 + u % 2, j * P:(j + 1) * P], prob[:, u % 2, j * P:j * P + w], ident)
                last.then_inc(sem("pd_turned"), 1)

            def values(u):
                h, i = u // 2, u % 2
                pe.wait_ge(sem("pdT_ready"), u + 1)
                if u >= 2:
                    pe.wait_ge(sem("o_squared"), u - 1)
                n = (KEYS[i] + P - 1) // P
                for j in range(n):
                    last = pe.matmul(ps[:, 6 + u % 2, 0:P], pdT[:, u % 2, j * P:(j + 1) * P],
                                     vtok[:, j, h * P:(h + 1) * P], start=(j == 0), stop=(j == n - 1))
                last.then_inc(sem("pv_ready"), 1)

            scores(0)
            for u in range(UNITS + 2):
                if u + 1 < UNITS:
                    scores(u + 1)
                if u // 2 + 3 < HEADS:
                    queries(u // 2 + 3, u % 2)
                if 1 <= u <= UNITS:
                    turn_probs(u - 1)
                if u >= 2:
                    values(u - 2)
            keep_warm(4, 4)
            for i in range(2):
                pe.wait_ge(sem(f"o_scaled{i}"), 1)
                for q in range(2):
                    for c in range(4):
                        last = pe.transpose(ps[:, 2 * i + q, c * P:(c + 1) * P], otok[:, 4 * q + c, i * P:(i + 1) * P], ident)
                    last.then_inc(sem("o_turned"), 1)
            pe.wait_ge(sem("oT_ready"), 4)
            project_and_norm(1, OB, oT, lambda k: None)
            post_norm_and_route(1)
            mixture(1)
            combine(1)

        @block.scalar
        def _(act):
            late = CONST_AT["late"][0]
            act.dma_start(const[:, 0:late], a["consts"][:, 0:late]).then_inc(sem("in_const"), 16)
            rows = vrow[:, 0, :]
            for name, src in (("b_pw1", a["conv_b_pw1"]), ("b_dw", a["conv_b_dw"]), ("ln_g", a["conv_ln_g"]),
                              ("ln_b", a["conv_ln_b"]), ("b_pw2", a["conv_b_pw2"]), ("subln", a["attn_subln_g"])):
                n = src.shape[0] * src.shape[1] // P
                act.dma_start(rows[VEC_AT[name]:VEC_AT[name] + n, :],
                              src.rearrange("l (c p) -> (l c) p", p=P)).then_inc(sem("in_vec"), 16)
            for name, src in (("post_g", a["post_ln_g"]), ("post_b", a["post_ln_b"])):
                act.dma_start(rows[VEC_AT[name]:VEC_AT[name] + 32, :],
                              src.rearrange("l s (c p) -> (l s c) p", p=P)).then_inc(sem("in_vec"), 16)
            taps = a["conv_w_dw"][0].rearrange("k (c p) -> (k c) p", p=P)
            act.dma_start(vrow[:, 1, :], taps[0:P, :]).then_inc(sem("in_taps"), 16)
            act.dma_start(vrow[0:120, 2, :], taps[P:P + 120, :]).then_inc(sem("in_taps"), 16)

            def move(dst, src):
                return act.activation(dst, src, ACT.Copy)

            for j in range(3):
                rows_ = min(P, T0 - j * P)
                act.wait_ge(sem("x_turned"), 2 * j + 1)
                move(xT[:, 0:4, j * P:j * P + rows_],
                     ps[:, 2 * j, 0:4 * rows_].rearrange("p (c t) -> p c t", c=4)).then_inc(sem("x_moved"), 1)
            act.wait_ge(sem("vec_ready"), 2)
            act.wait_ge(sem("x_turned"), 6)

            def build_diags(first, last):
                for i in range(first, last):
                    if i >= 16:
                        act.wait_ge(sem("diag_used"), i - 15)
                    act.activation(diag(i), ident, ACT.Copy, scale=tap(i % TAPS, DVE_CHUNKS + i // TAPS)).then_inc(sem("diag_ready"), 1)

            build_diags(0, 8)
            for c in range(NC_):
                act.wait_ge(sem("pw1_ready"), c + 1)
                if c >= 2:
                    act.wait_ge(sem("glu_ready"), c - 1)
                act.activation(sig[:, c % 2, :], ps[:, 2 * (c % 2) + 1, 0:T0], ACT.Sigmoid,
                               bias=V("b_pw1", 8 + c)).then_inc(sem("sig_ready"), 1)
                if c in (2, 3):
                    build_diags(4 * c, 4 * c + 4)
            build_diags(16, DIAGS)
            for i in range(NC_ - DVE_CHUNKS):
                act.wait_ge(sem("diag_used"), (i + 1) * TAPS)
                act.activation(cv[:, DVE_CHUNKS + i, :], ps[:, 6 + i, 0:T0], ACT.Identity,
                               bias=V("b_dw", DVE_CHUNKS + i)).then_inc(sem("conv_moved"), 1)
            for c in range(NC_):
                last = act.activation(xT[:, c, :], xT[:, c, :], ACT.Identity, scale=ALPHA, bias=alpha_b[:, c:c + 1])
            last.then_inc(sem("x_scaled0"), 1)
            act.dma_start(const[:, late:], a["consts"][:, late:]).then_inc(sem("in_const_late"), 16)
            for l in range(2):
                act.dma_start(wr[:, l, :, 0:GROUPS], a["moe_w_group"][l].rearrange("(k p) n -> p k n", p=P)).then_inc(sem("in_router"), 16)
                act.dma_start(wr[:, l, :, GROUPS:20], a["moe_w_expert"][l].rearrange("(k p) n -> p k n", p=P)).then_inc(sem("in_router"), 16)
                act.dma_start(br[0:GROUPS, l:l + 1], a["moe_b_group"][l:l + 1, :].rearrange("o n -> n o")).then_inc(sem("in_router"), 16)
                act.dma_start(br[GROUPS:20, l:l + 1], a["moe_b_expert"][l:l + 1, :].rearrange("o n -> n o")).then_inc(sem("in_router"), 16)
            for k, name in enumerate(("attn_lam_q1", "attn_lam_k1", "attn_lam_q2", "attn_lam_k2")):
                act.dma_start(lamv[:, k, :], a[name].broadcast_to([P, HEAD_DIM])).then_inc(sem("in_lam"), 16)

            def norm(turn, src, squares, dst, T, func, gain, bias):
                for p in range(PIECES):
                    act.wait_ge(sem("centred"), PIECES * turn + p + 1)
                    act.activation(squares[:, 2 * p:2 * p + 2, 0:T], src[:, 2 * p:2 * p + 2, 0:T], ACT.Square).then_inc(sem("sq_ready"), 1)
                act.wait_ge(sem("var_ready"), turn + 1)
                act.activation(std[:, 0:T], ps[:, 5, 0:T], ACT.Sqrt, bias=cst("eps")).then_inc(sem("std_ready"), 1)
                for c in range(NC_):
                    if c % 2 == 0:
                        act.wait_ge(sem("scaled"), PIECES * turn + c // 2 + 1)
                    act.activation(dst[:, c, 0:T], src[:, c, 0:T], func, scale=gain(c),
                                   bias=bias(c)).then_inc(sem("normed"), 1)

            def post(l):
                T, n = TOKENS[l], TILES[l]
                norm(1 + l, stream[l], sq_of(l), stream[l], T, ACT.Identity,
                     lambda c: V("post_g", 16 * l + c), lambda c: V("post_b", 16 * l + c))
                act.wait_ge(sem("logits_ready"), l + 1)
                act.wait_ge(sem("pad_ready"), l + 1)
                act.activation(lgT[0:20, 0:T], ps[0:20, 6, 0:T], ACT.Identity, bias=br[0:20, l:l + 1]).then_inc(sem("logits_moved"), 1)
                for j in range(n):
                    rows_ = min(P, T - j * P)
                    for half in range(2):
                        act.wait_ge(sem(f"tok_turned{l}"), 2 * j + half + 1)
                        move(tok[0:rows_, j, half * 512:(half + 1) * 512], ps[0:rows_, 2 * j + half, :]).then_inc(sem(f"tok_ready{l}"), 1)
                act.wait_ge(sem("gsub_ready"), l + 1)
                act.activation(gex[:, 0:n, :], gex[:, 0:n, :], ACT.Exp).then_inc(sem("gex_ready"), 1)
                act.wait_ge(sem("e2_sub"), l + 1)
                act.activation(e2[:, 0:n], e2[:, 0:n], ACT.Exp).then_inc(sem("e2_ready"), 1)

            def mixture(l):
                act.wait_ge(sem("tab_ready"), l + 1)
                n = act.value_load(tab[0:1, l, EXPERTS:EXPERTS + 1], min_val=MIN_ITEMS, max_val=MAX_ITEMS)
                act.wait_ge(sem(f"y_filled{l}"), 16)
                act.wait_ge(sem(f"xg_ready{l}"), 1)
                move(xg, ps[:, 2, 0:256]).then_inc(sem(f"xg_moved{l}"), 1)
                for buf in range(2):
                    act.sem_inc(sem(f"y_stored{l}_{buf}"), 16)

                def item(g, buf, turn):
                    act.wait_ge(sem(f"h_ready{l}"), g + 2)
                    act.activation(hs[64:128, :], ps[0:64, 0, 0:256], ACT.Silu).then_inc(sem(f"silu_ready{l}"), 1)
                    act.wait_ge(sem(f"xg_ready{l}"), g + 2)
                    act.wait_ge(sem(f"xg_turned{l}"), g + 1)
                    move(xg, ps[:, 2, 0:256]).then_inc(sem(f"xg_moved{l}"), 1)
                    act.wait_ge(sem(f"y_ready{l}"), g + 2)
                    act.wait_ge(sem(f"y_stored{l}_{buf}"), turn * 16 + 16)
                    move(ysb[:, buf, :], ps[:, 1, 0:256]).then_inc(sem(f"y_moved{l}"), 1)
                    act.wait_ge(sem(f"y_moved{l}"), g + 1)
                    act.dma_start(ybuf[l][bass.ds(g * SLOTS, SLOTS), :].rearrange("s (q c) -> q s c", q=QUARTERS),
                                  ysb[:, buf, :]).then_inc(sem(f"y_stored{l}_{buf}"), 16)

                with act.Fori(0, n >> 1) as turn:
                    item(turn * 2, 0, turn)
                    item(turn * 2 + 1, 1, turn)
                with act.If(n & 1):
                    item(n - 1, 0, n >> 1)
                combine(l, n)

            def combine(l, n):
                act.wait_ge(sem(f"xg_ready{l}"), n + 1)
                for j in range(TILES[l]):
                    rows_ = min(P, TOKENS[l] - j * P)
                    act.activation(tok[0:rows_, j, :], tok[0:rows_, j, :], ACT.Copy, scale=ALPHA).then_inc(sem(f"tok_scaled{l}"), 1)
                act.wait_ge(sem("weights_ready"), l + 1)
                for j in range(2):
                    for c in range(2):
                        act.activation(wdiag[:, 2 * j + c, :], ident, ACT.Copy, scale=wts[:, c, j:j + 1]).then_inc(sem("weights_turned"), 1)
                for j in range(TILES[l]):
                    rows_ = min(P, TOKENS[l] - j * P)
                    act.wait_ge(sem(f"stats_ready{l}"), j + 1)
                    act.activation(tstd[0:rows_, j:j + 1], mv[0:rows_, j, 1:2], ACT.Sqrt, bias=cst("eps")[0:rows_, :]).then_inc(sem(f"tstd_ready{l}"), 1)
                    if l == 0:
                        r = rows_of[l][j][0:rows_, 0, :]
                        act.wait_ge(sem("trs_ready"), j + 1)
                        for h in range(2):
                            dst = r[:, h * 512:(h + 1) * 512]
                            src = dst if h == 0 or j == 2 else ps[:, 6 + j, :]
                            last = act.activation(dst, src, ACT.Identity, scale=trs[0:rows_, j:j + 1], bias=centre[0:rows_, j:j + 1])
                        last.then_inc(sem("z_ready0"), 1)

            norm(0, cv, sq, cv, T0, ACT.Silu, lambda c: V("ln_g", c), lambda c: V("ln_b", c))
            act.wait_ge(sem("in_router"), 128)
            post(0)
            mixture(0)
            for j in range(3):
                rows_ = min(P, T0 - j * P)
                act.wait_ge(sem("z_turned"), 2 * j + 1)
                for c in range(4):
                    act.activation(xT[:, c, j * P:j * P + rows_], ps[:, 2 * j, c * rows_:(c + 1) * rows_], ACT.Identity,
                                   scale=V("post_g", 8 + c), bias=V("post_b", 8 + c)).then_inc(sem("xT_back"), 1)
            for c in range(NC_):
                act.wait_ge(sem("kq_ready"), c + 1)
                if c >= 2:
                    act.wait_ge(sem("rope_ready"), c - 1)
                move(raw[:, c % 2, :], ps[:, c % 4, 0:T0]).then_inc(sem("kq_moved"), 1)
            for i, (j, half) in enumerate(((0, 0), (1, 0), (0, 1), (1, 1))):
                act.wait_ge(sem("v_ready"), i + 1)
                move(vtok[:, j, half * 512:(half + 1) * 512], ps[:, 4 + i, :]).then_inc(sem("v_moved"), 1)
            act.wait_ge(sem("v_ready"), 5)
            for q in range(QUARTERS):
                move(vtok[0:META, 2, q * 256:(q + 1) * 256], ps[32 * q:32 * q + META, 4, 0:256]).then_inc(sem("v_moved"), 1)
            def move_queries(c):
                act.wait_ge(sem("kq_ready"), NC_ + c + 1)
                move(qT[:, c, :], ps[:, 1, 0:SEQ]).then_inc(sem("kq_moved"), 1)

            for c in range(3):
                move_queries(c)
            act.wait_ge(sem("lam_sums"), 2)
            act.activation(lame, lam2, ACT.Exp).then_inc(sem("lam_exp"), 1)
            UNITS = 2 * HEADS

            def move_probs(u):
                i, b = u % 2, u % 2
                act.wait_ge(sem("pd_turned"), u + 1)
                if u >= 2:
                    act.wait_ge(sem("pv_ready"), u - 1)
                else:
                    act.wait_ge(sem("pdT_zero"), 2)
                full = KEYS[i] // P
                move(pdT[:, b, 0:full * P], ps[:, 4 + b, 0:full * P])
                move(pdT[0:META, b, full * P:(full + 1) * P],
                     ps[0:META, 4 + b, full * P:(full + 1) * P]).then_inc(sem("pdT_ready"), 1)

            def move_output(u):
                h, i = u // 2, u % 2
                o = ps[:, 6 + i, 0:P]
                act.wait_ge(sem("pv_ready"), u + 1)
                act.wait_ge(sem("scores_ready"), 2 * h + 2)
                move(otok[:, h, i * P:(i + 1) * P], o)
                act.activation(ps[:, 6 + i, P:2 * P], o, ACT.Square,
                               accum_out=osum[:, u:u + 1]).then_inc(sem("o_squared"), 1)

            for u in range(UNITS):
                i = u % 2
                if i == 0 and 3 <= u // 2 + 2 < HEADS:
                    move_queries(u // 2 + 2)
                act.wait_ge(sem("max_ready"), u + 1)
                for c in range(2):
                    p_ = prob[:, u % 2, c * T0:c * T0 + KEYS[i]]
                    act.activation(p_, p_, ACT.Exp, bias=mx[:, u % 2, c:c + 1],
                                   accum_out=den[:, u % 2, c:c + 1]).then_inc(sem("exp_ready"), 1)
                if u >= 1:
                    move_probs(u - 1)
                if u >= 2:
                    move_output(u - 2)
            move_probs(UNITS - 1)
            move_output(UNITS - 2)
            move_output(UNITS - 1)
            act.wait_ge(sem("o_squared"), UNITS)
            act.activation(orms, osum, ACT.Sqrt, bias=cst("eps"), scale=1.0 / P).then_inc(sem("ostd_ready"), 1)
            act.wait_ge(sem("orms_ready"), 1)
            for h in range(HEADS):
                last = act.activation(otok[:, h, P:], otok[:, h, P:], ACT.Copy, scale=orms[:, 2 * h + 1:2 * h + 2])
            last.then_inc(sem("o_scaled1"), 1)
            for q in range(2):
                act.wait_ge(sem("o_turned"), 3 + q)
                act.activation(oT[:, 4 * q:4 * q + 4, P:], ps[:, 2 + q, :].rearrange("p (h t) -> p h t", h=4), ACT.Copy,
                               scale=subg).then_inc(sem("oT_ready"), 1)
            for c in range(NC_):
                last = act.activation(stream[1][:, c, :], stream[1][:, c, :], ACT.Copy, scale=ALPHA)
            last.then_inc(sem("x_scaled1"), 1)
            post(1)
            act.wait_ge(sem("tok_ready1"), 4)
            for k, name in enumerate(("post_ln_g", "post_ln_b")):
                act.dma_start(lnrow[:, k, :], a[name][1, 1:2, :].broadcast_to([P, D])).then_inc(sem("in_lnrow"), 16)
            mixture(1)

        @block.vector
        def _(dve):
            steps = [0]

            def step(ins):
                steps[0] += 1
                ins.then_inc(sem("dve_step"), 1)
                dve.wait_ge(sem("dve_step"), steps[0])

            def begin(ins):
                steps[0] += 1
                ins.then_inc(sem("dve_step"), 1)
                return steps[0]

            def after(count):
                dve.wait_ge(sem("dve_step"), count)

            for j in range(3):
                rows_ = min(P, T0 - j * P)
                dve.wait_ge(sem("x_turned"), 2 * j + 2)
                dve.tensor_copy(xT[:, 4:8, j * P:j * P + rows_],
                                ps[:, 2 * j + 1, 0:4 * rows_].rearrange("p (c t) -> p c t", c=4)).then_inc(sem("x_moved"), 1)
            dve.wait_ge(sem("vec_turned"), 1)
            dve.tensor_copy(vec[:, :], ps[:, 6, 0:VEC_ROWS]).then_inc(sem("vec_ready"), 1)
            dve.tensor_copy(wdw[:, :], ps[:, 7, 0:TAPS * NC_]).then_inc(sem("vec_ready"), 1)
            dve.wait_ge(sem("vec_ready"), 2)
            dve.wait_ge(sem("pad_zero"), 1)
            step(dve.tensor_copy(alpha_b, vec[:, VEC_AT["b_pw2"]:VEC_AT["b_pw2"] + 8]))

            def gate(c):
                dve.wait_ge(sem("sig_ready"), c + 1)
                dve.scalar_tensor_tensor(glu[:, c, PAD:], ps[:, 2 * (c % 2), 0:T0], V("b_pw1", c), sig[:, c % 2, :],
                                         ALU.add, ALU.mult).then_inc(sem("glu_ready"), 1)

            def convolve(cs, glus, then=lambda k: None):
                dve.wait_ge(sem("glu_ready"), glus)
                first = steps[0]
                for k in range(TAPS):
                    for i, c in enumerate(cs):
                        if k:
                            dve.wait_ge(sem("dve_step"), first + (k - 1) * len(cs) + i + 1)
                            ins = dve.scalar_tensor_tensor(cv[:, c, :], glu[:, c, k:k + T0], tap(k, c), cv[:, c, :], ALU.mult, ALU.add)
                        else:
                            ins = dve.tensor_scalar(cv[:, c, :], glu[:, c, 0:T0], tap(0, c), V("b_dw", c), ALU.mult, ALU.add)
                        if k < TAPS - 1:
                            ins.then_inc(sem("dve_step"), 1)
                            steps[0] += 1
                        else:
                            ins.then_inc(sem("conv_ready"), 1)
                    then(k)

            gate(0)
            gate(1)
            convolve((0, 1), 2, lambda k: gate({9: 2, 20: 3}[k]) if k in (9, 20) else None)
            convolve((2, 3), 4, lambda k: gate({0: 4, 10: 5, 20: 6, 29: 7}[k]) if k in (0, 10, 20, 29) else None)
            convolve((4, 5), 6)

            def norm(turn, src, T, src_sem, src_n=NC_):
                def over_chunks(t):
                    return t[:, 0:T].unsqueeze(1).broadcast_to([P, 2, T])

                dve.wait_ge(sem(src_sem), src_n)
                dve.wait_ge(sem("mean_ready"), turn + 1)
                for p in range(PIECES):
                    piece = src[:, 2 * p:2 * p + 2, 0:T]
                    dve.tensor_tensor(piece, piece, over_chunks(ps[:, 4, :]), ALU.subtract).then_inc(sem("centred"), 1)
                dve.wait_ge(sem("std_ready"), turn + 1)
                dve.wait_ge(sem("sq_ready"), PIECES * (turn + 1))
                step(dve.reciprocal(rstd[:, 0:T], std[:, 0:T]))
                for p in range(PIECES):
                    piece = src[:, 2 * p:2 * p + 2, 0:T]
                    dve.tensor_tensor(piece, piece, over_chunks(rstd), ALU.mult).then_inc(sem("scaled"), 1)

            def residual(l):
                T = TOKENS[l]
                dve.wait_ge(sem(f"x_scaled{l}"), 1)
                for c in range(NC_):
                    dve.wait_ge(sem(f"m_ready{l}"), c + 1)
                    dve.tensor_tensor(stream[l][:, c, 0:T], stream[l][:, c, 0:T], ps[:, m_bank(c), 0:T], ALU.add).then_inc(sem(f"r_ready{l}"), 1)

            def last_dim(t, n, m):
                return t.unsqueeze(2).broadcast_to([P, n, m])

            def post_and_route(l):
                T, n = TOKENS[l], TILES[l]
                step(dve.memset(lgT[0:20, :], 0.0)) if l == 0 else step(dve.memset(lgT[0:20, 0:SEQ], 0.0))
                dve.engine_nop().then_inc(sem("pad_ready"), 1)
                norm(1 + l, stream[l], T, f"r_ready{l}")
                neg4 = cst("neg4").unsqueeze(1).broadcast_to([P, n, 4])
                dve.wait_ge(sem("logits_turned"), l + 1)
                step(dve.tensor_copy(lg[:, 0:n, :], ps[:, 7, 64:64 + 20 * n].rearrange("p (n e) -> p n e", e=20)))
                G = lg[:, 0:n, 0:4]

                def first_max(values, maxv, onehot):
                    step(dve.tensor_reduce(maxv[:, 0:n], values, AX, ALU.max))
                    step(dve.tensor_tensor(geq[:, 0:n, :], values, last_dim(maxv[:, 0:n], n, 4), ALU.is_equal))
                    step(dve.tensor_tensor(cand[:, 0:n, :], geq[:, 0:n, :], neg4, ALU.mult))
                    step(dve.tensor_reduce(sel[:, 0:n], cand[:, 0:n, :], AX, ALU.min))
                    step(dve.tensor_tensor(onehot[:, 0:n, :], neg4, last_dim(sel[:, 0:n], n, 4), ALU.is_equal))

                first_max(G, gmax, gone)
                dve.tensor_tensor(gex[:, 0:n, :], G, last_dim(gmax[:, 0:n], n, 4), ALU.subtract).then_inc(sem("gsub_ready"), 1)
                chosen = prod4(PROD, (n, 4, 4))
                step(dve.tensor_tensor(chosen, lg[:, 0:n, 4:20].rearrange("p n (g e) -> p n g e", g=4),
                                       gone[:, 0:n, :].unsqueeze(3).broadcast_to([P, n, 4, 4]), ALU.mult))
                step(dve.tensor_reduce(el[:, 0:n, :], chosen.rearrange("p n g e -> p n e g"), AX, ALU.add))
                first_max(el[:, 0:n, :], m1, oh1)
                step(dve.scalar_tensor_tensor(el2[:, 0:n, :], oh1[:, 0:n, :], -BIG, el[:, 0:n, :], ALU.mult, ALU.add))
                first_max(el2[:, 0:n, :], m2, oh2)
                dve.tensor_tensor(e2[:, 0:n], m2[:, 0:n], m1[:, 0:n], ALU.subtract).then_inc(sem("e2_sub"), 1)
                step(dve.tensor_tensor(gone[:, 0:n, :], gone[:, 0:n, :], last_dim(cst("valid")[:, 0:n] if l == 0 else cst("ones")[:, 0:n], n, 4), ALU.mult))
                for c, oh in enumerate((oh1, oh2)):
                    step(dve.tensor_tensor(AA[:, c, 0:n, :].rearrange("p n (g e) -> p n g e", g=4),
                                           gone[:, 0:n, :].unsqueeze(3).broadcast_to([P, n, 4, 4]),
                                           oh[:, 0:n, :].unsqueeze(2).broadcast_to([P, n, 4, 4]), ALU.mult))
                dve.tensor_tensor(Asum[:, 0:n, :], AA[:, 0, 0:n, :], AA[:, 1, 0:n, :], ALU.add).then_inc(sem("picks_ready"), 1)
                step(dve.tensor_copy(turn_of[:, 0:AHEAD], cst("turn")[:, 0:AHEAD]))
                dve.wait_ge(sem("totals_ready"), l + 1)
                step(dve.tensor_reduce(nit, ps[:, 6, 0:16 * n].rearrange("p (n e) -> p e n", e=16), AX, ALU.add))
                over = prod4(PROD, (1, 16, FULL))[:, 0]
                step(dve.tensor_tensor(over, nit.unsqueeze(2).broadcast_to([P, 16, FULL]),
                                       cst("full").unsqueeze(1).broadcast_to([P, 16, FULL]), ALU.is_gt))
                step(dve.tensor_reduce(nit, over, AX, ALU.add))
                rest = EXPERTS - AHEAD
                made_key = begin(dve.scalar_tensor_tensor(key, nit, float(EXPERTS), cst("minus_e"), ALU.mult, ALU.add))
                made_live13 = begin(dve.tensor_scalar(live13, nit[:, AHEAD:], 0.0, None, ALU.is_gt))
                later, above = key[:, AHEAD:], prod4(PROD, (1, rest, rest))[:, 0]
                after(made_key)
                made_above = begin(dve.tensor_tensor(above, later.unsqueeze(1).broadcast_to([P, rest, rest]),
                                                     later.unsqueeze(2).broadcast_to([P, rest, rest]), ALU.is_gt))
                after(made_live13)
                made_live = begin(dve.tensor_reduce(live, live13, AX, ALU.add))
                after(made_above)
                begin(dve.tensor_reduce(srt, above, AX, ALU.add))
                after(made_live)
                after(begin(dve.tensor_scalar(live2, live, 2.0, -1.0, ALU.mult, ALU.add)))
                made_srt2 = begin(dve.tensor_scalar(srt2, srt, -2.0, live2, ALU.mult, ALU.add))
                begin(dve.scalar_tensor_tensor(live13, srt, live, srt, ALU.is_ge, ALU.mult))
                after(made_srt2)
                step(dve.scalar_tensor_tensor(srt2, srt, 2.0, srt2, ALU.mult, ALU.min))
                step(dve.tensor_tensor(turn_of[:, AHEAD:], live13, srt2, ALU.max))
                n17 = EXPERTS + 1
                square = lambda lo: prod4(lo, (1, 16, 16))[:, 0]
                pre, own, ahead = prod4(PROD, (1, n17, 16))[:, 0], square(PROD2), square(PROD3)
                items16 = nit.unsqueeze(1).broadcast_to([P, 16, 16])
                turns16 = turn_of.unsqueeze(1).broadcast_to([P, 16, 16])
                made_pre = begin(dve.tensor_tensor(pre, turn_of.unsqueeze(1).broadcast_to([P, n17, 16]),
                                                   cst("turn").unsqueeze(2).broadcast_to([P, n17, 16]), ALU.is_lt))
                made_own = begin(dve.tensor_tensor(own, turns16, cst("turn")[:, 0:16].unsqueeze(2).broadcast_to([P, 16, 16]), ALU.is_equal))
                after(made_pre)
                made_pre = begin(dve.tensor_tensor(pre, pre, nit.unsqueeze(1).broadcast_to([P, n17, 16]), ALU.mult))
                made_ahead = begin(dve.tensor_tensor(ahead, turns16, turn_of.unsqueeze(2).broadcast_to([P, 16, 16]), ALU.is_lt))
                after(made_pre)
                made_table = begin(dve.tensor_reduce(table[:, 0:n17], pre, AX, ALU.add))
                made_own = begin(dve.tensor_tensor(own, own, cst("expert").unsqueeze(1).broadcast_to([P, 16, 16]), ALU.mult))
                after(made_table)
                made_ahead = begin(dve.tensor_tensor(ahead, ahead, items16, ALU.mult))
                dve.tensor_copy(tab[0:1, l, 0:ORDER], table[0:1, 0:ORDER]).then_inc(sem("tab_ready"), 1)
                after(made_own)
                made_experts = begin(dve.tensor_reduce(table[:, ORDER:], own, AX, ALU.add))
                after(made_ahead)
                made_ebase = begin(dve.tensor_reduce(ebase, ahead, AX, ALU.add))
                after(made_experts)
                dve.tensor_copy(tab[0:1, l, ORDER:], table[0:1, ORDER:]).then_inc(sem("order_ready"), 1)
                dve.wait_ge(sem("ranks_ready"), l + 1)
                pr, pb = prod4(PROD4, (2, n, 16)), prod4(PROD, (2, n, 16))
                rk2, bs2, pos2 = (t.rearrange("p (c n) -> p c n", c=2)[:, :, 0:n] for t in (rk, bs, pos))
                for c in range(2):
                    made_pr = begin(dve.tensor_tensor(pr[:, c], AA[:, c, 0:n, :], ps[:, 7, 0:16 * n].rearrange("p (n e) -> p n e", e=16), ALU.mult))
                after(made_ebase)
                for c in range(2):
                    made_pb = begin(dve.tensor_tensor(pb[:, c], AA[:, c, 0:n, :], ebase.unsqueeze(1).broadcast_to([P, n, 16]), ALU.mult))
                after(made_pr)
                begin(dve.tensor_reduce(rk2, pr, AX, ALU.add))
                after(made_pb)
                step(dve.tensor_reduce(bs2, pb, AX, ALU.add))
                step(dve.scalar_tensor_tensor(pos2, bs2, float(SLOTS), rk2, ALU.mult, ALU.add))
                step(dve.tensor_copy(pos_i[:, l, :].rearrange("p (c n) -> p c n", c=2)[:, :, 0:n], pos2))
                dve.engine_nop().then_inc(sem("pos_ready"), 1)
                if l == 0:
                    step(dve.tensor_tensor(pos2, pos2, cst("far").rearrange("p (c n) -> p c n", c=2), ALU.add))
                pick_item(l, 0, True)
                dve.wait_ge(sem("gex_ready"), l + 1)
                step(dve.tensor_reduce(gsum[:, 0:n], gex[:, 0:n, :], AX, ALU.add))
                step(dve.reciprocal(gw[:, 0:n], gsum[:, 0:n]))
                dve.wait_ge(sem("e2_ready"), l + 1)
                step(dve.tensor_scalar(wsum[:, 0:n], e2[:, 0:n], 1.0, None, ALU.add))
                step(dve.reciprocal(wsum[:, 0:n], wsum[:, 0:n]))
                step(dve.tensor_tensor(wts[:, 0, 0:n], wsum[:, 0:n], gw[:, 0:n], ALU.mult))
                dve.tensor_tensor(wts[:, 1, 0:n], wts[:, 0, 0:n], e2[:, 0:n], ALU.mult).then_inc(sem("weights_ready"), 1)

            def pick_item(l, g, first):
                n = TILES[l]
                if not first:
                    dve.wait_ge(sem(f"xg_ready{l}"), g)
                    dve.wait_ge(sem(f"pos_next{l}"), g)
                eq = peq[:, 0:2 * n, :].rearrange("p (c n) s -> p c n s", c=2)
                pos2 = pos.rearrange("p (c n) -> p c n", c=2)
                for c in range(2):
                    ins = dve.tensor_tensor(eq[:, c], cst("slot").unsqueeze(1).broadcast_to([P, n, SLOTS]),
                                            pos2[:, c, 0:n].unsqueeze(2).broadcast_to([P, n, SLOTS]), ALU.is_equal)
                ins.then_inc(sem(f"peq_ready{l}"), 1)
                dve.wait_ge(sem(f"peq_ready{l}"), g + 1)
                dve.tensor_tensor(pick[:, 0:n, :], eq[:, 0], eq[:, 1], ALU.add).then_inc(sem(f"pick_ready{l}"), 1)
                dve.tensor_scalar(pos2[:, :, 0:n], pos2[:, :, 0:n], -float(SLOTS), None, ALU.add).then_inc(sem(f"pos_next{l}"), 1)

            def move_gathered(l, g, first):
                dve.wait_ge(sem(f"xg_turned{l}"), g + 1)
                if not first:
                    dve.wait_ge(sem(f"h_ready{l}"), g + 1)
                dve.tensor_copy(xTg.rearrange("p (q m) s -> p m q s", m=2),
                                ps[:, 3, 0:256].rearrange("p (m q s) -> p m q s", m=2, q=QUARTERS)).then_inc(sem(f"xT_ready{l}"), 1)

            def mixture(l):
                dve.wait_ge(sem("tab_ready"), l + 1)
                n = dve.value_load(tab[0:1, l, EXPERTS:EXPERTS + 1], min_val=MIN_ITEMS, max_val=MAX_ITEMS)
                move_gathered(l, 0, True)
                with dve.Fori(0, n) as g:
                    pick_item(l, g + 1, False)
                    dve.wait_ge(sem(f"silu_ready{l}"), g + 1)
                    dve.tensor_tensor(hs[64:128, :], hs[64:128, :], ps[64:128, 0, 0:256], ALU.mult).then_inc(sem(f"hs_ready{l}"), 1)
                    dve.wait_ge(sem(f"h_turned{l}"), g + 1)
                    dve.tensor_copy(hT.rearrange("p (a m) s -> p m a s", a=2),
                                    ps[:, 4, 0:128].rearrange("p (m a s) -> p m a s", m=2, a=2)).then_inc(sem(f"hT_ready{l}"), 1)
                    move_gathered(l, g + 1, False)

            def combine(l):
                def rows_in(j):
                    return min(P, TOKENS[l] - j * P)

                def halves(j):
                    r = rows_of[l][j][0:rows_in(j), 0, :]
                    return r[:, 0:512], ps[:, 6 + j, :] if j < 2 else r[:, 512:]

                def add(j):
                    n, r, w = rows_in(j), rows_of[l][j], 512 if j < 2 else D
                    first, second = r[0:n, 0, 0:w], r[0:n, 1, 0:w]
                    dve.wait_ge(sem(f"tok_scaled{l}"), j + 1)
                    dve.wait_ge(sem(f"rows{j}0"), 16 * l + 16)
                    step(dve.scalar_tensor_tensor(first, first, wts[0:n, 0, j:j + 1], tok[0:n, j, 0:w], ALU.mult, ALU.add))
                    dve.wait_ge(sem(f"rows{j}1"), 16 * l + 16)
                    step(dve.scalar_tensor_tensor(first, second, wts[0:n, 1, j:j + 1], first, ALU.mult, ALU.add))

                def stats(j):
                    n = rows_in(j)
                    for h in range(2):
                        if h == 1 and j < 2:
                            dve.wait_ge(sem("half_ready"), 2 * l + j + 1)
                        step(dve.bn_stats(bn[0:n, 6 * h:6 * h + 6], halves(j)[h]))
                    dve.bn_aggr(mv[0:n, j, :], bn[0:n, :]).then_inc(sem(f"stats_ready{l}"), 1)

                def finish(j):
                    n = rows_in(j)
                    rs, mean = trs[0:n, j:j + 1], mv[0:n, j, 0:1]
                    dve.wait_ge(sem(f"tstd_ready{l}"), j + 1)
                    step(dve.reciprocal(rs, tstd[0:n, j:j + 1]))
                    if l == 0:
                        dve.scalar_tensor_tensor(centre[0:n, j:j + 1], mean, -1.0, rs, ALU.mult, ALU.mult).then_inc(sem("trs_ready"), 1)
                        return
                    dve.wait_ge(sem("in_lnrow"), 32)
                    y = [rows_of[1][j][:, 0, h * 512:(h + 1) * 512] for h in range(2)]
                    gain, bias = ([lnrow[:, k, h * 512:(h + 1) * 512] for h in range(2)] for k in range(2))
                    for h in range(2):
                        dve.scalar_tensor_tensor(y[h], halves(j)[h], mean, gain[h], ALU.subtract, ALU.mult).then_inc(sem("out_gained"), 1)
                    for h in range(2):
                        dve.wait_ge(sem("out_gained"), 2 * j + h + 1)
                        dve.scalar_tensor_tensor(y[h], y[h], rs, bias[h], ALU.mult, ALU.add).then_inc(sem("out_half"), 1)

                add(0)
                stats(0)
                for j in range(1, TILES[l]):
                    add(j)
                    finish(j - 1)
                    stats(j)
                finish(TILES[l] - 1)

            norm(0, cv, T0, "conv_ready", DVE_CHUNKS)
            residual(0)
            post_and_route(0)
            mixture(0)
            combine(0)
            for j in range(3):
                rows_ = min(P, T0 - j * P)
                dve.wait_ge(sem("z_turned"), 2 * j + 2)
                for c in range(4):
                    dve.tensor_scalar(xT[:, 4 + c, j * P:j * P + rows_], ps[:, 2 * j + 1, c * rows_:(c + 1) * rows_],
                                      V("post_g", 12 + c), V("post_b", 12 + c), ALU.mult, ALU.add).then_inc(sem("xT_back"), 1)

            dve.wait_ge(sem("in_lam"), 64)
            for k in range(2):
                dve.tensor_tensor_reduce(lamv[:, 2 * k, :], lamv[:, 2 * k, :], lamv[:, 2 * k + 1, :], 1.0, 0.0,
                                         ALU.mult, ALU.add, lam2[:, k:k + 1]).then_inc(sem("lam_sums"), 1)
            step(dve.tensor_scalar(subg, V("subln", 0), 1.0 - LAM_INIT, None, ALU.mult))

            dve.wait_ge(sem("in_const_late"), 16)
            def rotate(dst, src, partners, T, lo):
                step(dve.stream_shuffle(partners, src, SWAP))
                step(dve.tensor_tensor(partners, partners, cst("sin")[:, lo:lo + T], ALU.mult))
                step(dve.tensor_tensor(dst, src, cst("cos")[:, lo:lo + T], ALU.mult))
                dve.tensor_tensor(dst, dst, partners, ALU.add).then_inc(sem("rope_ready"), 1)

            def rotate_queries(c):
                dve.wait_ge(sem("rope_ready"), NC_ + c)
                dve.wait_ge(sem("kq_moved"), NC_ + c + 1)
                rotate(qT[:, c, :], qT[:, c, :], qswp[:, :], SEQ, META)

            for c in range(NC_):
                if c:
                    dve.wait_ge(sem("rope_ready"), c)
                dve.wait_ge(sem("kq_moved"), c + 1)
                rotate(kT[:, c, :], raw[:, c % 2, :], swp[:, 0:T0], T0, 0)
            for c in range(3):
                rotate_queries(c)

            dve.wait_ge(sem("lam_exp"), 1)
            step(dve.tensor_tensor(nlam, lame[:, 1:2], lame[:, 0:1], ALU.subtract))
            step(dve.tensor_scalar(nlam, nlam, -LAM_INIT, None, ALU.add))

            def mask_and_max(u):
                i = u % 2
                b = u % 2
                w = KEYS[i]
                dve.wait_ge(sem("scores_ready"), u + 1)
                if u >= 2:
                    dve.wait_ge(sem("pd_turned"), u - 1)
                s = prob[:, b, :].rearrange("p (c k) -> p c k", c=2)[:, :, 0:w]
                dve.scalar_tensor_tensor(s, scores_of(i), HEAD_DIM ** -0.5,
                                         cst(f"mask{i}").unsqueeze(1).broadcast_to([P, 2, w]),
                                         ALU.mult, ALU.add).then_inc(sem("scores_moved"), 1)
                dve.wait_ge(sem("scores_moved"), u + 1)
                dve.tensor_reduce(mx[:, b, :], s, AX, ALU.max, negate=True).then_inc(sem("max_ready"), 1)

            def difference(u):
                i, b = u % 2, u % 2
                w = KEYS[i]
                dve.wait_ge(sem("exp_ready"), 2 * u + 2)
                step(dve.reciprocal(rden[:, b, :], den[:, b, :]))
                step(dve.tensor_tensor(r2[:, b:b + 1], rden[:, b, 1:2], nlam, ALU.mult))
                step(dve.tensor_scalar(prob[:, b, 0:w], prob[:, b, 0:w], rden[:, b, 0:1], None, ALU.mult))
                dve.scalar_tensor_tensor(prob[:, b, 0:w], prob[:, b, T0:T0 + w], r2[:, b:b + 1], prob[:, b, 0:w],
                                         ALU.mult, ALU.add).then_inc(sem("pd_ready"), 1)

            for u in range(2 * HEADS + 1):
                if u < 2 * HEADS:
                    mask_and_max(u)
                if u >= 1:
                    difference(u - 1)
                if u % 2 == 0 and 3 <= u // 2 + 2 < HEADS:
                    rotate_queries(u // 2 + 2)
            dve.wait_ge(sem("ostd_ready"), 1)
            dve.reciprocal(orms, orms).then_inc(sem("orms_ready"), 1)
            dve.wait_ge(sem("orms_ready"), 1)
            dve.tensor_tensor(otok[:, :, 0:P], otok[:, :, 0:P],
                              orms.rearrange("p (h i) -> p h i", i=2)[:, :, 0:1].broadcast_to([P, HEADS, P]),
                              ALU.mult).then_inc(sem("o_scaled0"), 1)
            for q in range(2):
                dve.wait_ge(sem("o_turned"), 1 + q)
                dve.tensor_scalar(oT[:, 4 * q:4 * q + 4, 0:P], ps[:, q, :].rearrange("p (h t) -> p h t", h=4),
                                  subg, None, ALU.mult).then_inc(sem("oT_ready"), 1)
            residual(1)
            post_and_route(1)
            mixture(1)
            combine(1)


def kernel(**inputs):
    import concourse.bacc as bacc
    from concourse.bass_utils import run_bass_kernel_spmd

    nc = bacc.Bacc("TRN2", target_bir_lowering=False, num_devices=1)
    arrays, aps = {}, {}
    for name, value in {**inputs, "consts": CONSTS}.items():
        v = np.ascontiguousarray(value)
        arrays[f"in_{name}"] = v
        aps[name] = nc.dram_tensor(f"in_{name}", v.shape, mybir.dt.from_np(v.dtype), kind="ExternalInput").ap()
    out = nc.dram_tensor("out", (1, SEQ, D), F32, kind="ExternalOutput").ap()
    trunk(nc, aps, out)
    return run_bass_kernel_spmd(nc, [arrays], core_ids=[0]).results[0]["out"]
```
